# Optimizing a Trainium2 kernel written in Bass

```python
import jax
import jax.numpy as jnp
from jax import lax
import numpy as np

D_MODEL = 1024
BATCH = 1
SEQ = 512
DEPTH = 1

CHUNK = 64
NORM_EPS = 1e-6
D_FF = 2816
RWKV_HEADS = 16
RWKV_HEAD_DIM = 64
D_RWKV = RWKV_HEADS * RWKV_HEAD_DIM
DECAY_LORA = 64
AAA_LORA = 64
GATE_LORA = 128
GN_EPS = RWKV_HEAD_DIM * 1e-5
ATT_HEADS = 16
ATT_HEAD_DIM = 64
D_ATT = ATT_HEADS * ATT_HEAD_DIM
IDX_HEADS = 8
IDX_HEAD_DIM = 64
INDEX_TOPK = 256
Q_BLOCK = 128
RWKV_COLS = (D_RWKV, D_RWKV, D_RWKV, DECAY_LORA, AAA_LORA, GATE_LORA)
DSA_COLS = (D_ATT, D_ATT, D_ATT, IDX_HEADS * IDX_HEAD_DIM, IDX_HEAD_DIM, IDX_HEADS)
GATE_COLS = (D_MODEL, D_MODEL)
D_SHIFT = sum(RWKV_COLS)
D_IN = sum(RWKV_COLS) + sum(DSA_COLS) + sum(GATE_COLS)

kernel_name = "hybrid_rwkv7_dsa_macaron_block"

def _rms_norm(x, gain):
    x32 = x.astype(jnp.float32)
    y = x32 * lax.rsqrt(jnp.mean(x32 * x32, axis=-1, keepdims=True) + NORM_EPS)
    return (y * gain.astype(jnp.float32)).astype(x.dtype)

def _swiglu(h, w_gate, w_up, w_down):
    return (jax.nn.silu(h @ w_gate) * (h @ w_up)) @ w_down

def _split(t, sizes):
    return jnp.split(t, np.cumsum(sizes)[:-1].tolist(), axis=-1)

def _causal_token_shift(p, mix):
    prev = jnp.pad(p, ((0, 0), (1, 0), (0, 0)))[:, :-1]
    return p + (prev - p) * mix

def _wkv7_scan(r, decay, k, v, kk, a):
    bsz = r.shape[0]

    def step(state, inp):
        r_t, w_t, k_t, v_t, kk_t, a_t = inp
        removal = jnp.einsum('bhij,bhj->bhi', state, kk_t)
        state = (state * w_t[:, :, None, :]
                 - removal[..., None] * (kk_t * a_t)[:, :, None, :]
                 + v_t[..., None] * k_t[:, :, None, :])
        return state, jnp.einsum('bhij,bhj->bhi', state, r_t)

    xs = tuple(jnp.moveaxis(t, 1, 0) for t in (r, decay, k, v, kk, a))
    s0 = jnp.zeros((bsz, RWKV_HEADS, RWKV_HEAD_DIM, RWKV_HEAD_DIM), jnp.float32)
    _, ys = lax.scan(step, s0, xs)
    return jnp.moveaxis(ys, 0, 1)

def _rwkv7_time_mix(r, k, v, xw, xa, xg, decay_lora, decay_base, aaa_lora, aaa_base,
                    gate_lora, k_k, k_a, r_k, gn_weight, gn_bias):
    bsz, seq_len = r.shape[0], r.shape[1]
    f32 = jnp.float32

    def heads(t):
        return t.reshape(bsz, seq_len, RWKV_HEADS, RWKV_HEAD_DIM)

    w = -jax.nn.softplus(-(decay_base + jnp.tanh(xw) @ decay_lora).astype(f32)) - 0.5
    decay = heads(jnp.exp(-jnp.exp(w)))
    a = heads(jax.nn.sigmoid((aaa_base + xa @ aaa_lora).astype(f32)))
    g = jax.nn.sigmoid(xg) @ gate_lora
    r32, k32, v32 = heads(r.astype(f32)), heads(k.astype(f32)), heads(v.astype(f32))
    kk = k32 * k_k.astype(f32).reshape(RWKV_HEADS, RWKV_HEAD_DIM)
    kk = kk / jnp.maximum(jnp.sqrt(jnp.sum(kk * kk, axis=-1, keepdims=True)), 1e-12)
    k32 = k32 * (1.0 + (a - 1.0) * k_a.astype(f32).reshape(RWKV_HEADS, RWKV_HEAD_DIM))
    y = _wkv7_scan(r32, decay, k32, v32, kk, a)
    mu = jnp.mean(y, axis=-1, keepdims=True)
    var = jnp.mean(jnp.square(y - mu), axis=-1, keepdims=True)
    y = ((y - mu) * lax.rsqrt(var + GN_EPS)).reshape(bsz, seq_len, D_RWKV)
    y = y * gn_weight.astype(f32) + gn_bias.astype(f32)
    bonus = jnp.sum(r32 * k32 * r_k.astype(f32), axis=-1, keepdims=True) * v32
    y = (y + bonus.reshape(bsz, seq_len, D_RWKV)) * g.astype(f32)
    return y.astype(r.dtype)

def _dsa_attention(q, k, v, iq, ik, iw):
    bsz, seq_len = q.shape[0], q.shape[1]
    f32 = jnp.float32
    top_k = min(INDEX_TOPK, seq_len // 4)
    n_blocks = seq_len // Q_BLOCK
    q = q.reshape(bsz, seq_len, ATT_HEADS, ATT_HEAD_DIM)
    k = k.reshape(bsz, seq_len, ATT_HEADS, ATT_HEAD_DIM)
    v = v.reshape(bsz, seq_len, ATT_HEADS, ATT_HEAD_DIM)
    iq = iq.reshape(bsz, seq_len, IDX_HEADS, IDX_HEAD_DIM).astype(f32)
    ik = ik.astype(f32)
    iw = iw.astype(f32) * (IDX_HEADS ** -0.5 * IDX_HEAD_DIM ** -0.5)
    key_pos = jnp.arange(seq_len)
    att_scale = ATT_HEAD_DIM ** -0.5
    gather = jax.vmap(lambda table, idx: table[idx])

    def one_block(blk):
        start = blk * Q_BLOCK
        qb = lax.dynamic_slice_in_dim(q, start, Q_BLOCK, axis=1)
        iqb = lax.dynamic_slice_in_dim(iq, start, Q_BLOCK, axis=1)
        iwb = lax.dynamic_slice_in_dim(iw, start, Q_BLOCK, axis=1)
        q_pos = start + jnp.arange(Q_BLOCK)
        visible_end = (q_pos // CHUNK + 1) * CHUNK
        admissible = key_pos[None, :] < visible_end[:, None]
        idx_score = jnp.einsum('bqhs,bqh->bqs',
                               jax.nn.relu(jnp.einsum('bqhd,bsd->bqhs', iqb, ik)), iwb)
        idx_score = jnp.where(admissible[None], idx_score, -jnp.inf)
        sel_score, sel_idx = lax.top_k(idx_score, top_k)
        valid = jnp.isfinite(sel_score)
        k_sel = gather(k, sel_idx)
        v_sel = gather(v, sel_idx)
        logits = jnp.einsum('bqhd,bqkhd->bhqk', qb, k_sel).astype(f32) * att_scale
        logits = jnp.where(valid[:, None], logits, -jnp.inf)
        probs = jax.nn.softmax(logits, axis=-1).astype(v.dtype)
        return jnp.einsum('bhqk,bqkhd->bqhd', probs, v_sel)

    out = lax.map(one_block, jnp.arange(n_blocks))
    return jnp.moveaxis(out, 0, 1).reshape(bsz, seq_len, D_ATT)

def _layer(x, ffn1_norm, ffn1_w_gate, ffn1_w_up, ffn1_w_down, mix_norm, w_in, time_mix,
           decay_lora, decay_base, aaa_lora, aaa_base, gate_lora, k_k, k_a, r_k, gn_weight, gn_bias,
           w_out_rwkv, w_out_attn, w_out, ffn2_norm, ffn2_w_gate, ffn2_w_up, ffn2_w_down):
    x = x + 0.5 * _swiglu(_rms_norm(x, ffn1_norm), ffn1_w_gate, ffn1_w_up, ffn1_w_down)
    h = _rms_norm(x, mix_norm)
    p = h @ w_in
    p_rwkv = _causal_token_shift(p[..., :D_SHIFT], time_mix)
    r, k, v, xw, xa, xg = _split(p_rwkv, RWKV_COLS)
    q_a, k_a_att, v_a, iq, ik, iw, gate_a, gate_b = _split(p[..., D_SHIFT:], DSA_COLS + GATE_COLS)
    y_a = _rwkv7_time_mix(r, k, v, xw, xa, xg, decay_lora, decay_base, aaa_lora, aaa_base,
                          gate_lora, k_k, k_a, r_k, gn_weight, gn_bias) @ w_out_rwkv
    y_b = _dsa_attention(q_a, k_a_att, v_a, iq, ik, iw) @ w_out_attn
    merged = jax.nn.sigmoid(gate_a) * y_a + jax.nn.sigmoid(gate_b) * y_b
    x = x + merged @ w_out
    x = x + 0.5 * _swiglu(_rms_norm(x, ffn2_norm), ffn2_w_gate, ffn2_w_up, ffn2_w_down)
    return x

def setup_inputs(seed: int = 0) -> dict:
    key = jax.random.key(seed)
    keys = jax.random.split(key, 32)
    counter = [0]

    def next_key():
        kk = keys[counter[0]]
        counter[0] += 1
        return kk

    def normal(shape, scale):
        return scale * jax.random.normal(next_key(), shape, jnp.float32)

    def gain(shape):
        return 1.0 + normal(shape, 0.05)

    L = DEPTH
    return {
        'x': normal((BATCH, SEQ, D_MODEL), 1.0),
        'ffn1_norm': gain((L, D_MODEL)),
        'ffn1_w_gate': normal((L, D_MODEL, D_FF), D_MODEL ** -0.5),
        'ffn1_w_up': normal((L, D_MODEL, D_FF), D_MODEL ** -0.5),
        'ffn1_w_down': normal((L, D_FF, D_MODEL), D_FF ** -0.5),
        'mix_norm': gain((L, D_MODEL)),
        'w_in': normal((L, D_MODEL, D_IN), D_MODEL ** -0.5),
        'time_mix': jax.random.uniform(next_key(), (L, D_SHIFT), jnp.float32),
        'decay_lora': normal((L, DECAY_LORA, D_RWKV), 0.5 * DECAY_LORA ** -0.5),
        'decay_base': normal((L, D_RWKV), 1.0) - 1.0,
        'aaa_lora': normal((L, AAA_LORA, D_RWKV), 0.5 * AAA_LORA ** -0.5),
        'aaa_base': normal((L, D_RWKV), 0.5),
        'gate_lora': normal((L, GATE_LORA, D_RWKV), GATE_LORA ** -0.5),
        'k_k': 0.85 + normal((L, D_RWKV), 0.05),
        'k_a': gain((L, D_RWKV)),
        'r_k': normal((L, RWKV_HEADS, RWKV_HEAD_DIM), 0.1),
        'gn_weight': gain((L, D_RWKV)),
        'gn_bias': normal((L, D_RWKV), 0.01),
        'w_out_rwkv': normal((L, D_RWKV, D_MODEL), D_RWKV ** -0.5),
        'w_out_attn': normal((L, D_ATT, D_MODEL), D_ATT ** -0.5),
        'w_out': normal((L, D_MODEL, D_MODEL), D_MODEL ** -0.5),
        'ffn2_norm': gain((L, D_MODEL)),
        'ffn2_w_gate': normal((L, D_MODEL, D_FF), D_MODEL ** -0.5),
        'ffn2_w_up': normal((L, D_MODEL, D_FF), D_MODEL ** -0.5),
        'ffn2_w_down': normal((L, D_FF, D_MODEL), D_FF ** -0.5),
        'final_norm': gain((D_MODEL,)),
    }

def reference(x, ffn1_norm, ffn1_w_gate, ffn1_w_up, ffn1_w_down, mix_norm, w_in, time_mix,
              decay_lora, decay_base, aaa_lora, aaa_base, gate_lora, k_k, k_a, r_k, gn_weight, gn_bias,
              w_out_rwkv, w_out_attn, w_out, ffn2_norm, ffn2_w_gate, ffn2_w_up, ffn2_w_down, final_norm):
    for layer in range(DEPTH):
        x = _layer(x, ffn1_norm[layer], ffn1_w_gate[layer], ffn1_w_up[layer], ffn1_w_down[layer],
                   mix_norm[layer], w_in[layer], time_mix[layer],
                   decay_lora[layer], decay_base[layer], aaa_lora[layer], aaa_base[layer],
                   gate_lora[layer], k_k[layer], k_a[layer], r_k[layer], gn_weight[layer], gn_bias[layer],
                   w_out_rwkv[layer], w_out_attn[layer], w_out[layer],
                   ffn2_norm[layer], ffn2_w_gate[layer], ffn2_w_up[layer], ffn2_w_down[layer])
    return _rms_norm(x, final_norm)


_drawn_inputs = setup_inputs


def setup_inputs(seed=0):
    import zlib

    import numpy as np

    out = dict(_drawn_inputs(seed))
    spreads = {}
    factors = {'decay_lora': 3.526,
     'k_k': 27.494,
     'k_a': 3.677,
     'gn_weight': 4.157,
     'gn_bias': 23.648,
     'ffn2_norm': 2.869}
    for name, (base, spread) in spreads.items():
        noise = np.random.default_rng([zlib.crc32(name.encode()), seed]).standard_normal(out[name].shape)
        drawn = base * np.exp(spread * noise) if base else spread * noise
        out[name] = jnp.asarray(drawn.astype(out[name].dtype))
    for name, factor in factors.items():
        out[name] = (out[name] * factor).astype(out[name].dtype)
    return out
```

```python
from contextlib import ExitStack

import numpy as np

import concourse.bass as bass
import concourse.mybir as mybir

F32 = mybir.dt.float32
F32R = mybir.dt.float32r
ALU = mybir.AluOpType
ACT = mybir.ActivationFunctionType
AX = mybir.AxisListType

P = 128
T = 512
D = 1024
KD = D // P
D_FF = 2816
NF = D_FF // P
CH = 64
NCH = T // CH
HEADS = 16
HD = 64
PAIRS = HEADS // 2
IDX_HEADS = 8
TOPK = 128
NQ = T // P
HALF = CH // 2
NORM_EPS = 1e-6
GN_EPS = HD * 1e-5
DECAY_C = float(np.exp(-0.5))
IW_SCALE = IDX_HEADS ** -0.5 * HD ** -0.5
NEG = -3.0e38
MASKED = 1.0e30

DBLK = 3 * KD
PHASES = [("f1", 2 * NF), ("d1", DBLK), ("idx", 8), ("att", 4 * PAIRS), ("ob", KD),
          ("rw", 4 * PAIRS), ("oa", KD), ("out", KD), ("f2", 2 * NF), ("d2", DBLK)]
FIRST, _at, USES, _use = {}, 0, {}, 0
for _n, _c in PHASES:
    FIRST[_n] = _at
    _at += _c
    USES[_n] = _use
    _use += {"f": 0, "d": 2}.get(_n[0], _c // 4)
NBLK = _at

PAR, _at = {}, 0
for _n, _c in [("ffn1_norm", KD), ("mix_norm", KD), ("ffn2_norm", KD), ("final_norm", KD), ("k_k", KD),
               ("k_a", KD), ("r_k", KD), ("gn_weight", KD), ("gn_bias", KD), ("decay_base", KD),
               ("aaa_base", KD), ("time_mix", 26)]:
    PAR[_n] = _at
    _at += _c
NPAR = _at
C_ID, C_ONE, C_HEAD, C_STRICT, C_INCL, C_SCAN, C_VIS, NCST = 0, 128, 256, 384, 512, 640, 1152, 1280


class Tally:

    def __init__(self, sem):
        self.sem, self.base, self.n, self.turn, self.per = sem, 0, 0, 0, 0

    def mark(self, ins):
        ins.then_inc(self.sem, 1)
        self.n += 1
        return self.value()

    def value(self):
        return self.turn * self.per + (self.base + self.n) if self.per else self.base + self.n

    def enter(self, turn, per):
        self.base, self.n, self.turn, self.per = self.base + self.n, 0, turn, per

    def leave(self, turns):
        assert self.n == self.per, (self.n, self.per)
        self.base, self.n, self.turn, self.per = self.base + self.per * turns, 0, 0, 0


def build(nc, x_in, ws, par_in, cst_in, lora_in, glora_in, out, sa_dram, l_dram, pd_dram, t11_dram):
    with ExitStack() as ctx:
        top = [(nc.sbuf_base + 63) // 64 * 64]

        def at(name, shape, dtype, offset):
            return nc.alloc_sbuf_tensor_at(name, shape, dtype, offset=offset)

        def fixed(name, shape, dtype=F32):
            o = top[0]
            size = 4
            for s in shape[1:]:
                size *= s
            top[0] += (size + 31) // 32 * 32
            return at(name, shape, dtype, o)

        x = fixed("x", [P, KD, T])
        raw = fixed("raw", [P, 4, 8, P])
        whi = fixed("whi", [P, 2, 8, P], F32R)
        wlo = fixed("wlo", [P, 2, 8, P], F32R)
        par = fixed("par", [P, NPAR])
        cst = fixed("cst", [P, NCST])
        lx = fixed("lx", [P, T])
        xg = fixed("xg", [P, T])
        wend = fixed("wend", [P, PAIRS, NCH])
        R0 = (top[0] + 63) // 64 * 64
        K = 1024

        ident, ones, headsum = cst[:, C_ID:C_ID + P], cst[:, C_ONE:C_ONE + P], cst[:, C_HEAD:C_HEAD + P]
        strict, incl = cst[:, C_STRICT:C_STRICT + P], cst[:, C_INCL:C_INCL + P]
        resets, visible = cst[:, C_SCAN:C_SCAN + T], cst[:, C_VIS:C_VIS + P]

        def gain(name, k):
            return par[:, PAR[name] + k:PAR[name] + k + 1]

        hhi = at("hhi", [P, KD, T], F32R, R0)
        hlo = at("hlo", [P, KD, T], F32R, R0 + 16 * K)
        yhi = at("yhi", [P, KD, T], F32R, R0 + 48 * K)
        ylo = at("ylo", [P, KD, T], F32R, R0 + 64 * K)
        ahi = at("ahi", [P, NF, T], F32R, R0 + 32 * K)
        alo = at("alo", [P, NF, T], F32R, R0 + 76 * K)
        silu_g = at("silu_g", [P, T], F32, R0 + 120 * K)
        prod = at("prod", [P, T], F32, R0 + 122 * K)
        sq = at("sq", [P, KD, T], F32, R0)
        hn = at("hn", [P, KD, T], F32, R0 + 16 * K)
        ssum = at("ssum", [P, T], F32, R0 + 124 * K)
        rstd = at("rstd", [P, T], F32, R0 + 126 * K)
        iq = at("iq", [P, 4, T], F32, R0 + 32 * K)
        ik = at("ik", [P, T], F32, R0 + 40 * K)
        iwt = at("iwt", [P, T], F32, R0 + 42 * K)
        iw = at("iw", [P, NQ, P], F32, R0 + 44 * K)
        score = at("score", [P, 3, T], F32, R0 + 46 * K)
        work = at("work", [P, 3, T], F32, R0 + 52 * K)
        relu = at("relu", [P, 2, T], F32, R0 + 58 * K)
        top8 = at("top8", [P, 8], F32, R0 + 62 * K)
        shl = at("shl", [P, 2, T + 8], F32, R0 + 64 * K)
        shd = at("shd", [P, 2, T], F32, R0 + 70 * K)
        sgb = at("sgb", [P, KD, T], F32, R0 + 32 * K)
        qs = at("qs", [P, 2, T], F32, R0 + 80 * K)
        ks = at("ks", [P, 2, T], F32, R0 + 84 * K)
        vf = at("vf", [P, 2, T], F32, R0 + 88 * K)
        vs = at("vs", [P, 2, T], F32, R0 + 92 * K)
        prob = at("prob", [P, NQ, T], F32, R0 + 96 * K)
        probt = at("probt", [P, NQ, T], F32, R0 + 104 * K)
        bias = at("bias", [P, NQ, T], F32, R0 + 112 * K)
        rmax = at("rmax", [P, 4 * NQ], F32, R0 + 120 * K)
        ra = at("ra", [P, PAIRS, T], F32, R0 + 48 * K)
        rb = at("rb", [P, PAIRS, T], F32, R0 + 64 * K)
        rk = at("rk", [P, PAIRS, T], F32, R0 + 80 * K)
        rr = at("rr", [P, PAIRS, T], F32, R0 + 96 * K)
        rv = at("rv", [P, PAIRS, T], F32, R0 + 112 * K)
        Z = R0 + 128 * K
        lora = at("lora", [P, 2, D], F32, Z)
        sh = at("sh", [P, 3, T + 8], F32, Z)
        gt = at("gt", [P, T], F32, Z + 6 * K + 96)
        zb = Z + 8 * K + 96
        t_k = at("t_k", [P, T], F32, zb)
        t_kk = at("t_kk", [P, T], F32, zb + 2 * K)
        t_sq = at("t_sq", [P, T], F32, zb + 4 * K)
        t_s = at("t_s", [P, T], F32, zb + 6 * K)
        t_sm = at("t_sm", [P, T], F32, zb + 8 * K)
        t_d = at("t_d", [P, T], F32, zb + 10 * K)
        slots = iter([R0 + 2 * K * n for n in range(16)] + [Z + 2 * K * n for n in range(9)])

        def bd(name):
            return at(name, [P, 4, P], F32, next(slots))

        m_x, m_u, m_g, m_p, vt, bt, kt, m_ak = [bd(n) for n in ("m_x", "m_u", "m_g", "m_p", "vt", "bt", "kt", "m_ak")]
        m_rb, m_rk = bd("m_rb"), bd("m_rk")
        state = [bd("state0"), bd("state1")]
        a_bd, b_bd, k_bd, r_bd = [bd(n) for n in ("a_bd", "b_bd", "k_bd", "r_bd")]
        v_bd, pd, l21, t11b = [bd(n) for n in ("v_bd", "pd", "l21", "t11b")]
        ls = at("ls", [P, CH, CH], F32, R0)
        tt = at("tt", [P, 2, HALF, HALF], F32, R0 + 16 * K)
        tprod = at("tprod", [P, 2, HALF, HALF], F32, R0 + 24 * K)
        t11 = at("t11", [P, HALF, HALF], F32, Z)
        a_l = at("a_l", [P, 4, P], F32, Z + 4 * K)
        b_l = at("b_l", [P, 4, P], F32, Z + 6 * K)
        lst = at("lst", [P, 4, CH], F32, Z + 8 * K)
        rkw = at("rkw", [P, PAIRS, P], F32, Z)
        g_d = at("g_d", [P, T], F32, Z + 4 * K)
        g_q = at("g_q", [P, T], F32, Z + 6 * K)
        g_r = at("g_r", [P, T], F32, Z + 8 * K)
        g_b = at("g_b", [P, T], F32, Z + 10 * K)
        g_c = at("g_c", [P, T], F32, Z + 12 * K)
        glora = at("glora", [P, D], F32, Z + 14 * K)
        sga = at("sga", [P, KD, T], F32, R0 + 80 * K)
        mtmp = at("mtmp", [P, 2, T], F32, R0 + 96 * K)
        outt = at("outt", [P, KD, T], F32, R0)

        bank = [ctx.enter_context(nc.psum_tensor(f"bank{n}", [P, T], F32)) for n in range(8)]

        def sem(name):
            return ctx.enter_context(nc.semaphore(name))

        loaded = [sem(f"loaded{n}") for n in range(4)]
        hi_ready, lo_ready, block_done = sem("hi_ready"), sem("lo_ready"), sem("block_done")
        taken = [sem(f"taken{n}") for n in range(4)]
        params = sem("params")
        x_loaded = sem("x_loaded")
        x_done = sem("x_done")
        n_sq, n_sum, n_mean, n_var, n_sd = sem("n_sq"), sem("n_sum"), sem("n_mean"), sem("n_var"), sem("n_sd")
        n_hn, h_hi, h_lo = sem("n_hn"), sem("h_hi"), sem("h_lo")
        silu_ready, prod_ready, act_hi, act_lo = sem("silu_ready"), sem("prod_ready"), sem("act_hi"), sem("act_lo")
        dve_step, act_step = sem("dve_step"), sem("act_step")
        iwt_done, iw_ready, sc_done, relu_ready, sc_used = (sem("iwt_done"), sem("iw_ready"), sem("sc_done"),
                                                           sem("relu_ready"), sem("sc_used"))
        bias_ready, lx_ready, lx_raw = sem("bias_ready"), sem("lx_ready"), sem("lx_raw")
        vt_done, vs_ready, logit, negmax, exped = (sem("vt_done"), sem("vs_ready"), sem("logit"), sem("negmax"),
                                                   sem("exped"))
        prob_ready, ptr, pt_taken, pv_done, y_hi, y_lo = (sem("prob_ready"), sem("ptr"), sem("pt_taken"),
                                                          sem("pv_done"), sem("y_hi"), sem("y_lo"))
        lora_loaded, lora_mm, lora_ready = sem("lora_loaded"), sem("lora_mm"), sem("lora_ready")
        shifted, kq_ready, kq_sq, kk_ss, kk_norm = (sem("shifted"), sem("kq_ready"), sem("kq_sq"), sem("kk_ss"),
                                                    sem("kk_norm"))
        scanned, decays, prepped, gate_kept, gate_out = (sem("scanned"), sem("decays"), sem("prepped"),
                                                         sem("gate_kept"), sem("gate_out"))
        l_a, l_b, l_mm, l_ready, l_kept = sem("l_a"), sem("l_b"), sem("l_mm"), sem("l_ready"), sem("l_kept")
        ls_loaded, solved, p_kept = sem("ls_loaded"), sem("solved"), sem("p_kept")
        zeroed, c_loaded, c_act, c_dve = sem("zeroed"), sem("c_loaded"), sem("c_act"), sem("c_dve")
        c_tr, c_gram, c_g, c_gs, c_ag = sem("c_tr"), sem("c_gram"), sem("c_g"), sem("c_gs"), sem("c_ag")
        c_mat, c_x, c_xs, c_u, c_us = sem("c_mat"), sem("c_x"), sem("c_xs"), sem("c_u"), sem("c_us")
        c_y, c_ys, c_s, c_ss = sem("c_y"), sem("c_ys"), sem("c_s"), sem("c_ss")
        rkw_ready, p_mean, p_sq, p_var, p_sd, p_ss = (sem("rkw_ready"), sem("p_mean"), sem("p_sq"), sem("p_var"),
                                                      sem("p_sd"), sem("p_ss"))
        p_bonus, p_gate, p_y, p_rk, p_diff = sem("p_bonus"), sem("p_gate"), sem("p_y"), sem("p_rk"), sem("p_diff")
        sga_loaded, merged, g_loaded = sem("sga_loaded"), sem("merged"), sem("g_loaded")
        settled = sem("settled")
        out_ready, out_kept = sem("out_ready"), sem("out_kept")

        block = ctx.enter_context(nc.Block())

        def settle(engine):
            engine.sem_inc(settled, 1)

        def begin_at_one(engine, *sems):
            for s in sems:
                engine.sem_inc(s, 1)

        def halves(buf):
            return [buf[HD * h:HD * h + HD, :, HD * h:HD * h + HD] for h in (0, 1)]

        @block.sync
        def _(sp):
            sp.dma_start(x[:, :, :], x_in.rearrange("k p t -> p k t")).then_inc(x_loaded, 16)
            sp.dma_start(par[:, :], par_in).then_inc(params, 16)
            sp.dma_start(cst[:, :], cst_in).then_inc(params, 16)
            for u in range(4):
                sp.dma_start(raw[:, u, :, :], ws[u, :, :, :]).then_inc(loaded[u], 16)
            sp.dma_start(lora[:, :, :], lora_in).then_inc(lora_loaded, 16)
            with sp.Fori(1, NBLK // 4) as i:
                for u in range(4):
                    sp.wait_ge(lo_ready, 4 * i + u - 3)
                    sp.dma_start(raw[:, u, :, :], ws[4 * i + u, :, :, :]).then_inc(loaded[u], 16)
            sp.wait_ge(out_ready, KD)
            sp.dma_start(out.rearrange("k p t -> p k t"), outt[:, :, :]).then_inc(out_kept, 16)
            sp.wait_ge(out_kept, 16)

        @block.gpsimd
        def _(pool):
            with pool.Fori(0, NBLK // 4) as i:
                for u in range(4):
                    pool.wait_ge(hi_ready, 4 * i + u + 1)
                    nc.gpsimd.tensor_tensor(wlo[:, u % 2, :, :], raw[:, u, :, :],
                                            whi[:, u % 2, :, :].bitcast(F32), ALU.subtract).then_inc(lo_ready, 1)

        @block.scalar
        def _(act):

            def split(first, per, i, u):
                b = first + u
                act.wait_ge(loaded[b % 4], 16 * (b // 4 + 1) + 4 * per * i)
                if b >= 2 or per:
                    act.wait_ge(block_done, b + per * i)
                nc.scalar.copy(whi[:, b % 2, :, :], raw[:, b % 4, :, :]).then_inc(hi_ready, 1)

            def norm(which, src_ready):
                for k in range(KD):
                    if src_ready is not None:
                        act.wait_ge(x_done, src_ready + k + 1)
                    nc.scalar.activation(sq[:, k, :], x[:, k, :], ACT.Square).then_inc(n_sq, 1)
                act.wait_ge(n_var, which + 1)
                nc.scalar.activation(rstd[:, :], ssum[:, :], ACT.Sqrt).then_inc(n_sd, 1)
                if which == 3:
                    return
                for k in range(KD):
                    act.wait_ge(n_hn, which * KD + k + 1)
                    nc.scalar.copy(hhi[:, k, :], hn[:, k, :]).then_inc(h_hi, 1)

            def feed(name, j0):
                b0 = FIRST[name]
                with act.Fori(0, NF // 2) as i:
                    for jj in range(2):
                        u = 2 * jj
                        split(b0, 4, i, u + 1)
                        act.wait_ge(block_done, 1 + b0 + u + 1 + 4 * i)
                        nc.scalar.activation(silu_g[:, :], bank[u][:, :], ACT.Silu).then_inc(silu_ready, 1)
                        split(b0, 4, i, u + 2)
                        act.wait_ge(prod_ready, 2 + j0 + jj + 1 + 2 * i)
                        settle(act)
                        nc.scalar.copy(ahi[:, 2 * i + jj, :], prod[:, :]).then_inc(act_hi, 1)

            def down(name, last):
                b0 = FIRST[name]
                if not last:
                    with act.Fori(0, 2) as i:
                        for u in range(12):
                            split(b0, 12, i, u + 1)
                else:
                    for u in range(2 * 12 - 1):
                        split(b0, 0, 0, u + 1)

            begin_at_one(act, pt_taken, gate_out, kk_norm, l_ready, l_kept, c_ys)
            split(0, 0, 0, 0)
            act.wait_ge(x_loaded, 16)
            norm(0, None)
            feed("f1", 0)
            down("d1", False)
            norm(1, 0)

            b0 = FIRST["idx"]
            for u in range(8):
                split(b0, 0, 0, u + 1)
                act.wait_ge(block_done, 1 + b0 + u + 1)
                if u < 4:
                    nc.scalar.copy(iq[:, u, :], bank[u][:, :]).then_inc(taken[u], 1)
                elif u == 4:
                    nc.scalar.copy(ik[:, :], bank[0][:, :]).then_inc(taken[0], 1)
                elif u == 5:
                    nc.scalar.mul(iwt[:, :], bank[1][:, :], IW_SCALE).then_inc(taken[1], 1)
                else:
                    nc.scalar.copy(shl[:, u - 6, 1:T + 1], bank[u - 4][:, :]).then_inc(taken[u - 4], 1)
            act.wait_ge(lx_raw, 2)
            nc.scalar.activation(lx[0:64, :], shd[0:64, 0, :], ACT.Tanh).then_inc(lx_ready, 1)
            nc.scalar.copy(lx[64:128, :], shd[64:128, 0, :]).then_inc(lx_ready, 1)
            nc.scalar.activation(xg[:, :], shd[:, 1, :], ACT.Sigmoid).then_inc(lx_ready, 1)
            for n in range(3 * IDX_HEADS):
                w = P * (n // IDX_HEADS + 2)
                act.wait_ge(sc_done, n + 1)
                if n >= 2:
                    act.wait_ge(sc_used, n - 1)
                nc.scalar.activation(relu[:, n % 2, 0:w], bank[4 + n % 4][:, 0:w], ACT.Relu)\
                    .then_inc(relu_ready, 1)

            b0, t0 = FIRST["att"], USES["att"]
            with act.Fori(0, PAIRS // 2) as i:
                for pp in range(2):
                    u = 4 * pp
                    p, np_ = 2 * i + pp, 2 * i + pp
                    split(b0, 8, i, u + 1)
                    act.wait_ge(block_done, 1 + b0 + u + 1 + 8 * i)
                    nc.scalar.mul(qs[:, pp, :], bank[0][:, :], HD ** -0.5).then_inc(taken[0], 1)
                    split(b0, 8, i, u + 2)
                    act.wait_ge(block_done, 1 + b0 + u + 2 + 8 * i)
                    nc.scalar.copy(ks[:, pp, :], bank[1][:, :]).then_inc(taken[1], 1)
                    split(b0, 8, i, u + 3)
                    split(b0, 8, i, u + 4)
                    act.wait_ge(block_done, 1 + b0 + u + 4 + 8 * i)
                    nc.scalar.activation(sgb[:, p, :], bank[3][:, :], ACT.Sigmoid).then_inc(taken[3], 1)
                    for hh in range(2):
                        act.wait_ge(negmax, 4 * i + 2 * pp + hh + 1)
                        for q in range(NQ):
                            w = P * (q + 1)
                            nc.scalar.activation(prob[:, q, 0:w], prob[:, q, 0:w], ACT.Exp,
                                                 bias=rmax[:, 4 + q:5 + q],
                                                 accum_out=rmax[:, 8 + q:9 + q]).then_inc(exped, 1)
                        act.wait_ge(pv_done, 1 + 4 * i + 2 * pp + hh)
                        for n, (a, b, bk) in enumerate([(0, 4, 4), (1, 3, 5), (2, 3, 6)]):
                            act.wait_ge(ptr, 1 + 12 * i + 6 * pp + 3 * hh + n + 1)
                            if n < 2:
                                nc.scalar.copy(probt[:, n, P * n:T], bank[bk][:, 0:P * (4 - n)])\
                                    .then_inc(pt_taken, 1)
                            else:
                                nc.scalar.copy(probt[:, 2, 2 * P:T], bank[6][:, 0:2 * P]).then_inc(pt_taken, 1)
                                nc.scalar.copy(probt[:, 3, 3 * P:T], bank[6][:, 2 * P:3 * P]).then_inc(pt_taken, 1)
                    act.wait_ge(pv_done, 1 + 4 * i + 2 * pp + 2)
                    settle(act)
                    nc.scalar.copy(yhi[:, p, :], bank[7][:, :]).then_inc(y_hi, 1)

            b0 = FIRST["ob"]
            with act.Fori(0, 2) as i:
                for u in range(4):
                    split(b0, 4, i, u + 1)

            for n in range(2 * KD):
                m, which = n // 2, n % 2
                act.wait_ge(lora_mm, n + 1)
                if n == 0:
                    act.wait_ge(block_done, 1 + FIRST["rw"])
                dst = (rb, rk)[which]
                nc.scalar.activation(dst[:, m, :], bank[4 + n % 4][:, :], ACT.Sigmoid,
                                     bias=gain(("decay_base", "aaa_base")[which], m)).then_inc(lora_ready, 1)

            b0, t0 = FIRST["rw"], USES["rw"]
            with act.Fori(0, PAIRS // 2) as i:
                for pp in range(2):
                    u = 4 * pp
                    p = 2 * i + pp
                    for s in range(3):
                        split(b0, 8, i, u + s + 1)
                        act.wait_ge(block_done, 1 + b0 + u + s + 1 + 8 * i)
                        act.wait_ge(shifted, 1 + 6 * i + 3 * pp)
                        if pp == 0 and s == 0:
                            act.wait_ge(zeroed, 1)
                        nc.scalar.copy(sh[:, s, 1:T + 1], bank[s][:, :]).then_inc(taken[s], 1)
                    split(b0, 8, i, u + 4)
                    act.wait_ge(block_done, 1 + b0 + u + 4 + 8 * i)
                    act.wait_ge(gate_out, 1 + 32 * i + 16 * pp)
                    nc.scalar.activation(gt[:, :], bank[3][:, :], ACT.Sigmoid).then_inc(taken[3], 1)
                    act.wait_ge(taken[3], 1 + t0 + pp + 1 + 2 * i)
                    act.dma_start(sa_dram[p, :, :], gt[:, :]).then_inc(gate_out, 16)
                    act.wait_ge(kq_ready, 2 * i + pp + 1)
                    nc.scalar.activation(t_sq[:, :], t_kk[:, :], ACT.Square).then_inc(kq_sq, 1)
                    act.wait_ge(kk_ss, 2 * i + pp + 1)
                    nc.scalar.activation(t_sq[:, :], bank[4][:, :], ACT.Sqrt).then_inc(kk_norm, 1)
                    act.wait_ge(scanned, 2 * i + pp + 1)
                    nc.scalar.activation(rb[:, p, :], t_s[:, :], ACT.Exp, scale=DECAY_C).then_inc(decays, 1)
                    nc.scalar.activation(t_sm[:, :], t_sm[:, :], ACT.Exp, scale=-DECAY_C).then_inc(decays, 1)
                    nc.scalar.activation(t_s[:, :], t_s[:, :], ACT.Exp, scale=-DECAY_C).then_inc(decays, 1)

            act.wait_ge(prepped, PAIRS)
            act.wait_ge(zeroed, 2)
            with act.Fori(0, NCH) as c:
                for g in range(2):
                    it = 2 * c + g
                    act.wait_ge(l_mm, 1 + it)
                    settle(act)
                    for h, d in enumerate(halves(a_l)):
                        nc.scalar.copy(d, ra[HD * h:HD * h + HD, 4 * g:4 * g + 4, bass.ds(CH * c, CH)])\
                            .then_inc(l_a, 1)
                    act.wait_ge(l_mm, 1 + it + 1)
                    act.wait_ge(l_kept, 1 + 32 * it)
                    for h in range(2):
                        nc.scalar.copy(lst[HD * h:HD * h + HD, :, :], bank[0][HD * h:HD * h + HD, :]
                                       .rearrange("p (n s) -> p n s", n=4)[:, :, HD * h:HD * h + HD])\
                            .then_inc(l_ready, 1)
                    act.wait_ge(l_ready, 1 + 2 * it + 2)
                    for h in range(2):
                        act.dma_start(l_dram[c, h, :, 4 * g:4 * g + 4, :], lst[HD * h:HD * h + HD, :, :])\
                            .then_inc(l_kept, 16)
            act.wait_ge(l_kept, 1 + 16 * 4 * NCH)
            for n in range(2 * NCH):
                act.dma_start(ls[8 * n:8 * n + 8, :, :], l_dram[n // 2, n % 2].rearrange("t p s -> p t s"))\
                    .then_inc(ls_loaded, 16)
            act.wait_ge(solved, 2)
            act.dma_start(pd_dram, tt[:, :, :, :]).then_inc(p_kept, 16)
            act.dma_start(t11_dram, t11[:, :, :]).then_inc(p_kept, 16)
            act.wait_ge(p_kept, 32)

            act.wait_ge(zeroed, 3)
            with act.Fori(0, NCH) as c:
                for g in range(2):
                    it = 2 * c + g
                    g4 = 4 * g
                    act.wait_ge(c_mat, 1 + it)
                    for h in range(2):
                        for k in range(2):
                            o = HD * h + HALF * k
                            act.dma_start(pd[o:o + HALF, :, o:o + HALF],
                                          pd_dram[bass.ds(16 * c + 8 * h + g4, 4), k, :, :].rearrange("p s t -> s p t"))\
                                .then_inc(c_loaded, 16)
                        o = HD * h
                        act.dma_start(t11b[o:o + HALF, :, o:o + HALF],
                                      t11_dram[bass.ds(16 * c + 8 * h + g4, 4), :, :].rearrange("p a b -> a p b"))\
                            .then_inc(c_loaded, 16)
                        act.dma_start(l21[o + HALF:o + CH, :, o:o + HALF],
                                      l_dram[c, h, HALF:CH, g4:g4 + 4, 0:HALF]).then_inc(c_loaded, 16)
                    act.wait_ge(c_y, 1 + it)
                    settle(act)
                    for dst, src in ((a_bd, ra), (r_bd, rr)):
                        for h, d in enumerate(halves(dst)):
                            nc.scalar.copy(d, src[HD * h:HD * h + HD, g4:g4 + 4, bass.ds(CH * c, CH)])\
                                .then_inc(c_act, 1)
                    act.wait_ge(c_g, it + 1)
                    nc.scalar.copy(m_g[:, :, :], bank[6][:, :].rearrange("p (n s) -> p n s", n=4)).then_inc(c_gs, 1)
                    act.wait_ge(c_x, it + 1)
                    nc.scalar.copy(m_x[:, :, :], bank[6][:, :].rearrange("p (n s) -> p n s", n=4)).then_inc(c_xs, 1)
                    act.wait_ge(c_y, 1 + it + 1)
                    settle(act)
                    for h in range(2):
                        nc.scalar.copy(ra[HD * h:HD * h + HD, g4:g4 + 4, bass.ds(CH * c, CH)],
                                       bank[0][HD * h:HD * h + HD, :].rearrange("p (n s) -> p n s", n=4)
                                       [:, :, HD * h:HD * h + HD]).then_inc(c_ys, 1)

            act.wait_ge(c_ss, 2 * NCH)
            act.dma_start(glora[:, :], glora_in).then_inc(g_loaded, 16)
            for p in range(PAIRS):
                act.wait_ge(p_diff, p + 1)
                nc.scalar.activation(g_q[:, :], g_d[:, :], ACT.Square).then_inc(p_sq, 1)
                act.wait_ge(p_var, p + 1)
                nc.scalar.activation(g_r[:, :], g_r[:, :], ACT.Sqrt).then_inc(p_sd, 1)
                act.wait_ge(p_y, p + 1)
                nc.scalar.copy(hhi[:, p, :], g_c[:, :]).then_inc(h_hi, 1)

            b0 = FIRST["oa"]
            act.wait_ge(gate_out, 1 + 16 * KD)
            for k in range(KD):
                act.dma_start(sga[:, k, :], sa_dram[k, :, :]).then_inc(sga_loaded, 16)
            with act.Fori(0, 2) as i:
                for u in range(4):
                    split(b0, 4, i, u + 1)
                    act.wait_ge(merged, u + 1 + 4 * i)
                    settle(act)
                    nc.scalar.copy(yhi[:, 4 * i + u, :], mtmp[:, u % 2, :]).then_inc(y_hi, 1)
            b0 = FIRST["out"]
            with act.Fori(0, 2) as i:
                for u in range(4):
                    split(b0, 4, i, u + 1)
            norm(2, 2 * KD - KD)
            feed("f2", NF)
            down("d2", True)
            norm(3, 2 * KD)

        @block.vector
        def _(dve):
            step = Tally(dve_step)

            def chain(ins):
                dve.wait_ge(dve_step, step.mark(ins))

            def norm(which, name, h0):
                for k in range(1, KD):
                    dve.wait_ge(n_sq, which * KD + k + 1)
                    src = sq[:, 0, :] if k == 1 else ssum[:, :]
                    if k < KD - 1:
                        chain(nc.vector.tensor_tensor(ssum[:, :], src, sq[:, k, :], ALU.add))
                    else:
                        nc.vector.tensor_tensor(rstd[:, :], src, sq[:, k, :], ALU.add).then_inc(n_sum, 1)
                dve.wait_ge(n_mean, which + 1)
                nc.vector.tensor_scalar(ssum[:, :], bank[4][:, :], 1.0 / D, NORM_EPS, ALU.mult, ALU.add)\
                    .then_inc(n_var, 1)
                dve.wait_ge(n_sd, which + 1)
                chain(nc.vector.reciprocal(rstd[:, :], rstd[:, :]))
                for k in range(KD):
                    dst = outt[:, k, :] if which == 3 else hn[:, k, :]
                    nc.vector.scalar_tensor_tensor(out=dst, in0=x[:, k, :], scalar=gain(name, k), in1=rstd[:, :],
                                                   op0=ALU.mult, op1=ALU.mult)\
                        .then_inc(out_ready if which == 3 else n_hn, 1)
                if which == 3:
                    return
                for k in range(KD):
                    dve.wait_ge(h_hi, h0 + k + 1)
                    nc.vector.tensor_tensor(hlo[:, k, :], hn[:, k, :], hhi[:, k, :].bitcast(F32), ALU.subtract)\
                        .then_inc(h_lo, 1)

            def feed(name, j0):
                b0 = FIRST[name]
                with dve.Fori(0, NF // 2) as i:
                    for jj in range(2):
                        dve.wait_ge(silu_ready, j0 + jj + 1 + 2 * i)
                        dve.wait_ge(block_done, 1 + b0 + 2 * jj + 2 + 4 * i)
                        dve.wait_ge(act_lo, 1 + j0 + jj + 2 * i)
                        nc.vector.tensor_tensor(prod[:, :], silu_g[:, :], bank[2 * jj + 1][:, :], ALU.mult)\
                            .then_inc(prod_ready, 1)
                        dve.wait_ge(act_hi, j0 + jj + 1 + 2 * i)
                        nc.vector.tensor_tensor(alo[:, 2 * i + jj, :], prod[:, :],
                                                ahi[:, 2 * i + jj, :].bitcast(F32), ALU.subtract).then_inc(act_lo, 1)

            def down(name):
                b0 = FIRST[name]
                with dve.Fori(0, 2) as i:
                    for m in range(4):
                        dve.wait_ge(block_done, 1 + b0 + 3 * m + 3 + 12 * i)
                        xm = x[:, 4 * i + m, :]
                        nc.vector.scalar_tensor_tensor(out=xm, in0=bank[m][:, :], scalar=0.5, in1=xm,
                                                       op0=ALU.mult, op1=ALU.add).then_inc(x_done, 1)
                        dve.wait_ge(x_done, X0[name] + m + 1 + 4 * i)
                        dve.sem_inc(taken[m], 1)

            X0 = {"d1": 0, "d2": 2 * KD}
            begin_at_one(dve, *taken, act_lo, y_lo, shifted, c_mat)
            dve.sem_inc(prod_ready, 2)
            dve.wait_ge(params, 32)
            norm(0, "ffn1_norm", 0)
            feed("f1", 0)
            down("d1")
            norm(1, "mix_norm", KD)

            chain(nc.vector.memset(shl[:, :, 0:1], 0.0))
            for s in range(2):
                dve.wait_ge(taken[2 + s], 1 + USES["idx"] + 2)
                chain(nc.vector.tensor_tensor(shd[:, s, :], shl[:, s, 0:T], shl[:, s, 1:T + 1], ALU.subtract))
                nc.vector.scalar_tensor_tensor(out=shd[:, s, :], in0=shd[:, s, :], scalar=gain("time_mix", 24 + s),
                                               in1=shl[:, s, 1:T + 1], op0=ALU.mult, op1=ALU.add).then_inc(lx_raw, 1)
            dve.wait_ge(iwt_done, 1)
            nc.vector.tensor_copy(iw[:, :, :], bank[4][:, :].rearrange("p (n s) -> p n s", n=4)).then_inc(iw_ready, 1)
            dve.wait_ge(iw_ready, 1)
            for n in range(3 * IDX_HEADS):
                q, hd = n // IDX_HEADS + 1, n % IDX_HEADS
                w = P * (q + 1)
                sc = score[:, q - 1, 0:w]
                dve.wait_ge(relu_ready, n + 1)
                if hd == 0:
                    ins = nc.vector.tensor_scalar(sc, relu[:, n % 2, 0:w], iw[:, q, hd:hd + 1], None, ALU.mult)
                else:
                    dve.wait_ge(sc_used, n)
                    ins = nc.vector.scalar_tensor_tensor(out=sc, in0=relu[:, n % 2, 0:w], scalar=iw[:, q, hd:hd + 1],
                                                         in1=sc, op0=ALU.mult, op1=ALU.add)
                ins.then_inc(sc_used, 1)
            dve.wait_ge(sc_used, 3 * IDX_HEADS)
            for q in range(1, NQ):
                w = P * (q + 1)
                chain(nc.vector.memset(score[0:CH, q - 1, w - CH:w], NEG))
                chain(nc.vector.tensor_copy(work[:, q - 1, 0:w], score[:, q - 1, 0:w]))
                for _ in range(TOPK // 8):
                    chain(nc.vector.max(top8[:, :], work[:, q - 1, 0:w]))
                    chain(nc.vector.match_replace(work[:, q - 1, 0:w], top8[:, :], work[:, q - 1, 0:w], NEG))
                chain(nc.vector.tensor_tensor(bias[:, q, 0:w], score[:, q - 1, 0:w], work[:, q - 1, 0:w],
                                              ALU.not_equal))
                chain(nc.vector.tensor_scalar(bias[:, q, 0:w], bias[:, q, 0:w], -1.0, MASKED, ALU.add, ALU.mult))
            chain(nc.vector.tensor_scalar(bias[:, 0, 0:P], visible, -1.0, MASKED, ALU.add, ALU.mult))

            b0, t0 = FIRST["att"], USES["att"]
            per = 2 * 2 * 5
            with dve.Fori(0, PAIRS // 2) as i:
                step.enter(i, per)
                for pp in range(2):
                    p = 2 * i + pp
                    dve.wait_ge(block_done, 1 + b0 + 4 * pp + 3 + 8 * i)
                    nc.vector.tensor_copy(vf[:, pp, :], bank[2][:, :]).then_inc(taken[2], 1)
                    dve.wait_ge(vt_done, 2 * i + pp + 1)
                    nc.vector.tensor_copy(vs[:, pp, :], bank[7][:, :]).then_inc(vs_ready, 1)
                    for hh in range(2):
                        head = 4 * i + 2 * pp + hh
                        dve.wait_ge(ptr, 1 + 3 * head)
                        for q in range(NQ):
                            w = P * (q + 1)
                            if q != 1:
                                dve.wait_ge(logit, 3 * head + max(q, 1))
                            src = bank[(4, 4, 5, 6)[q]][:, (P if q == 1 else 0):(P if q == 1 else 0) + w]
                            settle(dve)
                            ins = nc.vector.tensor_tensor_reduce(
                                out=prob[:, q, 0:w], in0=src, in1=bias[:, q, 0:w], scale=1.0, scalar=NEG,
                                op0=ALU.add, op1=ALU.max, accum_out=rmax[:, q:q + 1])
                            chain(ins)
                        nc.vector.tensor_scalar(rmax[:, 4:8], rmax[:, 0:4], -1.0, None, ALU.mult).then_inc(negmax, 1)
                        dve.wait_ge(exped, 4 * head + 4)
                        chain(nc.vector.reciprocal(rmax[:, 12:16], rmax[:, 8:12]))
                        for q in range(NQ):
                            w = P * (q + 1)
                            nc.vector.tensor_scalar(prob[:, q, 0:w], prob[:, q, 0:w], rmax[:, 12 + q:13 + q], None,
                                                    ALU.mult).then_inc(prob_ready, 1)
                    dve.wait_ge(y_hi, 2 * i + pp + 1)
                    nc.vector.tensor_tensor(ylo[:, p, :], bank[7][:, :], yhi[:, p, :].bitcast(F32), ALU.subtract)\
                        .then_inc(y_lo, 1)
            step.leave(PAIRS // 2)

            b0 = FIRST["ob"]
            with dve.Fori(0, 2) as i:
                for u in range(4):
                    dve.wait_ge(block_done, 1 + b0 + u + 1 + 4 * i)
                    m = sgb[:, 4 * i + u, :]
                    nc.vector.tensor_tensor(m, m, bank[u][:, :], ALU.mult).then_inc(taken[u], 1)

            dve.wait_ge(lora_mm, 2 * KD)
            nc.vector.memset(sh[:, :, 0:1], 0.0).then_inc(zeroed, 1)
            t0 = USES["rw"]
            per = 2 * (3 + 2 + 1 + 2 + 2 + 3)
            with dve.Fori(0, PAIRS // 2) as i:
                step.enter(i, per)
                for pp in range(2):
                    p = 2 * i + pp
                    for s, dst in enumerate((rr[:, p, :], t_k[:, :], rv[:, p, :])):
                        dve.wait_ge(taken[s], 1 + t0 + pp + 1 + 2 * i)
                        dve.wait_ge(shifted, 1 + 6 * i + 3 * pp + s)
                        chain(nc.vector.tensor_tensor(t_d[:, :], sh[:, s, 0:T], sh[:, s, 1:T + 1], ALU.subtract))
                        mix = PAR["time_mix"] + 8 * s
                        nc.vector.scalar_tensor_tensor(out=dst, in0=t_d[:, :],
                                                       scalar=par[:, bass.ds(mix + p, 1)],
                                                       in1=sh[:, s, 1:T + 1], op0=ALU.mult, op1=ALU.add)\
                            .then_inc(shifted, 1)
                    dve.wait_ge(shifted, 1 + 6 * i + 3 * pp + 3)
                    nc.vector.tensor_scalar(t_kk[:, :], t_k[:, :], par[:, bass.ds(PAR["k_k"] + p, 1)], None, ALU.mult)\
                        .then_inc(kq_ready, 1)
                    dve.wait_ge(lora_ready, 2 * KD)
                    chain(nc.vector.tensor_tensor_scan(t_s[:, :], resets, rb[:, p, :], 0.0, ALU.mult, ALU.add))
                    nc.vector.tensor_tensor(t_sm[:, :], t_s[:, :], rb[:, p, :], ALU.subtract).then_inc(scanned, 1)
                    chain(nc.vector.tensor_scalar(t_d[:, :], rk[:, p, :], -1.0, par[:, bass.ds(PAR["k_a"] + p, 1)],
                                                  ALU.add, ALU.mult))
                    chain(nc.vector.scalar_tensor_tensor(out=t_d[:, :], in0=t_d[:, :], scalar=1.0, in1=t_k[:, :],
                                                         op0=ALU.add, op1=ALU.mult))
                    dve.wait_ge(kk_norm, 1 + 2 * i + pp + 1)
                    chain(nc.vector.tensor_scalar(t_sq[:, :], t_sq[:, :], 1e-12, None, ALU.max))
                    chain(nc.vector.reciprocal(t_sq[:, :], t_sq[:, :]))
                    chain(nc.vector.tensor_tensor(t_kk[:, :], t_kk[:, :], t_sq[:, :], ALU.mult))
                    chain(nc.vector.tensor_tensor(t_sq[:, :], t_kk[:, :], rk[:, p, :], ALU.mult))
                    dve.wait_ge(decays, 6 * i + 3 * pp + 3)
                    chain(nc.vector.tensor_tensor(rk[:, p, :], t_d[:, :], rb[:, p, :], ALU.mult))
                    chain(nc.vector.tensor_tensor(rb[:, p, :], t_sq[:, :], rb[:, p, :], ALU.mult))
                    nc.vector.scalar_tensor_tensor(out=ra[:, p, :], in0=t_kk[:, :], scalar=-1.0, in1=t_sm[:, :],
                                                   op0=ALU.mult, op1=ALU.mult)
                    nc.vector.tensor_tensor(rr[:, p, :], rr[:, p, :], t_s[:, :], ALU.mult)
                    chain(nc.vector.tensor_copy(wend[:, p, :], t_s[:, CH - 1:T:CH]))
                    dve.sem_inc(prepped, 1)
            step.leave(PAIRS // 2)

            dve.wait_ge(gate_out, 1 + 16 * PAIRS)
            chain(nc.vector.memset(a_l[:, :, :], 0.0))
            nc.vector.memset(b_l[:, :, :], 0.0).then_inc(zeroed, 1)
            dve.wait_ge(zeroed, 2)
            with dve.Fori(0, NCH) as c:
                for g in range(2):
                    it = 2 * c + g
                    dve.wait_ge(l_mm, 1 + it)
                    for h, d in enumerate(halves(b_l)):
                        nc.vector.tensor_copy(d, rb[HD * h:HD * h + HD, 4 * g:4 * g + 4, bass.ds(CH * c, CH)])\
                            .then_inc(l_b, 1)

            dve.wait_ge(l_mm, 1 + 2 * NCH)
            chain(nc.vector.memset(tt[:, :, :, :], 0.0))
            chain(nc.vector.memset(tt[:, :, :, :].rearrange("p k a b -> p k (a b)")[:, :, 0::HALF + 1], 1.0))
            dve.wait_ge(ls_loaded, 16 * 2 * NCH)
            for t in range(1, HALF):
                rows = bass.AP(ls, ls[:, t, 0:1].offset, [list(ls[:, 0, 0:1].ap[0]), [HALF * CH + HALF, 2], [0, t], [1, t]])
                chain(nc.vector.tensor_tensor(tprod[:, :, 0:t, 0:t], rows, tt[:, :, 0:t, 0:t], ALU.mult))
                chain(nc.vector.tensor_reduce(tt[:, :, 0:t, t:t + 1], tprod[:, :, 0:t, 0:t], AX.X, ALU.add))
            nc.vector.tensor_copy(t11[:, :, :], tt[:, 0, :, :].rearrange("p a b -> p b a")).then_inc(solved, 2)

            dve.wait_ge(p_kept, 32)
            for buf in (a_bd, b_bd, k_bd, r_bd, v_bd, pd, l21, t11b, state[0]):
                nc.vector.memset(buf[:, :, :], 0.0)
            chain(nc.vector.memset(state[1][:, :, :], 0.0))
            dve.sem_inc(zeroed, 1)

            def four(b):
                return bank[b][:, :].rearrange("p (n s) -> p n s", n=4)

            with dve.Fori(0, NCH) as c:
                step.enter(c, 2)
                for g in range(2):
                    it = 2 * c + g
                    g4 = 4 * g
                    dve.wait_ge(c_s, 1 + it)
                    for dst, src in ((b_bd, rb), (k_bd, rk), (v_bd, rv)):
                        for h, d in enumerate(halves(dst)):
                            nc.vector.tensor_copy(d, src[HD * h:HD * h + HD, g4:g4 + 4, bass.ds(CH * c, CH)])\
                                .then_inc(c_dve, 1)
                    for n, dst in enumerate((vt, bt, kt)):
                        dve.wait_ge(c_tr, 3 * it + n + 1)
                        nc.vector.tensor_copy(dst[:, :, :], four(n)).then_inc(c_us, 1)
                    for n, (dst, mask) in enumerate(((m_rb, incl), (m_ak, strict), (m_rk, incl))):
                        dve.wait_ge(c_gram, 3 * it + n + 1)
                        nc.vector.tensor_tensor(dst[:, :, :], four(3 + n), mask.unsqueeze(1).to_broadcast([P, 4, P]),
                                                ALU.mult).then_inc(c_us, 1)
                    dve.wait_ge(c_ag, it + 1)
                    nc.vector.tensor_tensor(m_p[:, :, :], pd[:, :, :], four(7), ALU.add).then_inc(c_mat, 1)
                    dve.wait_ge(c_u, it + 1)
                    nc.vector.tensor_copy(m_u[:, :, :], four(7)).then_inc(c_us, 1)
                    dve.wait_ge(c_s, 1 + it + 1)
                    chain(nc.vector.tensor_tensor(state[g][:, :, :], state[g][:, :, :], four(1), ALU.add))
                    nc.vector.tensor_tensor(state[g][:, :, :], state[g][:, :, :],
                                            wend[:, g4:g4 + 4, bass.ds(c, 1)].to_broadcast([P, 4, P]), ALU.mult)\
                        .then_inc(c_ss, 1)
            step.leave(NCH)

            dve.wait_ge(c_ys, 1 + 4 * NCH)
            for p in range(PAIRS):
                nc.vector.tensor_scalar(rkw[:, p, :], headsum, gain("r_k", p), None, ALU.mult).then_inc(rkw_ready, 1)
            for p in range(PAIRS):
                dve.wait_ge(p_mean, p + 1)
                nc.vector.scalar_tensor_tensor(out=g_d[:, :], in0=bank[4][:, :], scalar=-1.0 / HD, in1=ra[:, p, :],
                                               op0=ALU.mult, op1=ALU.add).then_inc(p_diff, 1)
                nc.vector.tensor_tensor(g_b[:, :], rr[:, p, :], rk[:, p, :], ALU.mult).then_inc(p_rk, 1)
                dve.wait_ge(p_ss, p + 1)
                nc.vector.tensor_scalar(g_r[:, :], bank[5][:, :], 1.0 / HD, GN_EPS, ALU.mult, ALU.add)\
                    .then_inc(p_var, 1)
                dve.wait_ge(p_sd, p + 1)
                chain(nc.vector.reciprocal(g_r[:, :], g_r[:, :]))
                chain(nc.vector.tensor_tensor(g_d[:, :], g_d[:, :], g_r[:, :], ALU.mult))
                chain(nc.vector.tensor_scalar(g_d[:, :], g_d[:, :], gain("gn_weight", p), gain("gn_bias", p),
                                              ALU.mult, ALU.add))
                dve.wait_ge(p_bonus, p + 1)
                chain(nc.vector.tensor_tensor(g_b[:, :], rv[:, p, :], bank[6][:, :], ALU.mult))
                chain(nc.vector.tensor_tensor(g_d[:, :], g_d[:, :], g_b[:, :], ALU.add))
                dve.wait_ge(p_gate, p + 1)
                nc.vector.tensor_tensor(g_c[:, :], g_d[:, :], bank[7][:, :], ALU.mult).then_inc(p_y, 1)
                dve.wait_ge(h_hi, 2 * KD + p + 1)
                nc.vector.tensor_tensor(hlo[:, p, :], g_c[:, :], hhi[:, p, :].bitcast(F32), ALU.subtract)\
                    .then_inc(h_lo, 1)

            b0 = FIRST["oa"]
            dve.wait_ge(sga_loaded, 16 * KD)
            per = 4
            with dve.Fori(0, 2) as i:
                step.enter(i, per)
                for u in range(4):
                    m = 4 * i + u
                    dve.wait_ge(block_done, 1 + b0 + u + 1 + 4 * i)
                    nc.vector.tensor_tensor(mtmp[:, u % 2, :], sga[:, m, :], bank[u][:, :], ALU.mult)\
                        .then_inc(taken[u], 1)
                    dve.wait_ge(taken[u], 1 + USES["oa"] + 1 + i)
                    nc.vector.tensor_tensor(mtmp[:, u % 2, :], mtmp[:, u % 2, :], sgb[:, m, :], ALU.add)\
                        .then_inc(merged, 1)
                    dve.wait_ge(y_hi, PAIRS + u + 1 + 4 * i)
                    chain(nc.vector.tensor_tensor(ylo[:, m, :], mtmp[:, u % 2, :], yhi[:, m, :].bitcast(F32),
                                                  ALU.subtract))
            step.leave(2)
            dve.sem_inc(y_lo, KD)
            b0 = FIRST["out"]
            with dve.Fori(0, 2) as i:
                for u in range(4):
                    xm = x[:, 4 * i + u, :]
                    dve.wait_ge(block_done, 1 + b0 + u + 1 + 4 * i)
                    nc.vector.tensor_tensor(xm, xm, bank[u][:, :], ALU.add).then_inc(x_done, 1)
                    dve.wait_ge(x_done, KD + u + 1 + 4 * i)
                    dve.sem_inc(taken[u], 1)
            norm(2, "ffn2_norm", 3 * KD)
            feed("f2", NF)
            down("d2")
            norm(3, "final_norm", 0)

        @block.tensor
        def _(pe):
            def products(u, acc, hi, lo, tiles, first, last):
                n = len(tiles)
                for t, k in enumerate(tiles):
                    a, b = whi[:, u % 2, t, :], wlo[:, u % 2, t, :]
                    nc.tensor.matmul(acc, a, hi[:, k, :], start=first and t == 0, stop=False)
                    nc.tensor.matmul(acc, a, lo[:, k, :], start=False, stop=False)
                    ins = nc.tensor.matmul(acc, b, hi[:, k, :], start=False, stop=last and t == n - 1)
                ins.then_inc(block_done, 1)

            def project(first, per, i, u, hi, lo):
                pe.wait_ge(lo_ready, first + u + 1 + per * i)
                products(u, bank[u % 4][:, :], hi, lo, range(8), True, True)

            def norm(which, h0):
                pe.wait_ge(n_sum, which + 1)
                nc.tensor.matmul(bank[4][:, :], ones, rstd[:, :], start=True, stop=True).then_inc(n_mean, 1)
                if which < 3:
                    pe.wait_ge(h_lo, h0 + KD)

            def feed(name, j0):
                b0 = FIRST[name]
                with pe.Fori(0, NF // 2) as i:
                    for u in range(4):
                        if u % 2 == 0:
                            pe.wait_ge(prod_ready, 2 + j0 + u // 2 - 1 + 2 * i)
                        project(b0, 4, i, u, hhi, hlo)

            def down(name, a0):
                b0, t0 = FIRST[name], USES[name]
                pe.wait_ge(act_lo, 1 + a0)
                with pe.Fori(0, 2) as i:
                    for m in range(4):
                        pe.wait_ge(taken[m], 1 + t0 + i)
                        for k in range(3):
                            u = 3 * m + k
                            pe.wait_ge(lo_ready, b0 + u + 1 + 12 * i)
                            products(u, bank[m][:, :], ahi, alo, range(8 * k, min(8 * k + 8, NF)), k == 0, k == 2)

            begin_at_one(pe, block_done, ptr, pv_done, l_mm, c_s, c_y)
            pe.wait_ge(params, 32)
            norm(0, 0)
            feed("f1", 0)
            down("d1", NF)
            norm(1, KD)

            b0, t0 = FIRST["idx"], USES["idx"]
            for u in range(8):
                pe.wait_ge(taken[u % 4], 1 + t0 + u // 4)
                project(b0, 0, 0, u, hhi, hlo)
            pe.wait_ge(taken[1], 1 + t0 + 2)
            for q in range(NQ):
                ins = nc.tensor.transpose(bank[4][:, P * q:P * q + P], iwt[:, P * q:P * q + P], ident)
            ins.then_inc(iwt_done, 1)
            pe.wait_ge(taken[0], 1 + t0 + 2)
            pe.wait_ge(taken[3], 1 + t0 + 1)
            for n in range(3 * IDX_HEADS):
                q, hd = n // IDX_HEADS + 1, n % IDX_HEADS
                o = HD * (hd % 2)
                if n == 0:
                    pe.wait_ge(iw_ready, 1)
                if n >= 4:
                    pe.wait_ge(relu_ready, n - 3)
                nc.tensor.matmul(bank[4 + n % 4][:, 0:P * (q + 1)], iq[o:o + HD, hd // 2, P * q:P * q + P],
                                 ik[o:o + HD, 0:P * (q + 1)], start=True, stop=True).then_inc(sc_done, 1)

            b0, t0 = FIRST["att"], USES["att"]
            with pe.Fori(0, PAIRS // 2) as i:
                for pp in range(2):
                    for u in range(4):
                        pe.wait_ge(taken[u], 1 + t0 + pp + 2 * i)
                        project(b0, 8, i, 4 * pp + u, hhi, hlo)
                    pe.wait_ge(taken[2], 1 + t0 + pp + 1 + 2 * i)
                    pe.wait_ge(y_lo, 1 + 2 * i + pp)
                    pe.wait_ge(relu_ready, 3 * IDX_HEADS)
                    for q in range(NQ):
                        ins = nc.tensor.transpose(bank[7][:, P * q:P * q + P], vf[:, pp, P * q:P * q + P], ident)
                    ins.then_inc(vt_done, 1)
                    pe.wait_ge(taken[0], 1 + t0 + pp + 1 + 2 * i)
                    pe.wait_ge(taken[1], 1 + t0 + pp + 1 + 2 * i)
                    for hh in range(2):
                        o = HD * hh
                        head = 4 * i + 2 * pp + hh
                        pe.wait_ge(pt_taken, 1 + 4 * head)
                        for q in range(NQ):
                            w = P * (q + 1)
                            c0 = P if q == 1 else 0
                            ins = nc.tensor.matmul(bank[(4, 4, 5, 6)[q]][:, c0:c0 + w], qs[o:o + HD, pp, P * q:P * q + P],
                                                   ks[o:o + HD, pp, 0:w], start=True, stop=True)
                            if q != 0:
                                ins.then_inc(logit, 1)
                        for kt_, (lo_q, bk, c0) in enumerate([(0, 4, 0), (1, 5, 0), (2, 6, 0), (3, 6, 2 * P)]):
                            pe.wait_ge(prob_ready, 4 * head + 4)
                            for q in range(lo_q, NQ):
                                ins = nc.tensor.transpose(bank[bk][:, c0 + P * (q - lo_q):c0 + P * (q - lo_q) + P],
                                                          prob[:, q, P * kt_:P * kt_ + P], ident)
                            if kt_ != 2:
                                ins.then_inc(ptr, 1)
                        if hh == 0:
                            pe.wait_ge(vs_ready, 2 * i + pp + 1)
                        pe.wait_ge(pt_taken, 1 + 4 * head + 4)
                        for kt_ in range(NQ):
                            ins = nc.tensor.matmul(bank[7][o:o + HD, P * kt_:T], vs[:, pp, P * kt_ + o:P * kt_ + o + HD],
                                                   probt[:, kt_, P * kt_:T], start=(kt_ == 0), stop=(kt_ == NQ - 1))
                        ins.then_inc(pv_done, 1)

            b0, t0 = FIRST["ob"], USES["ob"]
            pe.wait_ge(y_lo, 1 + PAIRS)
            with pe.Fori(0, 2) as i:
                for u in range(4):
                    pe.wait_ge(taken[u], 1 + t0 + i)
                    project(b0, 4, i, u, yhi, ylo)

            pe.wait_ge(lx_ready, 3)
            pe.wait_ge(lora_loaded, 16)
            for n in range(2 * KD):
                if n >= 4:
                    pe.wait_ge(lora_ready, n - 3)
                m = n // 2
                nc.tensor.matmul(bank[4 + n % 4][:, :], lora[:, n % 2, P * m:P * m + P], lx[:, :],
                                 start=True, stop=True).then_inc(lora_mm, 1)

            b0, t0 = FIRST["rw"], USES["rw"]
            pe.wait_ge(lora_ready, 2 * KD)
            with pe.Fori(0, PAIRS // 2) as i:
                for pp in range(2):
                    for u in range(4):
                        pe.wait_ge(taken[u], 1 + t0 + pp + 2 * i)
                        project(b0, 8, i, 4 * pp + u, hhi, hlo)
                    pe.wait_ge(kq_sq, 2 * i + pp + 1)
                    pe.wait_ge(kk_norm, 1 + 2 * i + pp)
                    nc.tensor.matmul(bank[4][:, :], headsum, t_sq[:, :], start=True, stop=True).then_inc(kk_ss, 1)

            pe.wait_ge(taken[0], 1 + t0 + 8)
            with pe.Fori(0, NCH) as c:
                for g in range(2):
                    it = 2 * c + g
                    pe.wait_ge(l_a, 2 * it + 2)
                    pe.wait_ge(l_b, 2 * it + 2)
                    pe.wait_ge(l_ready, 1 + 2 * it)
                    for n in range(4):
                        ins = nc.tensor.matmul(bank[0][:, P * n:P * n + P], a_l[:, n, :], b_l[:, n, :],
                                               start=True, stop=True)
                    ins.then_inc(l_mm, 1)

            def group(b, terms):
                for n in range(4):
                    for k, (lhs, rhs) in enumerate(terms):
                        ins = nc.tensor.matmul(bank[b][:, P * n:P * n + P], lhs[:, n, :], rhs[:, n, :],
                                               start=k == 0, stop=k == len(terms) - 1)
                return ins

            pe.wait_ge(taken[1], 1 + t0 + 8)
            pe.wait_ge(taken[2], 1 + t0 + 8)
            pe.wait_ge(taken[3], 1 + t0 + 8)
            with pe.Fori(0, NCH) as c:
                for g in range(2):
                    it = 2 * c + g
                    pe.wait_ge(c_dve, 6 * it + 6)
                    pe.wait_ge(c_ys, 1 + 2 * it)
                    for n, src in enumerate((v_bd, b_bd, k_bd)):
                        for j in range(4):
                            ins = nc.tensor.transpose(bank[n][:, P * j:P * j + P], src[:, j, :], ident)
                        ins.then_inc(c_tr, 1)
                    pe.wait_ge(c_act, 4 * it + 4)
                    group(3, [(b_bd, r_bd)]).then_inc(c_gram, 1)
                    group(4, [(k_bd, a_bd)]).then_inc(c_gram, 1)
                    group(5, [(k_bd, r_bd)]).then_inc(c_gram, 1)
                    pe.wait_ge(c_loaded, 128 * it + 128)
                    group(6, [(l21, pd)]).then_inc(c_g, 1)
                    pe.wait_ge(c_gs, it + 1)
                    group(7, [(t11b, m_g)]).then_inc(c_ag, 1)
                    pe.wait_ge(c_us, 7 * it + 6)
                    group(6, [(a_bd, state[g]), (m_ak, vt)]).then_inc(c_x, 1)
                    pe.wait_ge(c_mat, 1 + it + 1)
                    pe.wait_ge(c_xs, it + 1)
                    group(7, [(m_p, m_x)]).then_inc(c_u, 1)
                    pe.wait_ge(c_us, 7 * it + 7)
                    group(0, [(state[g], r_bd), (m_u, m_rb), (vt, m_rk)]).then_inc(c_y, 1)
                    group(1, [(bt, m_u), (kt, vt)]).then_inc(c_s, 1)
                    pe.wait_ge(c_ss, it + 1)

            for p in range(PAIRS):
                if p == 0:
                    pe.wait_ge(c_ys, 1 + 4 * NCH)
                    pe.wait_ge(rkw_ready, PAIRS)
                    pe.wait_ge(g_loaded, 16)
                else:
                    pe.wait_ge(p_y, p)
                nc.tensor.matmul(bank[4][:, :], headsum, ra[:, p, :], start=True, stop=True).then_inc(p_mean, 1)
                nc.tensor.matmul(bank[7][:, :], glora[:, P * p:P * p + P], xg[:, :], start=True, stop=True)\
                    .then_inc(p_gate, 1)
                pe.wait_ge(p_rk, p + 1)
                nc.tensor.matmul(bank[6][:, :], rkw[:, p, :], g_b[:, :], start=True, stop=True).then_inc(p_bonus, 1)
                pe.wait_ge(p_sq, p + 1)
                nc.tensor.matmul(bank[5][:, :], headsum, g_q[:, :], start=True, stop=True).then_inc(p_ss, 1)

            b0, t0 = FIRST["oa"], USES["oa"]
            pe.wait_ge(h_lo, 3 * KD)
            with pe.Fori(0, 2) as i:
                for u in range(4):
                    pe.wait_ge(taken[u], 1 + t0 + i)
                    project(b0, 4, i, u, hhi, hlo)
            b0, t0 = FIRST["out"], USES["out"]
            pe.wait_ge(y_lo, 1 + PAIRS + KD)
            with pe.Fori(0, 2) as i:
                for u in range(4):
                    pe.wait_ge(taken[u], 1 + t0 + i)
                    project(b0, 4, i, u, yhi, ylo)
            norm(2, 3 * KD)
            feed("f2", NF)
            down("d2", 2 * NF)
            norm(3, 0)


def _tiles(w):
    k, n = w.shape
    return w.reshape(k // P, P, n // P, P).transpose(2, 1, 0, 3)


def _down(w):
    t = _tiles(w)
    pad = np.zeros((t.shape[0], P, 24 - NF, P), w.dtype)
    return np.concatenate([t, pad], 2).reshape(KD, P, 3, 8, P).transpose(0, 2, 1, 3, 4).reshape(DBLK, P, 8, P)


def _stream(inp):
    w_in = inp["w_in"][0]
    c = np.cumsum([0, D, D, D, 128, 128, D, D, D, 512, 64, 8, D, D])
    r, k, v, xwa, xg, q, ka, va, iq, ik, iw, ga, gb = [w_in[:, a:b] for a, b in zip(c[:-1], c[1:])]
    pad = np.zeros((D, P - IDX_HEADS), w_in.dtype)

    def woven(*parts):
        t = np.stack([_tiles(p) for p in parts], 1)
        return t.reshape(-1, *t.shape[2:])

    return np.concatenate([
        woven(inp["ffn1_w_gate"][0], inp["ffn1_w_up"][0]), _down(inp["ffn1_w_down"][0]),
        _tiles(np.concatenate([iq, ik, ik, iw, pad, xwa, xg], 1)),
        woven(q, ka, va, gb), _tiles(inp["w_out_attn"][0]),
        woven(r, k, v, ga), _tiles(inp["w_out_rwkv"][0]), _tiles(inp["w_out"][0]),
        woven(inp["ffn2_w_gate"][0], inp["ffn2_w_up"][0]), _down(inp["ffn2_w_down"][0])])


def _params(inp):
    cols = [np.ravel(inp[n]).reshape(-1, P).T for n in PAR]
    return np.ascontiguousarray(np.concatenate(cols, 1))


def _constants():
    c = np.zeros((P, NCST), np.float32)
    i = np.arange(P)
    same = i[:, None] // HD == i[None, :] // HD
    c[:, C_ID:C_ID + P] = np.eye(P)
    c[:, C_ONE:C_ONE + P] = 1
    c[:, C_HEAD:C_HEAD + P] = same
    c[:, C_STRICT:C_STRICT + P] = same & (i[:, None] < i[None, :])
    c[:, C_INCL:C_INCL + P] = same & (i[:, None] <= i[None, :])
    c[:, C_SCAN:C_SCAN + T] = np.arange(T) % CH != 0
    c[:, C_VIS:C_VIS + P] = i[None, :] // CH <= i[:, None] // CH
    return c


def _layout(inputs):
    inp = {k: np.asarray(v) for k, v in inputs.items()}
    lora = np.zeros((P, 2, D), np.float32)
    lora[0:64, 0] = inp["decay_lora"][0]
    lora[64:128, 1] = inp["aaa_lora"][0]
    return {
        "x_in": np.ascontiguousarray(inp["x"][0].T.reshape(KD, P, T)),
        "ws": np.ascontiguousarray(_stream(inp)),
        "par_in": _params(inp),
        "cst_in": _constants(),
        "lora_in": lora,
        "glora_in": np.ascontiguousarray(inp["gate_lora"][0]),
    }


SHAPES = {"x_in": (KD, P, T), "ws": (NBLK, P, 8, P), "par_in": (P, NPAR), "cst_in": (P, NCST),
          "lora_in": (P, 2, D), "glora_in": (P, D)}
SCRATCH = {"sa_dram": (KD, P, T), "l_dram": (NCH, 2, CH, PAIRS, CH), "pd_dram": (P, 2, HALF, HALF),
           "t11_dram": (P, HALF, HALF)}


def program(nc):
    ins = [nc.dram_tensor(n, s, F32, kind="ExternalInput").ap() for n, s in SHAPES.items()]
    out = nc.dram_tensor("out", (KD, P, T), F32, kind="ExternalOutput").ap()
    scratch = [nc.dram_tensor(n, s, F32, kind="Internal").ap() for n, s in SCRATCH.items()]
    build(nc, *ins, out, *scratch)


def kernel(**inputs):
    import concourse.bacc as _bacc
    from concourse.bass_utils import run_bass_kernel_spmd as _run

    nc = _bacc.Bacc("TRN2", target_bir_lowering=False, num_devices=1)
    program(nc)
    r = _run(nc, [_layout(inputs)], core_ids=[0])
    return r.results[0]["out"].reshape(1, D, T).transpose(0, 2, 1)
```

```python
from contextlib import ExitStack

import numpy as np

import concourse.bass as bass
import concourse.mybir as mybir

F32 = mybir.dt.float32
F32R = mybir.dt.float32r
ALU = mybir.AluOpType
ACT = mybir.ActivationFunctionType
AX = mybir.AxisListType

P = 128
T = 512
D = 1024
KD = D // P
D_FF = 2816
NF = D_FF // P
CH = 64
NCH = T // CH
HEADS = 16
HD = 64
PAIRS = HEADS // 2
IDX_HEADS = 8
TOPK = 128
NQ = T // P
HALF = CH // 2
NORM_EPS = 1e-6
GN_EPS = HD * 1e-5
DECAY_C = float(np.exp(-0.5))
IW_SCALE = IDX_HEADS ** -0.5 * HD ** -0.5
NEG = -3.0e38
MASKED = 1.0e30

DBLK = 3 * KD
PHASES = [("f1", 2 * NF), ("d1", DBLK), ("idx", 8), ("rw", 4 * PAIRS), ("att", 4 * PAIRS),
          ("ob", KD), ("oa", KD), ("out", KD), ("f2", 2 * NF), ("d2", DBLK)]
FIRST, _at, USES, _use = {}, 0, {}, 0
for _n, _c in PHASES:
    FIRST[_n] = _at
    _at += _c
    USES[_n] = _use
    _use += {"f": 0, "d": 2}.get(_n[0], _c // 4)
NBLK = _at

PAR, _at = {}, 0
for _n, _c in [("ffn1_norm", KD), ("mix_norm", KD), ("ffn2_norm", KD), ("final_norm", KD), ("k_k", KD),
               ("k_a", KD), ("r_k", KD), ("gn_weight", KD), ("gn_bias", KD), ("decay_base", KD),
               ("aaa_base", KD), ("time_mix", 26)]:
    PAR[_n] = _at
    _at += _c
NPAR = _at
C_ID, C_ONE, C_HEAD, C_STRICT, C_INCL, C_SCAN, C_VIS, C_EPS, NCST = 0, 128, 256, 384, 512, 640, 1152, 1280, 1282


class Tally:

    def __init__(self, sem):
        self.sem, self.base, self.n, self.turn, self.per = sem, 0, 0, 0, 0

    def mark(self, ins):
        ins.then_inc(self.sem, 1)
        self.n += 1
        return self.value()

    def value(self):
        return self.turn * self.per + (self.base + self.n) if self.per else self.base + self.n

    def enter(self, turn, per):
        self.base, self.n, self.turn, self.per = self.base + self.n, 0, turn, per

    def leave(self, turns):
        assert self.n == self.per, (self.n, self.per)
        self.base, self.n, self.turn, self.per = self.base + self.per * turns, 0, 0, 0


def build(nc, x_in, ws, par_in, cst_in, lora_in, glora_in, out, sa_dram, sb_dram, rw_dram, l_dram, pd_dram,
          t11_dram):
    with ExitStack() as ctx:
        top = [(nc.sbuf_base + 63) // 64 * 64]

        def at(name, shape, dtype, offset):
            return nc.alloc_sbuf_tensor_at(name, shape, dtype, offset=offset)

        def fixed(name, shape, dtype=F32):
            o = top[0]
            size = 4
            for s in shape[1:]:
                size *= s
            top[0] += (size + 31) // 32 * 32
            return at(name, shape, dtype, o)

        x = fixed("x", [P, KD, T])
        raw = fixed("raw", [P, 4, 8, P])
        whi = fixed("whi", [P, 2, 8, P], F32R)
        wlo = fixed("wlo", [P, 2, 8, P], F32R)
        par = fixed("par", [P, NPAR])
        cst = fixed("cst", [P, NCST])
        lx = fixed("lx", [P, T])
        xg = fixed("xg", [P, T])
        wend = fixed("wend", [P, PAIRS, NCH])
        top8 = fixed("top8", [P, 8])
        rmax = fixed("rmax", [P, 4 * NQ])
        R0 = top[0]
        K = 1024

        ident, ones, headsum = cst[:, C_ID:C_ID + P], cst[:, C_ONE:C_ONE + P], cst[:, C_HEAD:C_HEAD + P]
        strict, incl = cst[:, C_STRICT:C_STRICT + P], cst[:, C_INCL:C_INCL + P]
        resets, visible = cst[:, C_SCAN:C_SCAN + T], cst[:, C_VIS:C_VIS + P]

        def gain(name, k):
            return par[:, PAR[name] + k:PAR[name] + k + 1]

        hhi = at("hhi", [P, KD, T], F32R, R0)
        hlo = at("hlo", [P, KD, T], F32R, R0 + 16 * K)
        yhi = at("yhi", [P, KD, T], F32R, R0 + 118 * K)
        ylo = at("ylo", [P, KD, T], F32R, R0 + 134 * K)
        ahi = at("ahi", [P, NF, T], F32R, R0 + 32 * K)
        alo = at("alo", [P, NF, T], F32R, R0 + 76 * K)
        silu_g = at("silu_g", [P, T], F32, R0 + 120 * K)
        prod = at("prod", [P, T], F32, R0 + 122 * K)
        sq = at("sq", [P, KD, T], F32, R0)
        hn = at("hn", [P, KD, T], F32, R0 + 16 * K)
        ssums = [at(f"ssum{n}", [P, T], F32, R0 + k * K) for n, k in enumerate((124, 124, 102, 124))]
        rstds = [at(f"rstd{n}", [P, T], F32, R0 + k * K) for n, k in enumerate((126, 126, 104, 126))]
        iq = at("iq", [P, 4, T], F32, R0 + 32 * K)
        ik = at("ik", [P, T], F32, R0 + 40 * K)
        iwt = at("iwt", [P, T], F32, R0 + 42 * K)
        iw = at("iw", [P, NQ, P], F32, R0 + 44 * K)
        relu = at("relu", [P, 2, T], F32, R0 + 46 * K)
        score = at("score", [P, 3, T], F32, R0 + 56 * K)
        work = at("work", [P, 3, T], F32, R0 + 62 * K)
        bias = at("bias", [P, NQ, T], F32, R0 + 48 * K)
        shl = at("shl", [P, 2, T + 8], F32, R0 + 76 * K)
        shd = at("shd", [P, 2, T], F32, R0 + 81 * K)
        lora = at("lora", [P, 2, D], F32, R0 + 68 * K)
        zs = at("zs", [P, PAIRS, T], F32, R0 + 76 * K)
        az = at("az", [P, PAIRS, T], F32, R0 + 92 * K)
        kr = at("kr", [P, 2, T], F32, R0 + 32 * K)
        t_v = at("t_v", [P, T], F32, R0 + 36 * K)
        t_r = at("t_r", [P, T], F32, R0 + 38 * K)
        t_k = at("t_k", [P, T], F32, R0 + 40 * K)
        t_kk = at("t_kk", [P, T], F32, R0 + 42 * K)
        t_sq = at("t_sq", [P, T], F32, R0 + 44 * K)
        t_s = at("t_s", [P, T], F32, R0 + 46 * K)
        t_sm = at("t_sm", [P, T], F32, R0 + 48 * K)
        t_d = at("t_d", [P, T], F32, R0 + 50 * K)
        t_e = at("t_e", [P, T], F32, R0 + 52 * K)
        a_l = at("a_l", [P, NCH, P], F32, R0 + 68 * K)
        b_l = at("b_l", [P, NCH, P], F32, R0 + 72 * K)
        sh = at("sh", [P, 3, T + 8], F32, R0 + 108 * K)
        gt = at("gt", [P, T], F32, R0 + 114 * K + 128)
        lst = at("lst", [P, NCH, P], F32, R0 + 146 * K)
        qa = at("qa", [P, PAIRS, T], F32, R0 + 118 * K)
        ka = at("ka", [P, PAIRS, T], F32, R0 + 134 * K)
        va = at("va", [P, PAIRS, T], F32, R0 + 32 * K)
        vf = at("vf", [P, T], F32, R0 + 112 * K)
        ls = at("ls", [P, CH, CH], F32, R0 + 76 * K)
        tt = at("tt", [P, CH, CH], F32, R0 + 92 * K)
        tprod = at("tprod", [P, 2, HALF, HALF], F32, R0 + 68 * K)
        t11 = at("t11", [P, HALF, HALF], F32, R0 + 108 * K)
        qs = at("qs", [P, T], F32, R0 + 80 * K)
        ks = at("ks", [P, T], F32, R0 + 82 * K)
        vs = at("vs", [P, T], F32, R0 + 84 * K)
        prob = at("prob", [P, NQ, T], F32, R0 + 86 * K)
        probt = at("probt", [P, NQ, T], F32, R0 + 94 * K)
        abkrv = [at(f"abkrv{g}", [P, 4, 5, P], F32, R0 + 10 * K * g) for g in (0, 1)]
        a_bd, b_bd, k_bd, r_bd, v_bd = [[m[:, :, j, :] for m in abkrv] for j in range(5)]
        slots = iter([R0 + 20 * K + 2 * K * n for n in range(6)] + [R0 + 56 * K + 2 * K * n for n in range(12)])

        def bd(name):
            return at(name, [P, 4, P], F32, next(slots))

        pd, t11b, l21 = [[bd(f"{n}_{g}") for g in (0, 1)] for n in ("pd", "t11b", "l21")]
        m_x, m_u, m_g, m_p, vt, bt, kt = [bd(n) for n in ("m_x", "m_u", "m_g", "m_p", "vt", "bt", "kt")]
        m_ak, m_rb, m_rk = bd("m_ak"), bd("m_rb"), bd("m_rk")
        state = [bd("state0"), bd("state1")]
        yo = at("yo", [P, PAIRS, T], F32, R0 + 102 * K)
        sgb = at("sgb", [P, KD, T], F32, R0 + 32 * K)
        rkw = at("rkw", [P, PAIRS, P], F32, R0 + 48 * K)
        glora = at("glora", [P, D], F32, R0 + 52 * K)
        krv = at("krv", [P, 2, 3, T], F32, R0 + 56 * K)
        g_d = at("g_d", [P, T], F32, R0 + 68 * K)
        g_q = at("g_q", [P, T], F32, R0 + 70 * K)
        g_r = at("g_r", [P, T], F32, R0 + 72 * K)
        g_b = at("g_b", [P, T], F32, R0 + 74 * K)
        g_c = at("g_c", [P, T], F32, R0 + 76 * K)
        sga = at("sga", [P, KD, T], F32, R0 + 86 * K)
        mtmp = at("mtmp", [P, 2, T], F32, R0 + 80 * K)
        outt = at("outt", [P, KD, T], F32, R0)

        bank = [ctx.enter_context(nc.psum_tensor(f"bank{n}", [P, T], F32)) for n in range(8)]

        def sem(name):
            return ctx.enter_context(nc.semaphore(name))

        loaded = [sem(f"loaded{n}") for n in range(4)]
        hi_ready, lo_ready, block_done = sem("hi_ready"), sem("lo_ready"), sem("block_done")
        taken = [sem(f"taken{n}") for n in range(4)]
        params = sem("params")
        x_loaded = sem("x_loaded")
        x_done = sem("x_done")
        n_sq, n_sum, n_mean, n_sd = sem("n_sq"), sem("n_sum"), sem("n_mean"), sem("n_sd")
        n_hn, h_hi, h_lo = sem("n_hn"), sem("h_hi"), sem("h_lo")
        silu_ready, prod_ready, act_hi, act_lo = sem("silu_ready"), sem("prod_ready"), sem("act_hi"), sem("act_lo")
        dve_step, act_step = sem("dve_step"), sem("act_step")
        iwt_done, iw_ready, sc_done, relu_ready, sc_used = (sem("iwt_done"), sem("iw_ready"), sem("sc_done"),
                                                           sem("relu_ready"), sem("sc_used"))
        lx_ready, lx_raw = sem("lx_ready"), sem("lx_raw")
        lora_loaded, lora_mm, lora_ready = sem("lora_loaded"), sem("lora_mm"), sem("lora_ready")
        zeroed = sem("zeroed")
        shifted, kq_ready, kq_sq, kk_ss, kk_norm = (sem("shifted"), sem("kq_ready"), sem("kq_sq"), sem("kk_ss"),
                                                    sem("kk_norm"))
        scanned, decays, prepped = sem("scanned"), sem("decays"), sem("prepped")
        v_kept, kr_kept, ab_kept = sem("v_kept"), sem("kr_kept"), sem("ab_kept")
        sa_kept, sb_kept, l_kept, p_kept = sem("sa_kept"), sem("sb_kept"), sem("l_kept"), sem("p_kept")
        l_mm, l_out, ls_loaded, solved = sem("l_mm"), sem("l_out"), sem("ls_loaded"), sem("solved")
        vt_done, va_ready, biased = sem("vt_done"), sem("va_ready"), sem("biased")
        qk_copied, v_copied = sem("qk_copied"), sem("v_copied")
        logit, negmax, exped, prob_ready = sem("logit"), sem("negmax"), sem("exped"), sem("prob_ready")
        ptr, pt_taken, pv_done, y_hi, y_lo = sem("ptr"), sem("pt_taken"), sem("pv_done"), sem("y_hi"), sem("y_lo")
        c_cleared, c_loaded = [sem("c_clear0"), sem("c_clear1")], [sem("c_loaded0"), sem("c_loaded1")]
        c_tr, c_gram, c_g, c_gs, c_ag = sem("c_tr"), sem("c_gram"), sem("c_g"), sem("c_gs"), sem("c_ag")
        c_av, c_us, c_mat, c_x, c_xs, c_u = (sem("c_av"), sem("c_us"), sem("c_mat"), sem("c_x"), sem("c_xs"),
                                             sem("c_u"))
        c_y, c_ys, c_s, c_ss = sem("c_y"), sem("c_ys"), sem("c_s"), sem("c_ss")
        rkw_ready, krv_loaded, p_mean, p_sq, p_sd, p_ss = (sem("rkw_ready"), [sem("krv_a"), sem("krv_b")],
                                                           sem("p_mean"), sem("p_sq"), sem("p_sd"), sem("p_ss"))
        p_bonus, p_gate, p_y, p_rk, p_diff = sem("p_bonus"), sem("p_gate"), sem("p_y"), sem("p_rk"), sem("p_diff")
        sga_loaded, sgb_loaded, merged, g_loaded = sem("sga_loaded"), sem("sgb_loaded"), sem("merged"), sem("g_loaded")
        settled = sem("settled")
        out_ready, out_kept = sem("out_ready"), sem("out_kept")

        block = ctx.enter_context(nc.Block())

        def settle(engine):
            engine.sem_inc(settled, 1)

        def begin_at_one(engine, *sems):
            for s in sems:
                engine.sem_inc(s, 1)

        def halves(buf):
            return [buf[HD * h:HD * h + HD, :, HD * h:HD * h + HD] for h in (0, 1)]

        @block.sync
        def _(sp):
            sp.dma_start(x[:, :, :], x_in.rearrange("k p t -> p k t")).then_inc(x_loaded, 16)
            sp.dma_start(par[:, :], par_in).then_inc(params, 16)
            sp.dma_start(cst[:, :], cst_in).then_inc(params, 16)
            for u in range(4):
                sp.dma_start(raw[:, u, :, :], ws[u, :, :, :]).then_inc(loaded[u], 16)
            def stream(turns):
                with sp.Fori(*turns) as i:
                    for u in range(4):
                        sp.wait_ge(lo_ready, 4 * i + u - 3)
                        sp.dma_start(raw[:, u, :, :], ws[4 * i + u, :, :, :]).then_inc(loaded[u], 16)

            def stage(g, c):
                g4 = 4 * g
                for h in range(2):
                    o = HD * h
                    sp.dma_start(abkrv[g][o:o + HD, :, :, o:o + HD].rearrange("p n j t -> p (n j) t"),
                                 rw_dram[g4:g4 + 4, :, o:o + HD, bass.ds(CH * c, CH)]
                                 .rearrange("n j p t -> p (n j) t")).then_inc(c_loaded[g], 16)
                for h in range(2):
                    o = HD * h
                    sp.dma_start(l21[g][o + HALF:o + CH, :, o:o + HALF],
                                 l_dram[g4:g4 + 4, h, c, HALF:CH, 0:HALF].rearrange("n t s -> t n s"))\
                        .then_inc(c_loaded[g], 16)
                    sp.dma_start(pd[g][o:o + HD, :, o:o + HD],
                                 pd_dram[g4:g4 + 4, h, c, :, :].rearrange("n s t -> s n t"))\
                        .then_inc(c_loaded[g], 16)
                    sp.dma_start(t11b[g][o:o + HALF, :, o:o + HALF],
                                 t11_dram[g4:g4 + 4, h, c, :, :].rearrange("n a b -> a n b"))\
                        .then_inc(c_loaded[g], 16)

            stream((1, FIRST["ob"] // 4 + 1))
            sp.wait_ge(ab_kept, 1 + 64 * PAIRS)
            sp.wait_ge(kr_kept, 1 + 16 * PAIRS)
            sp.wait_ge(v_kept, 1 + 16 * PAIRS)
            sp.wait_ge(p_kept, 32)
            for g in range(2):
                sp.wait_ge(c_cleared[g], 1)
                stage(g, 0)
            with sp.Fori(1, NCH) as c:
                for g in range(2):
                    sp.wait_ge(c_s, 2 * c + g)
                    stage(g, c)
            stream((FIRST["ob"] // 4 + 1, NBLK // 4))
            sp.wait_ge(out_ready, KD)
            sp.dma_start(out.rearrange("k p t -> p k t"), outt[:, :, :]).then_inc(out_kept, 16)
            sp.wait_ge(out_kept, 16)

        @block.gpsimd
        def _(pool):
            def low_parts(turns):
                with pool.Fori(*turns) as i:
                    for u in range(4):
                        pool.wait_ge(hi_ready, 4 * i + u + 1)
                        nc.gpsimd.tensor_tensor(wlo[:, u % 2, :, :], raw[:, u, :, :],
                                                whi[:, u % 2, :, :].bitcast(F32), ALU.subtract).then_inc(lo_ready, 1)

            def stage(p):
                nc.gpsimd.tensor_copy(qs[:, :], qa[:, p, :]).then_inc(qk_copied, 1)
                nc.gpsimd.tensor_copy(ks[:, :], ka[:, p, :]).then_inc(qk_copied, 1)

            low_parts((0, FIRST["ob"] // 4))
            pool.wait_ge(solved, 2)
            pool.wait_ge(va_ready, PAIRS)
            stage(0)
            nc.gpsimd.tensor_copy(vs[:, :], va[:, 0, :]).then_inc(v_copied, 1)
            pool.wait_ge(block_done, 1 + FIRST["ob"])
            for buf in (abkrv[1][:, :, :, :], pd[1][:, :, :], l21[1][:, :, :]):
                nc.gpsimd.memset(buf, 0.0)
            nc.gpsimd.memset(t11b[1][:, :, :], 0.0).then_inc(c_cleared[1], 1)
            with pool.Fori(1, NCH) as c:
                pool.wait_ge(logit, 6 * c)
                settle(pool)
                stage(c)
                pool.wait_ge(pv_done, 1 + 2 * c)
                settle(pool)
                nc.gpsimd.tensor_copy(vs[:, :], va[:, c, :]).then_inc(v_copied, 1)
            low_parts((FIRST["ob"] // 4, NBLK // 4))

        @block.scalar
        def _(act):

            def split(first, per, i, u):
                b = first + u
                act.wait_ge(loaded[b % 4], 16 * (b // 4 + 1) + 4 * per * i)
                if b >= 2 or per:
                    act.wait_ge(block_done, b + per * i)
                nc.scalar.copy(whi[:, b % 2, :, :], raw[:, b % 4, :, :]).then_inc(hi_ready, 1)

            def norm(which, src_ready):
                rstd = rstds[which]
                for k in range(KD):
                    if src_ready is not None:
                        act.wait_ge(x_done, src_ready + k + 1)
                    nc.scalar.activation(sq[:, k, :], x[:, k, :], ACT.Square).then_inc(n_sq, 1)
                act.wait_ge(n_mean, which + 1)
                nc.scalar.activation(rstd[:, :], bank[4][:, :], ACT.Sqrt, scale=1.0 / D,
                                     bias=cst[:, C_EPS:C_EPS + 1]).then_inc(n_sd, 1)
                if which == 3:
                    return
                for k in range(KD):
                    act.wait_ge(n_hn, which * KD + k + 1)
                    nc.scalar.copy(hhi[:, k, :], hn[:, k, :]).then_inc(h_hi, 1)

            def feed(name, j0):
                b0 = FIRST[name]
                with act.Fori(0, NF // 2) as i:
                    for jj in range(2):
                        u = 2 * jj
                        split(b0, 4, i, u + 1)
                        act.wait_ge(block_done, 1 + b0 + u + 1 + 4 * i)
                        nc.scalar.activation(silu_g[:, :], bank[u][:, :], ACT.Silu).then_inc(silu_ready, 1)
                        split(b0, 4, i, u + 2)
                        act.wait_ge(prod_ready, 2 + j0 + jj + 1 + 2 * i)
                        settle(act)
                        nc.scalar.copy(ahi[:, 2 * i + jj, :], prod[:, :]).then_inc(act_hi, 1)

            def down(name, last):
                b0 = FIRST[name]
                if not last:
                    with act.Fori(0, 2) as i:
                        for u in range(12):
                            split(b0, 12, i, u + 1)
                else:
                    for u in range(2 * 12 - 1):
                        split(b0, 0, 0, u + 1)

            begin_at_one(act, pt_taken, sa_kept, sb_kept, v_kept, kr_kept, ab_kept, l_kept, l_out, c_ys, c_av)
            split(0, 0, 0, 0)
            act.wait_ge(x_loaded, 16)
            norm(0, None)
            feed("f1", 0)
            down("d1", False)
            norm(1, 0)

            act.dma_start(lora[:, :, :], lora_in).then_inc(lora_loaded, 16)
            b0 = FIRST["idx"]
            for u in range(8):
                split(b0, 0, 0, u + 1)
                act.wait_ge(block_done, 1 + b0 + u + 1)
                if u < 4:
                    nc.scalar.copy(iq[:, u, :], bank[u][:, :]).then_inc(taken[u], 1)
                elif u == 4:
                    nc.scalar.copy(ik[:, :], bank[0][:, :]).then_inc(taken[0], 1)
                elif u == 5:
                    nc.scalar.mul(iwt[:, :], bank[1][:, :], IW_SCALE).then_inc(taken[1], 1)
                else:
                    nc.scalar.copy(shl[:, u - 6, 1:T + 1], bank[u - 4][:, :]).then_inc(taken[u - 4], 1)
            act.wait_ge(lx_raw, 2)
            nc.scalar.activation(lx[0:64, :], shd[0:64, 0, :], ACT.Tanh).then_inc(lx_ready, 1)
            nc.scalar.copy(lx[64:128, :], shd[64:128, 0, :]).then_inc(lx_ready, 1)
            nc.scalar.activation(xg[:, :], shd[:, 1, :], ACT.Sigmoid).then_inc(lx_ready, 1)
            for n in range(3 * IDX_HEADS):
                w = P * (n // IDX_HEADS + 2)
                act.wait_ge(sc_done, n + 1)
                if n >= 2:
                    act.wait_ge(sc_used, n - 1)
                nc.scalar.activation(relu[:, n % 2, 0:w], bank[4 + n % 4][:, 0:w], ACT.Relu)\
                    .then_inc(relu_ready, 1)

            act.wait_ge(lx_ready, 3)
            for n in range(2 * KD):
                m, which = n // 2, n % 2
                act.wait_ge(lora_mm, n + 1)
                nc.scalar.activation((zs, az)[which][:, m, :], bank[4 + n % 4][:, :], ACT.Sigmoid,
                                     bias=gain(("decay_base", "aaa_base")[which], m)).then_inc(lora_ready, 1)

            def finish_decays(p):
                act.wait_ge(kk_ss, p + 1)
                nc.scalar.activation(t_sq[:, :], bank[4][:, :], ACT.Sqrt).then_inc(kk_norm, 1)
                act.wait_ge(scanned, p + 1)
                nc.scalar.activation(t_e[:, :], t_s[:, :], ACT.Exp, scale=DECAY_C).then_inc(decays, 1)
                nc.scalar.activation(t_sm[:, :], t_sm[:, :], ACT.Exp, scale=-DECAY_C).then_inc(decays, 1)
                nc.scalar.activation(t_s[:, :], t_s[:, :], ACT.Exp, scale=-DECAY_C).then_inc(decays, 1)
                act.dma_start(rw_dram[p, 4, :, :], t_v[:, :]).then_inc(v_kept, 16)

            def keep_pair(p):
                act.wait_ge(prepped, p + 1)
                act.dma_start(rw_dram[p, 2:4, :, :].rearrange("j p t -> p j t"), kr[:, :, :]).then_inc(kr_kept, 16)
                for j, buf in enumerate((a_l, b_l)):
                    for h in range(2):
                        o = HD * h
                        act.dma_start(rw_dram[p, j, o:o + HD, :].rearrange("p (c t) -> p c t", c=NCH),
                                      buf[o:o + HD, :, o:o + HD]).then_inc(ab_kept, 16)
                act.wait_ge(l_kept, 1 + 32 * p)
                for n in range(2):
                    act.wait_ge(l_mm, 2 * p + n + 1)
                    nc.scalar.copy(lst[:, 4 * n:4 * n + 4, :], bank[5 + n][:, :].rearrange("p (n s) -> p n s", n=4))\
                        .then_inc(l_out, 1)
                act.wait_ge(l_out, 1 + 2 * p + 2)
                for h in range(2):
                    o = HD * h
                    act.dma_start(l_dram[p, h].rearrange("c t s -> t c s"), lst[o:o + HD, :, o:o + HD])\
                        .then_inc(l_kept, 16)

            def rwkv_pair(p, p_before):
                b0, t0 = FIRST["rw"], USES["rw"]
                for s in range(4):
                    split(b0, 4, p, s + 1)
                    if s == 0 and p_before is not None:
                        finish_decays(p_before)
                    act.wait_ge(block_done, 1 + b0 + s + 1 + 4 * p)
                    if s < 3:
                        if s == 0:
                            act.wait_ge(zeroed, 1)
                        if p_before is not None:
                            act.wait_ge(shifted, 1 + 3 * p_before + (2, 1, 3)[s])
                        nc.scalar.copy(sh[:, s, 1:T + 1], bank[s][:, :]).then_inc(taken[s], 1)
                    if s == 2:
                        act.wait_ge(kq_ready, p + 1)
                        nc.scalar.activation(t_sq[:, :], t_kk[:, :], ACT.Square).then_inc(kq_sq, 1)
                        if p_before is not None:
                            keep_pair(p_before)
                    if s == 3:
                        act.wait_ge(sa_kept, 1 + 16 * p)
                        nc.scalar.activation(gt[:, :], bank[3][:, :], ACT.Sigmoid).then_inc(taken[3], 1)
                        act.wait_ge(taken[3], 1 + t0 + 1 + p)
                        act.dma_start(sa_dram[p, :, :], gt[:, :]).then_inc(sa_kept, 16)

            def attention_pair(p, first):
                b0, t0 = FIRST["att"], USES["att"]
                for s in range(4):
                    split(b0, 4, p, s + 1)
                    if s == 0 and first:
                        finish_decays(PAIRS - 1)
                    act.wait_ge(block_done, 1 + b0 + s + 1 + 4 * p)
                    settle(act)
                    if s == 0:
                        nc.scalar.activation(qa[:, p, :], bank[0][:, :], ACT.Copy, scale=HD ** -0.5).then_inc(taken[0], 1)
                    elif s == 1:
                        nc.scalar.copy(ka[:, p, :], bank[1][:, :]).then_inc(taken[1], 1)
                    elif s == 2:
                        if first:
                            act.wait_ge(shifted, 1 + 3 * PAIRS)
                        nc.scalar.copy(vf[:, :], bank[2][:, :]).then_inc(taken[2], 1)
                        if first:
                            keep_pair(PAIRS - 1)
                    else:
                        if first:
                            act.wait_ge(sa_kept, 1 + 16 * PAIRS)
                        act.wait_ge(sb_kept, 1 + 16 * p)
                        nc.scalar.activation(gt[:, :], bank[3][:, :], ACT.Sigmoid).then_inc(taken[3], 1)
                        act.wait_ge(taken[3], 1 + t0 + 1 + p)
                        act.dma_start(sb_dram[p, :, :], gt[:, :]).then_inc(sb_kept, 16)
                        if first:
                            act.wait_ge(kr_kept, 1 + 16 * PAIRS)
                            act.wait_ge(v_kept, 1 + 16 * PAIRS)
                        act.wait_ge(vt_done, p + 1)
                        settle(act)
                        nc.scalar.copy(va[:, p, :], bank[7][:, :]).then_inc(va_ready, 1)

            rwkv_pair(0, None)
            with act.Fori(0, PAIRS - 1) as i:
                rwkv_pair(i + 1, i)
            attention_pair(0, True)
            attention_pair(1, False)
            act.wait_ge(l_kept, 1 + 32 * PAIRS)
            act.dma_start(ls[:, :, :], l_dram.rearrange("n h c t s -> (n h c) t s")).then_inc(ls_loaded, 16)
            with act.Fori(2, PAIRS) as i:
                attention_pair(i, False)
            act.wait_ge(solved, 2)
            act.dma_start(pd_dram.rearrange("n h c s t -> (n h c) s t"), tt[:, :, :]).then_inc(p_kept, 16)
            act.dma_start(t11_dram.rearrange("n h c a b -> (n h c) a b"), t11[:, :, :]).then_inc(p_kept, 16)
            act.wait_ge(p_kept, 32)

            with act.Fori(0, NCH) as c:
                for g in range(2):
                    it = 2 * c + g
                    o = HD * g
                    act.wait_ge(c_g, it + 1)
                    nc.scalar.copy(m_g[:, :, :], bank[3][:, :].rearrange("p (n s) -> p n s", n=4)).then_inc(c_gs, 1)
                    act.wait_ge(c_tr, 3 * it + 1)
                    nc.scalar.copy(vt[:, :, :], bank[0][:, :].rearrange("p (n s) -> p n s", n=4)).then_inc(c_av, 1)
                    act.wait_ge(negmax, it + 1)
                    for q in range(NQ):
                        w = P * (q + 1)
                        nc.scalar.activation(prob[:, q, 0:w], prob[:, q, 0:w], ACT.Exp, bias=rmax[:, 4 + q:5 + q],
                                             accum_out=rmax[:, 8 + q:9 + q]).then_inc(exped, 1)
                    act.wait_ge(c_tr, 3 * it + 3)
                    nc.scalar.copy(kt[:, :, :], bank[2][:, :].rearrange("p (n s) -> p n s", n=4)).then_inc(c_av, 1)
                    act.wait_ge(c_x, it + 1)
                    nc.scalar.copy(m_x[:, :, :], bank[2][:, :].rearrange("p (n s) -> p n s", n=4)).then_inc(c_xs, 1)
                    act.wait_ge(pv_done, 1 + it)
                    for n in range(3):
                        act.wait_ge(ptr, 1 + 3 * it + n + 1)
                        if n < 2:
                            nc.scalar.copy(probt[:, n, P * n:T], bank[4 + n][:, 0:P * (4 - n)]).then_inc(pt_taken, 1)
                        else:
                            nc.scalar.copy(probt[:, 2, 2 * P:T], bank[6][:, 0:2 * P]).then_inc(pt_taken, 1)
                            nc.scalar.copy(probt[:, 3, 3 * P:T], bank[6][:, 2 * P:3 * P]).then_inc(pt_taken, 1)
                    act.wait_ge(pv_done, 1 + it + 1)
                    settle(act)
                    nc.scalar.copy(yhi[o:o + HD, c, :], bank[7][o:o + HD, :]).then_inc(y_hi, 1)
                    act.wait_ge(c_y, it + 1)
                    settle(act)
                    for h in range(2):
                        nc.scalar.copy(yo[HD * h:HD * h + HD, 4 * g:4 * g + 4, bass.ds(CH * c, CH)],
                                       bank[0][HD * h:HD * h + HD, :].rearrange("p (n s) -> p n s", n=4)
                                       [:, :, HD * h:HD * h + HD]).then_inc(c_ys, 1)

            act.wait_ge(v_copied, PAIRS)
            act.wait_ge(y_lo, 1 + HEADS)
            act.wait_ge(sb_kept, 1 + 16 * PAIRS)
            act.dma_start(sgb[:, :, :], sb_dram.rearrange("k p t -> p k t")).then_inc(sgb_loaded, 16)
            act.dma_start(glora[:, :], glora_in).then_inc(g_loaded, 16)
            act.wait_ge(c_ss, 1 + 2 * NCH)
            for p in range(2):
                act.dma_start(krv[:, p, :, :], rw_dram[p, 2:5, :, :].rearrange("j p t -> p j t"))\
                    .then_inc(krv_loaded[p], 16)
            act.dma_start(sga[:, :, :], sa_dram.rearrange("k p t -> p k t")).then_inc(sga_loaded, 16)
            b0 = FIRST["ob"]
            for p in range(PAIRS):
                split(b0, 0, 0, p + 1)
                act.wait_ge(p_diff, p + 1)
                nc.scalar.activation(g_q[:, :], g_d[:, :], ACT.Square).then_inc(p_sq, 1)
                act.wait_ge(p_ss, p + 1)
                nc.scalar.activation(g_r[:, :], bank[5][:, :], ACT.Sqrt, scale=1.0 / HD,
                                     bias=cst[:, C_EPS + 1:C_EPS + 2]).then_inc(p_sd, 1)
                act.wait_ge(p_y, p + 1)
                nc.scalar.copy(hhi[:, p, :], g_c[:, :]).then_inc(h_hi, 1)
                if p + 2 < PAIRS:
                    act.dma_start(krv[:, p % 2, :, :], rw_dram[p + 2, 2:5, :, :].rearrange("j p t -> p j t"))\
                        .then_inc(krv_loaded[p % 2], 16)

            b0 = FIRST["oa"]
            with act.Fori(0, 2) as i:
                for u in range(4):
                    split(b0, 4, i, u + 1)
                    act.wait_ge(merged, u + 1 + 4 * i)
                    settle(act)
                    nc.scalar.copy(yhi[:, 4 * i + u, :], mtmp[:, u % 2, :]).then_inc(y_hi, 1)
            b0 = FIRST["out"]
            with act.Fori(0, 2) as i:
                for u in range(4):
                    split(b0, 4, i, u + 1)
            norm(2, 2 * KD - KD)
            feed("f2", NF)
            down("d2", True)
            norm(3, 2 * KD)

        @block.vector
        def _(dve):
            step = Tally(dve_step)

            def chain(ins):
                dve.wait_ge(dve_step, step.mark(ins))

            def norm(which, name, h0):
                ssum, rstd = ssums[which], rstds[which]
                for k in range(1, KD):
                    dve.wait_ge(n_sq, which * KD + k + 1)
                    src = sq[:, 0, :] if k == 1 else ssum[:, :]
                    if k < KD - 1:
                        chain(nc.vector.tensor_tensor(ssum[:, :], src, sq[:, k, :], ALU.add))
                    else:
                        nc.vector.tensor_tensor(rstd[:, :], src, sq[:, k, :], ALU.add).then_inc(n_sum, 1)
                dve.wait_ge(n_sd, which + 1)
                chain(nc.vector.reciprocal(rstd[:, :], rstd[:, :]))
                for k in range(KD):
                    dst = outt[:, k, :] if which == 3 else hn[:, k, :]
                    nc.vector.scalar_tensor_tensor(out=dst, in0=x[:, k, :], scalar=gain(name, k), in1=rstd[:, :],
                                                   op0=ALU.mult, op1=ALU.mult)\
                        .then_inc(out_ready if which == 3 else n_hn, 1)
                if which == 3:
                    return
                for k in range(KD):
                    dve.wait_ge(h_hi, h0 + k + 1)
                    nc.vector.tensor_tensor(hlo[:, k, :], hn[:, k, :], hhi[:, k, :].bitcast(F32), ALU.subtract)\
                        .then_inc(h_lo, 1)

            def feed(name, j0):
                b0 = FIRST[name]
                with dve.Fori(0, NF // 2) as i:
                    for jj in range(2):
                        dve.wait_ge(silu_ready, j0 + jj + 1 + 2 * i)
                        dve.wait_ge(block_done, 1 + b0 + 2 * jj + 2 + 4 * i)
                        dve.wait_ge(act_lo, 1 + j0 + jj + 2 * i)
                        nc.vector.tensor_tensor(prod[:, :], silu_g[:, :], bank[2 * jj + 1][:, :], ALU.mult)\
                            .then_inc(prod_ready, 1)
                        dve.wait_ge(act_hi, j0 + jj + 1 + 2 * i)
                        nc.vector.tensor_tensor(alo[:, 2 * i + jj, :], prod[:, :],
                                                ahi[:, 2 * i + jj, :].bitcast(F32), ALU.subtract).then_inc(act_lo, 1)

            def down(name):
                b0 = FIRST[name]
                with dve.Fori(0, 2) as i:
                    for m in range(4):
                        dve.wait_ge(block_done, 1 + b0 + 3 * m + 3 + 12 * i)
                        xm = x[:, 4 * i + m, :]
                        nc.vector.scalar_tensor_tensor(out=xm, in0=bank[m][:, :], scalar=0.5, in1=xm,
                                                       op0=ALU.mult, op1=ALU.add).then_inc(x_done, 1)
                        dve.wait_ge(x_done, X0[name] + m + 1 + 4 * i)
                        dve.sem_inc(taken[m], 1)

            X0 = {"d1": 0, "d2": 2 * KD}
            begin_at_one(dve, *taken, act_lo, y_lo, shifted, c_us, c_mat, c_ss)
            dve.sem_inc(prod_ready, 2)
            dve.wait_ge(params, 32)
            norm(0, "ffn1_norm", 0)
            feed("f1", 0)
            down("d1")
            norm(1, "mix_norm", KD)

            nc.vector.memset(sh[:, :, 0:1], 0.0).then_inc(zeroed, 1)
            chain(nc.vector.memset(shl[:, :, 0:1], 0.0))
            for s in range(2):
                dve.wait_ge(taken[2 + s], 1 + USES["idx"] + 2)
                chain(nc.vector.tensor_tensor(shd[:, s, :], shl[:, s, 0:T], shl[:, s, 1:T + 1], ALU.subtract))
                nc.vector.scalar_tensor_tensor(out=shd[:, s, :], in0=shd[:, s, :], scalar=gain("time_mix", 24 + s),
                                               in1=shl[:, s, 1:T + 1], op0=ALU.mult, op1=ALU.add).then_inc(lx_raw, 1)
            dve.wait_ge(iwt_done, 1)
            nc.vector.tensor_copy(iw[:, :, :], bank[4][:, :].rearrange("p (n s) -> p n s", n=4)).then_inc(iw_ready, 1)
            dve.wait_ge(iw_ready, 1)
            for n in range(3 * IDX_HEADS):
                q, hd = n // IDX_HEADS + 1, n % IDX_HEADS
                w = P * (q + 1)
                sc = score[:, q - 1, 0:w]
                dve.wait_ge(relu_ready, n + 1)
                if hd == 0:
                    ins = nc.vector.tensor_scalar(sc, relu[:, n % 2, 0:w], iw[:, q, hd:hd + 1], None, ALU.mult)
                else:
                    dve.wait_ge(sc_used, n)
                    ins = nc.vector.scalar_tensor_tensor(out=sc, in0=relu[:, n % 2, 0:w], scalar=iw[:, q, hd:hd + 1],
                                                         in1=sc, op0=ALU.mult, op1=ALU.add)
                ins.then_inc(sc_used, 1)
            dve.wait_ge(sc_used, 3 * IDX_HEADS)
            dve.wait_ge(lora_mm, 2 * KD)
            chain(nc.vector.memset(a_l[:, :, :], 0.0))
            chain(nc.vector.memset(b_l[:, :, :], 0.0))
            dve.wait_ge(lora_ready, 2 * KD)

            def chunks(buf):
                return [buf[HD * h:HD * h + HD, :].rearrange("p (c t) -> p c t", c=NCH) for h in (0, 1)]

            def shift_pair(p):
                t0 = USES["rw"]
                for n, (s, dst) in enumerate(((1, t_k), (0, t_r), (2, t_v))):
                    dve.wait_ge(taken[s], 1 + t0 + 1 + p)
                    if s == 2:
                        dve.wait_ge(v_kept, 1 + 16 * p)
                    chain(nc.vector.tensor_tensor(t_d[:, :], sh[:, s, 0:T], sh[:, s, 1:T + 1], ALU.subtract))
                    mix = PAR["time_mix"] + 8 * s
                    nc.vector.scalar_tensor_tensor(out=dst[:, :], in0=t_d[:, :], scalar=par[:, bass.ds(mix + p, 1)],
                                                   in1=sh[:, s, 1:T + 1], op0=ALU.mult, op1=ALU.add)\
                        .then_inc(shifted, 1)
                    dve.wait_ge(shifted, 1 + 3 * p + n + 1)
                    if s == 1:
                        nc.vector.tensor_scalar(t_kk[:, :], t_k[:, :], par[:, bass.ds(PAR["k_k"] + p, 1)], None,
                                                ALU.mult).then_inc(kq_ready, 1)
                chain(nc.vector.tensor_tensor_scan(t_s[:, :], resets, zs[:, p, :], 0.0, ALU.mult, ALU.add))
                nc.vector.tensor_tensor(t_sm[:, :], t_s[:, :], zs[:, p, :], ALU.subtract).then_inc(scanned, 1)

            def prepare_pair(p):
                chain(nc.vector.tensor_scalar(t_d[:, :], az[:, p, :], -1.0, par[:, bass.ds(PAR["k_a"] + p, 1)],
                                              ALU.add, ALU.mult))
                chain(nc.vector.scalar_tensor_tensor(out=t_d[:, :], in0=t_d[:, :], scalar=1.0, in1=t_k[:, :],
                                                     op0=ALU.add, op1=ALU.mult))
                dve.wait_ge(kk_norm, p + 1)
                chain(nc.vector.tensor_scalar(t_sq[:, :], t_sq[:, :], 1e-12, None, ALU.max))
                chain(nc.vector.reciprocal(t_sq[:, :], t_sq[:, :]))
                chain(nc.vector.tensor_tensor(t_kk[:, :], t_kk[:, :], t_sq[:, :], ALU.mult))
                chain(nc.vector.tensor_tensor(t_sq[:, :], t_kk[:, :], az[:, p, :], ALU.mult))
                dve.wait_ge(decays, 3 * p + 3)
                dve.wait_ge(ab_kept, 1 + 64 * p)
                dve.wait_ge(kr_kept, 1 + 16 * p)
                for d, k_, s_, b_, e_ in zip(halves(a_l), chunks(t_kk), chunks(t_sm), chunks(t_sq), chunks(t_e)):
                    nc.vector.scalar_tensor_tensor(out=d, in0=k_, scalar=-1.0, in1=s_, op0=ALU.mult, op1=ALU.mult)
                for d, b_, e_ in zip(halves(b_l), chunks(t_sq), chunks(t_e)):
                    nc.vector.tensor_tensor(d, b_, e_, ALU.mult)
                nc.vector.tensor_tensor(kr[:, 0, :], t_d[:, :], t_e[:, :], ALU.mult)
                chain(nc.vector.tensor_copy(wend[:, p, :], t_s[:, CH - 1:T:CH]))
                chain(nc.vector.tensor_tensor(kr[:, 1, :], t_r[:, :], t_s[:, :], ALU.mult))
                dve.sem_inc(prepped, 1)

            shift_pair(0)
            with dve.Fori(0, PAIRS - 1) as i:
                step.enter(i, 8 + 4)
                prepare_pair(i)
                shift_pair(i + 1)
            step.leave(PAIRS - 1)
            prepare_pair(PAIRS - 1)

            for q in range(1, NQ):
                w = P * (q + 1)
                chain(nc.vector.memset(score[0:CH, q - 1, w - CH:w], NEG))
                chain(nc.vector.tensor_copy(work[:, q - 1, 0:w], score[:, q - 1, 0:w]))
                for _ in range(TOPK // 8):
                    chain(nc.vector.max(top8[:, :], work[:, q - 1, 0:w]))
                    chain(nc.vector.match_replace(work[:, q - 1, 0:w], top8[:, :], work[:, q - 1, 0:w], NEG))
                chain(nc.vector.tensor_tensor(bias[:, q, 0:w], score[:, q - 1, 0:w], work[:, q - 1, 0:w],
                                              ALU.not_equal))
                chain(nc.vector.tensor_scalar(bias[:, q, 0:w], bias[:, q, 0:w], -1.0, MASKED, ALU.add, ALU.mult))
            chain(nc.vector.tensor_scalar(bias[:, 0, 0:P], visible, -1.0, MASKED, ALU.add, ALU.mult))

            def blocks(buf, a, b, step_a, step_b, n_a, n_b):
                return bass.AP(buf, buf[:, a, b:b + 1].offset,
                               [list(buf[:, 0, 0:1].ap[0]), [HALF * CH + HALF, 2], [step_a, n_a], [step_b, n_b]])

            dve.wait_ge(l_mm, 2 * PAIRS)
            dve.wait_ge(ab_kept, 1 + 64 * PAIRS)
            dve.wait_ge(ls_loaded, 16)
            chain(nc.vector.memset(tt[:, :, :], 0.0))
            chain(nc.vector.memset(tt[:, :, :].rearrange("p a b -> p (a b)")[:, 0::CH + 1], 1.0))
            for t in range(1, HALF):
                chain(nc.vector.tensor_tensor(tprod[:, :, 0:t, 0:t], blocks(ls, t, 0, 0, 1, t, t),
                                              blocks(tt, 0, 0, CH, 1, t, t), ALU.mult))
                chain(nc.vector.tensor_reduce(blocks(tt, 0, t, CH, 1, t, 1), tprod[:, :, 0:t, 0:t], AX.X, ALU.add))
            nc.vector.tensor_copy(t11[:, :, :], tt[:, 0:HALF, 0:HALF].rearrange("p a b -> p b a")).then_inc(solved, 2)

            nc.vector.memset(state[0][:, :, :], 0.0)
            chain(nc.vector.memset(state[1][:, :, :], 0.0))
            dve.wait_ge(block_done, 1 + FIRST["ob"])
            for buf in (abkrv[0][:, :, :, :], pd[0][:, :, :], l21[0][:, :, :]):
                nc.vector.memset(buf, 0.0)
            chain(nc.vector.memset(t11b[0][:, :, :], 0.0))
            dve.sem_inc(c_cleared[0], 1)
            dve.wait_ge(p_kept, 32)

            def four(b):
                return bank[b][:, :].rearrange("p (n s) -> p n s", n=4)

            def masked(dst, b, mask):
                nc.vector.tensor_tensor(dst[:, :, :], four(b), mask.unsqueeze(1).to_broadcast([P, 4, P]),
                                        ALU.mult).then_inc(c_us, 1)

            with dve.Fori(0, NCH) as c:
                step.enter(c, 2 * 6)
                for g in range(2):
                    it = 2 * c + g
                    g4 = 4 * g
                    o = HD * g
                    dve.wait_ge(ptr, 1 + 3 * it)
                    for q in range(NQ):
                        w = P * (q + 1)
                        if q != 1:
                            dve.wait_ge(logit, 3 * it + max(q, 1))
                        c0 = P if q == 1 else 0
                        settle(dve)
                        chain(nc.vector.tensor_tensor_reduce(
                            out=prob[:, q, 0:w], in0=bank[(4, 4, 5, 6)[q]][:, c0:c0 + w], in1=bias[:, q, 0:w],
                            scale=1.0, scalar=NEG, op0=ALU.add, op1=ALU.max, accum_out=rmax[:, q:q + 1]))
                    nc.vector.tensor_scalar(rmax[:, 4:8], rmax[:, 0:4], -1.0, None, ALU.mult).then_inc(negmax, 1)
                    dve.wait_ge(c_tr, 3 * it + 2)
                    nc.vector.tensor_copy(bt[:, :, :], four(1)).then_inc(c_us, 1)
                    dve.wait_ge(c_gram, 3 * it + 1)
                    masked(m_rb, 7, incl)
                    dve.wait_ge(exped, 4 * it + 4)
                    chain(nc.vector.reciprocal(rmax[:, 12:16], rmax[:, 8:12]))
                    for q in range(NQ):
                        w = P * (q + 1)
                        nc.vector.tensor_scalar(prob[:, q, 0:w], prob[:, q, 0:w], rmax[:, 12 + q:13 + q], None,
                                                ALU.mult).then_inc(prob_ready, 1)
                    dve.wait_ge(c_gram, 3 * it + 2)
                    masked(m_ak, 0, strict)
                    dve.wait_ge(c_gram, 3 * it + 3)
                    masked(m_rk, 1, incl)
                    dve.wait_ge(c_ag, it + 1)
                    nc.vector.tensor_tensor(m_p[:, :, :], pd[g][:, :, :], four(3), ALU.add).then_inc(c_mat, 1)
                    dve.wait_ge(c_u, it + 1)
                    nc.vector.tensor_copy(m_u[:, :, :], four(3)).then_inc(c_us, 1)
                    dve.wait_ge(y_hi, it + 1)
                    nc.vector.tensor_tensor(ylo[o:o + HD, c, :], bank[7][o:o + HD, :],
                                            yhi[o:o + HD, c, :].bitcast(F32), ALU.subtract).then_inc(y_lo, 1)
                    dve.wait_ge(c_s, 1 + it + 1)
                    chain(nc.vector.tensor_tensor(state[g][:, :, :], state[g][:, :, :], four(1), ALU.add))
                    nc.vector.tensor_tensor(state[g][:, :, :], state[g][:, :, :],
                                            wend[:, g4:g4 + 4, bass.ds(c, 1)].to_broadcast([P, 4, P]), ALU.mult)\
                        .then_inc(c_ss, 1)
            step.leave(NCH)

            for p in range(PAIRS):
                nc.vector.tensor_scalar(rkw[:, p, :], headsum, gain("r_k", p), None, ALU.mult).then_inc(rkw_ready, 1)
            b0 = FIRST["ob"]
            for p in range(PAIRS):
                k_, r_, v_ = [krv[:, p % 2, j, :] for j in range(3)]
                dve.wait_ge(p_mean, p + 1)
                if p == 0:
                    dve.wait_ge(c_ys, 1 + 4 * NCH)
                nc.vector.scalar_tensor_tensor(out=g_d[:, :], in0=bank[4][:, :], scalar=-1.0 / HD, in1=yo[:, p, :],
                                               op0=ALU.mult, op1=ALU.add).then_inc(p_diff, 1)
                dve.wait_ge(krv_loaded[p % 2], 16 * (p // 2 + 1))
                nc.vector.tensor_tensor(g_b[:, :], r_, k_, ALU.mult).then_inc(p_rk, 1)
                dve.wait_ge(block_done, 1 + b0 + p + 1)
                dve.wait_ge(sgb_loaded, 16)
                nc.vector.tensor_tensor(sgb[:, p, :], sgb[:, p, :], bank[p % 4][:, :], ALU.mult)\
                    .then_inc(taken[p % 4], 1)
                dve.wait_ge(p_sd, p + 1)
                chain(nc.vector.reciprocal(g_r[:, :], g_r[:, :]))
                chain(nc.vector.tensor_tensor(g_d[:, :], g_d[:, :], g_r[:, :], ALU.mult))
                chain(nc.vector.tensor_scalar(g_d[:, :], g_d[:, :], gain("gn_weight", p), gain("gn_bias", p),
                                              ALU.mult, ALU.add))
                dve.wait_ge(p_bonus, p + 1)
                chain(nc.vector.tensor_tensor(g_b[:, :], v_, bank[6][:, :], ALU.mult))
                chain(nc.vector.tensor_tensor(g_d[:, :], g_d[:, :], g_b[:, :], ALU.add))
                dve.wait_ge(p_gate, p + 1)
                nc.vector.tensor_tensor(g_c[:, :], g_d[:, :], bank[7][:, :], ALU.mult).then_inc(p_y, 1)
                dve.wait_ge(h_hi, 2 * KD + p + 1)
                nc.vector.tensor_tensor(hlo[:, p, :], g_c[:, :], hhi[:, p, :].bitcast(F32), ALU.subtract)\
                    .then_inc(h_lo, 1)

            b0 = FIRST["oa"]
            dve.wait_ge(sga_loaded, 16)
            per = 4
            with dve.Fori(0, 2) as i:
                step.enter(i, per)
                for u in range(4):
                    m = 4 * i + u
                    dve.wait_ge(block_done, 1 + b0 + u + 1 + 4 * i)
                    nc.vector.tensor_tensor(mtmp[:, u % 2, :], sga[:, m, :], bank[u][:, :], ALU.mult)\
                        .then_inc(taken[u], 1)
                    dve.wait_ge(taken[u], 1 + USES["oa"] + 1 + i)
                    nc.vector.tensor_tensor(mtmp[:, u % 2, :], mtmp[:, u % 2, :], sgb[:, m, :], ALU.add)\
                        .then_inc(merged, 1)
                    dve.wait_ge(y_hi, HEADS + u + 1 + 4 * i)
                    chain(nc.vector.tensor_tensor(ylo[:, m, :], mtmp[:, u % 2, :], yhi[:, m, :].bitcast(F32),
                                                  ALU.subtract))
            step.leave(2)
            dve.sem_inc(y_lo, KD)
            b0 = FIRST["out"]
            with dve.Fori(0, 2) as i:
                for u in range(4):
                    xm = x[:, 4 * i + u, :]
                    dve.wait_ge(block_done, 1 + b0 + u + 1 + 4 * i)
                    nc.vector.tensor_tensor(xm, xm, bank[u][:, :], ALU.add).then_inc(x_done, 1)
                    dve.wait_ge(x_done, KD + u + 1 + 4 * i)
                    dve.sem_inc(taken[u], 1)
            norm(2, "ffn2_norm", 3 * KD)
            feed("f2", NF)
            down("d2")
            norm(3, "final_norm", 0)

        @block.tensor
        def _(pe):
            def products(u, acc, hi, lo, tiles, first, last):
                n = len(tiles)
                for t, k in enumerate(tiles):
                    a, b = whi[:, u % 2, t, :], wlo[:, u % 2, t, :]
                    nc.tensor.matmul(acc, a, hi[:, k, :], start=first and t == 0, stop=False)
                    nc.tensor.matmul(acc, a, lo[:, k, :], start=False, stop=False)
                    ins = nc.tensor.matmul(acc, b, hi[:, k, :], start=False, stop=last and t == n - 1)
                ins.then_inc(block_done, 1)

            def project(first, per, i, u, hi, lo):
                pe.wait_ge(lo_ready, first + u + 1 + per * i)
                products(u, bank[u % 4][:, :], hi, lo, range(8), True, True)

            def norm(which, h0):
                pe.wait_ge(n_sum, which + 1)
                nc.tensor.matmul(bank[4][:, :], ones, rstds[which][:, :], start=True, stop=True).then_inc(n_mean, 1)
                if which < 3:
                    pe.wait_ge(h_lo, h0 + KD)

            def feed(name, j0):
                b0 = FIRST[name]
                with pe.Fori(0, NF // 2) as i:
                    for u in range(4):
                        if u % 2 == 0:
                            pe.wait_ge(prod_ready, 2 + j0 + u // 2 - 1 + 2 * i)
                        project(b0, 4, i, u, hhi, hlo)

            def down(name, a0):
                b0, t0 = FIRST[name], USES[name]
                pe.wait_ge(act_lo, 1 + a0)
                with pe.Fori(0, 2) as i:
                    for m in range(4):
                        pe.wait_ge(taken[m], 1 + t0 + i)
                        for k in range(3):
                            u = 3 * m + k
                            pe.wait_ge(lo_ready, b0 + u + 1 + 12 * i)
                            products(u, bank[m][:, :], ahi, alo, range(8 * k, min(8 * k + 8, NF)), k == 0, k == 2)

            begin_at_one(pe, block_done, ptr, pv_done, c_s)
            pe.wait_ge(params, 32)
            norm(0, 0)
            feed("f1", 0)
            down("d1", NF)
            norm(1, KD)

            b0, t0 = FIRST["idx"], USES["idx"]
            for u in range(8):
                pe.wait_ge(taken[u % 4], 1 + t0 + u // 4)
                project(b0, 0, 0, u, hhi, hlo)
            pe.wait_ge(taken[1], 1 + t0 + 2)
            for q in range(NQ):
                ins = nc.tensor.transpose(bank[4][:, P * q:P * q + P], iwt[:, P * q:P * q + P], ident)
            ins.then_inc(iwt_done, 1)
            pe.wait_ge(taken[0], 1 + t0 + 2)
            pe.wait_ge(taken[3], 1 + t0 + 1)
            for n in range(3 * IDX_HEADS):
                q, hd = n // IDX_HEADS + 1, n % IDX_HEADS
                o = HD * (hd % 2)
                if n == 0:
                    pe.wait_ge(iw_ready, 1)
                if n >= 4:
                    pe.wait_ge(relu_ready, n - 3)
                nc.tensor.matmul(bank[4 + n % 4][:, 0:P * (q + 1)], iq[o:o + HD, hd // 2, P * q:P * q + P],
                                 ik[o:o + HD, 0:P * (q + 1)], start=True, stop=True).then_inc(sc_done, 1)

            pe.wait_ge(relu_ready, 3 * IDX_HEADS)
            pe.wait_ge(lx_ready, 3)
            pe.wait_ge(lora_loaded, 16)
            for n in range(2 * KD):
                if n >= 4:
                    pe.wait_ge(lora_ready, n - 3)
                m = n // 2
                nc.tensor.matmul(bank[4 + n % 4][:, :], lora[:, n % 2, P * m:P * m + P], lx[:, :],
                                 start=True, stop=True).then_inc(lora_mm, 1)
            pe.wait_ge(lora_ready, 2 * KD)

            def chunk_products(p):
                pe.wait_ge(prepped, p + 1)
                pe.wait_ge(l_out, 1 + 2 * p)
                for n in range(2):
                    for j in range(4):
                        ins = nc.tensor.matmul(bank[5 + n][:, P * j:P * j + P], a_l[:, 4 * n + j, :],
                                               b_l[:, 4 * n + j, :], start=True, stop=True)
                    ins.then_inc(l_mm, 1)

            def quad(name, p, p_before):
                b0, t0 = FIRST[name], USES[name]
                for u in range(4):
                    pe.wait_ge(taken[u], 1 + t0 + p)
                    project(b0, 4, p, u, hhi, hlo)
                    if u == 2 and p_before is not None:
                        chunk_products(p_before)

            def rwkv_pair(p, p_before):
                quad("rw", p, p_before)
                pe.wait_ge(kq_sq, p + 1)
                nc.tensor.matmul(bank[4][:, :], headsum, t_sq[:, :], start=True, stop=True).then_inc(kk_ss, 1)

            def attention_pair(p, p_before):
                quad("att", p, p_before)
                pe.wait_ge(taken[2], 1 + USES["att"] + 1 + p)
                if p_before is None:
                    pe.wait_ge(va_ready, p)
                for q in range(NQ):
                    ins = nc.tensor.transpose(bank[7][:, P * q:P * q + P], vf[:, P * q:P * q + P], ident)
                ins.then_inc(vt_done, 1)

            rwkv_pair(0, None)
            with pe.Fori(0, PAIRS - 1) as i:
                rwkv_pair(i + 1, i)
            attention_pair(0, PAIRS - 1)
            with pe.Fori(1, PAIRS) as i:
                attention_pair(i, None)

            def group(b, *terms):
                for n in range(4):
                    for k, (lhs, rhs) in enumerate(terms):
                        ins = nc.tensor.matmul(bank[b][:, P * n:P * n + P], lhs[:, n, :], rhs[:, n, :],
                                               start=k == 0, stop=k == len(terms) - 1)
                return ins

            def turned(b, src):
                for n in range(4):
                    ins = nc.tensor.transpose(bank[b][:, P * n:P * n + P], src[:, n, :], ident)
                return ins

            pe.wait_ge(va_ready, PAIRS)
            pe.wait_ge(l_out, 1 + 2 * PAIRS)
            for m in range(4):
                pe.wait_ge(taken[m], 1 + USES["ob"])
            with pe.Fori(0, NCH) as c:
                for g in range(2):
                    it = 2 * c + g
                    o = HD * g
                    pe.wait_ge(qk_copied, 2 * c + 2)
                    pe.wait_ge(pt_taken, 1 + 4 * it)
                    for q in range(NQ):
                        w = P * (q + 1)
                        c0 = P if q == 1 else 0
                        ins = nc.tensor.matmul(bank[(4, 4, 5, 6)[q]][:, c0:c0 + w], qs[o:o + HD, P * q:P * q + P],
                                               ks[o:o + HD, 0:w], start=True, stop=True)
                        if q != 0:
                            ins.then_inc(logit, 1)
                    pe.wait_ge(c_loaded[g], 128 * c + 128)
                    pe.wait_ge(c_us, 1 + 5 * it)
                    group(3, (l21[g], pd[g])).then_inc(c_g, 1)
                    pe.wait_ge(c_ys, 1 + 2 * it)
                    turned(0, v_bd[g]).then_inc(c_tr, 1)
                    pe.wait_ge(c_ss, 1 + it)
                    turned(1, b_bd[g]).then_inc(c_tr, 1)
                    turned(2, k_bd[g]).then_inc(c_tr, 1)
                    pe.wait_ge(y_lo, 1 + it)
                    group(7, (b_bd[g], r_bd[g])).then_inc(c_gram, 1)
                    pe.wait_ge(c_gs, it + 1)
                    group(3, (t11b[g], m_g)).then_inc(c_ag, 1)
                    pe.wait_ge(c_av, 1 + 2 * it + 1)
                    group(0, (k_bd[g], a_bd[g])).then_inc(c_gram, 1)
                    pe.wait_ge(c_us, 1 + 5 * it + 1)
                    group(1, (k_bd[g], r_bd[g])).then_inc(c_gram, 1)
                    pe.wait_ge(c_av, 1 + 2 * it + 2)
                    pe.wait_ge(c_us, 1 + 5 * it + 3)
                    group(2, (a_bd[g], state[g]), (m_ak, vt)).then_inc(c_x, 1)
                    pe.wait_ge(prob_ready, 4 * it + 4)
                    for kt_, (lo_q, bk, c0) in enumerate([(0, 4, 0), (1, 5, 0), (2, 6, 0), (3, 6, 2 * P)]):
                        for q in range(lo_q, NQ):
                            ins = nc.tensor.transpose(bank[bk][:, c0 + P * (q - lo_q):c0 + P * (q - lo_q) + P],
                                                      prob[:, q, P * kt_:P * kt_ + P], ident)
                        if kt_ != 2:
                            ins.then_inc(ptr, 1)
                    pe.wait_ge(c_mat, 1 + it + 1)
                    pe.wait_ge(c_xs, it + 1)
                    group(3, (m_p, m_x)).then_inc(c_u, 1)
                    pe.wait_ge(v_copied, c + 1)
                    pe.wait_ge(pt_taken, 1 + 4 * it + 4)
                    for kt_ in range(NQ):
                        ins = nc.tensor.matmul(bank[7][o:o + HD, P * kt_:T], vs[:, P * kt_ + o:P * kt_ + o + HD],
                                               probt[:, kt_, P * kt_:T], start=(kt_ == 0), stop=(kt_ == NQ - 1))
                    ins.then_inc(pv_done, 1)
                    pe.wait_ge(c_us, 1 + 5 * it + 5)
                    group(0, (state[g], r_bd[g]), (m_u, m_rb), (vt, m_rk)).then_inc(c_y, 1)
                    group(1, (bt, m_u), (kt, vt)).then_inc(c_s, 1)

            b0, t0 = FIRST["ob"], USES["ob"]
            pe.wait_ge(c_ys, 1 + 4 * NCH)
            pe.wait_ge(c_ss, 1 + 2 * NCH)
            pe.wait_ge(y_lo, 1 + HEADS)
            for p in range(PAIRS):
                nc.tensor.matmul(bank[4][:, :], headsum, yo[:, p, :], start=True, stop=True).then_inc(p_mean, 1)
                pe.wait_ge(taken[p % 4], 1 + t0 + p // 4)
                project(b0, 0, 0, p, yhi, ylo)
                if p == 0:
                    pe.wait_ge(rkw_ready, PAIRS)
                    pe.wait_ge(g_loaded, 16)
                else:
                    pe.wait_ge(p_y, p)
                pe.wait_ge(p_sq, p + 1)
                nc.tensor.matmul(bank[5][:, :], headsum, g_q[:, :], start=True, stop=True).then_inc(p_ss, 1)
                pe.wait_ge(p_rk, p + 1)
                nc.tensor.matmul(bank[6][:, :], rkw[:, p, :], g_b[:, :], start=True, stop=True).then_inc(p_bonus, 1)
                nc.tensor.matmul(bank[7][:, :], glora[:, P * p:P * p + P], xg[:, :], start=True, stop=True)\
                    .then_inc(p_gate, 1)

            b0, t0 = FIRST["oa"], USES["oa"]
            pe.wait_ge(h_lo, 3 * KD)
            with pe.Fori(0, 2) as i:
                for u in range(4):
                    pe.wait_ge(taken[u], 1 + t0 + i)
                    project(b0, 4, i, u, hhi, hlo)
            b0, t0 = FIRST["out"], USES["out"]
            pe.wait_ge(y_lo, 1 + HEADS + KD)
            with pe.Fori(0, 2) as i:
                for u in range(4):
                    pe.wait_ge(taken[u], 1 + t0 + i)
                    project(b0, 4, i, u, yhi, ylo)
            norm(2, 3 * KD)
            feed("f2", NF)
            down("d2", 2 * NF)
            norm(3, 0)


def _tiles(w):
    k, n = w.shape
    return w.reshape(k // P, P, n // P, P).transpose(2, 1, 0, 3)


def _down(w):
    t = _tiles(w)
    pad = np.zeros((t.shape[0], P, 24 - NF, P), w.dtype)
    return np.concatenate([t, pad], 2).reshape(KD, P, 3, 8, P).transpose(0, 2, 1, 3, 4).reshape(DBLK, P, 8, P)


def _stream(inp):
    w_in = inp["w_in"][0]
    c = np.cumsum([0, D, D, D, 128, 128, D, D, D, 512, 64, 8, D, D])
    r, k, v, xwa, xg, q, ka, va, iq, ik, iw, ga, gb = [w_in[:, a:b] for a, b in zip(c[:-1], c[1:])]
    pad = np.zeros((D, P - IDX_HEADS), w_in.dtype)

    def woven(*parts):
        t = np.stack([_tiles(p) for p in parts], 1)
        return t.reshape(-1, *t.shape[2:])

    return np.concatenate([
        woven(inp["ffn1_w_gate"][0], inp["ffn1_w_up"][0]), _down(inp["ffn1_w_down"][0]),
        _tiles(np.concatenate([iq, ik, ik, iw, pad, xwa, xg], 1)),
        woven(r, k, v, ga), woven(q, ka, va, gb),
        _tiles(inp["w_out_attn"][0]), _tiles(inp["w_out_rwkv"][0]), _tiles(inp["w_out"][0]),
        woven(inp["ffn2_w_gate"][0], inp["ffn2_w_up"][0]), _down(inp["ffn2_w_down"][0])])


def _params(inp):
    cols = [np.ravel(inp[n]).reshape(-1, P).T for n in PAR]
    return np.ascontiguousarray(np.concatenate(cols, 1))


def _constants():
    c = np.zeros((P, NCST), np.float32)
    i = np.arange(P)
    same = i[:, None] // HD == i[None, :] // HD
    c[:, C_ID:C_ID + P] = np.eye(P)
    c[:, C_ONE:C_ONE + P] = 1
    c[:, C_HEAD:C_HEAD + P] = same
    c[:, C_STRICT:C_STRICT + P] = same & (i[:, None] < i[None, :])
    c[:, C_INCL:C_INCL + P] = same & (i[:, None] <= i[None, :])
    c[:, C_SCAN:C_SCAN + T] = np.arange(T) % CH != 0
    c[:, C_VIS:C_VIS + P] = i[None, :] // CH <= i[:, None] // CH
    c[:, C_EPS], c[:, C_EPS + 1] = NORM_EPS, GN_EPS
    return c


def _layout(inputs):
    inp = {k: np.asarray(v) for k, v in inputs.items()}
    lora = np.zeros((P, 2, D), np.float32)
    lora[0:64, 0] = inp["decay_lora"][0]
    lora[64:128, 1] = inp["aaa_lora"][0]
    return {
        "x_in": np.ascontiguousarray(inp["x"][0].T.reshape(KD, P, T)),
        "ws": np.ascontiguousarray(_stream(inp)),
        "par_in": _params(inp),
        "cst_in": _constants(),
        "lora_in": lora,
        "glora_in": np.ascontiguousarray(inp["gate_lora"][0]),
    }


SHAPES = {"x_in": (KD, P, T), "ws": (NBLK, P, 8, P), "par_in": (P, NPAR), "cst_in": (P, NCST),
          "lora_in": (P, 2, D), "glora_in": (P, D)}
SCRATCH = {"sa_dram": (KD, P, T), "sb_dram": (KD, P, T), "rw_dram": (PAIRS, 5, P, T),
           "l_dram": (PAIRS, 2, NCH, CH, CH), "pd_dram": (PAIRS, 2, NCH, CH, CH),
           "t11_dram": (PAIRS, 2, NCH, HALF, HALF)}


def program(nc):
    ins = [nc.dram_tensor(n, s, F32, kind="ExternalInput").ap() for n, s in SHAPES.items()]
    out = nc.dram_tensor("out", (KD, P, T), F32, kind="ExternalOutput").ap()
    scratch = [nc.dram_tensor(n, s, F32, kind="Internal").ap() for n, s in SCRATCH.items()]
    build(nc, *ins, out, *scratch)


def kernel(**inputs):
    import concourse.bacc as _bacc
    from concourse.bass_utils import run_bass_kernel_spmd as _run

    nc = _bacc.Bacc("TRN2", target_bir_lowering=False, num_devices=1)
    program(nc)
    r = _run(nc, [_layout(inputs)], core_ids=[0])
    return r.results[0]["out"].reshape(1, D, T).transpose(0, 2, 1)
```

```python
from contextlib import ExitStack

import numpy as np

import concourse.bass as bass
import concourse.mybir as mybir

F32 = mybir.dt.float32
F32R = mybir.dt.float32r
ALU = mybir.AluOpType
ACT = mybir.ActivationFunctionType
AX = mybir.AxisListType

P = 128
T = 512
D = 1024
KD = D // P
D_FF = 2816
NF = D_FF // P
CH = 64
NCH = T // CH
HEADS = 16
HD = 64
PAIRS = HEADS // 2
IDX_HEADS = 8
TOPK = 128
NQ = T // P
HALF = CH // 2
NORM_EPS = 1e-6
GN_EPS = HD * 1e-5
DECAY_C = float(np.exp(-0.5))
IW_SCALE = IDX_HEADS ** -0.5 * HD ** -0.5
NEG = -3.0e38
MASKED = 1.0e30

DBLK = 3 * KD
PHASES = [("f1", 2 * NF), ("d1", DBLK), ("idx", 8), ("rw", 4 * PAIRS), ("att", 4 * PAIRS),
          ("ob", KD), ("oa", KD), ("out", KD), ("f2", 2 * NF), ("d2", DBLK)]
FIRST, _at, USES, _use = {}, 0, {}, 0
for _n, _c in PHASES:
    FIRST[_n] = _at
    _at += _c
    USES[_n] = _use
    _use += {"f": 0, "d": 2}.get(_n[0], _c // 4)
NBLK = _at

PAR, _at = {}, 0
for _n, _c in [("ffn1_norm", KD), ("mix_norm", KD), ("ffn2_norm", KD), ("final_norm", KD), ("k_k", KD),
               ("k_a", KD), ("r_k", KD), ("gn_weight", KD), ("gn_bias", KD), ("decay_base", KD),
               ("aaa_base", KD), ("time_mix", 26)]:
    PAR[_n] = _at
    _at += _c
NPAR = _at
C_ID, C_ONE, C_HEAD, C_STRICT, C_INCL, C_SCAN, C_VIS, C_EPS, NCST = 0, 128, 256, 384, 512, 640, 1152, 1280, 1282


class Tally:

    def __init__(self, sem):
        self.sem, self.base, self.n, self.turn, self.per = sem, 0, 0, 0, 0

    def mark(self, ins):
        ins.then_inc(self.sem, 1)
        self.n += 1
        return self.value()

    def value(self):
        return self.turn * self.per + (self.base + self.n) if self.per else self.base + self.n

    def enter(self, turn, per):
        self.base, self.n, self.turn, self.per = self.base + self.n, 0, turn, per

    def leave(self, turns):
        assert self.n == self.per, (self.n, self.per)
        self.base, self.n, self.turn, self.per = self.base + self.per * turns, 0, 0, 0


def build(nc, x_in, ws, par_in, cst_in, lora_in, glora_in, out, sa_dram, sb_dram, rw_dram, l_dram, pd_dram,
          t11_dram):
    with ExitStack() as ctx:
        top = [(nc.sbuf_base + 63) // 64 * 64]

        def at(name, shape, dtype, offset):
            return nc.alloc_sbuf_tensor_at(name, shape, dtype, offset=offset)

        def fixed(name, shape, dtype=F32):
            o = top[0]
            size = 4
            for s in shape[1:]:
                size *= s
            top[0] += (size + 31) // 32 * 32
            return at(name, shape, dtype, o)

        x = fixed("x", [P, KD, T])
        raw = fixed("raw", [P, 4, 8, P])
        whi = fixed("whi", [P, 2, 8, P], F32R)
        wlo = fixed("wlo", [P, 2, 8, P], F32R)
        par = fixed("par", [P, NPAR])
        cst = fixed("cst", [P, NCST + 1])
        warm = cst[:, NCST:NCST + 1]
        lx = fixed("lx", [P, T])
        xg = fixed("xg", [P, T])
        wend = fixed("wend", [P, PAIRS, NCH])
        rmax = fixed("rmax", [P, 4 * NQ])
        rms = fixed("rms", [P, NQ])
        R0 = top[0]
        K = 1024

        ident, ones, headsum = cst[:, C_ID:C_ID + P], cst[:, C_ONE:C_ONE + P], cst[:, C_HEAD:C_HEAD + P]
        strict, incl = cst[:, C_STRICT:C_STRICT + P], cst[:, C_INCL:C_INCL + P]
        resets, visible = cst[:, C_SCAN:C_SCAN + T], cst[:, C_VIS:C_VIS + P]

        def gain(name, k):
            return par[:, PAR[name] + k:PAR[name] + k + 1]

        hhi = at("hhi", [P, KD, T], F32R, R0)
        hlo = at("hlo", [P, KD, T], F32R, R0 + 16 * K)
        yhi = at("yhi", [P, KD, T], F32R, R0 + 118 * K)
        ylo = at("ylo", [P, KD, T], F32R, R0 + 134 * K)
        ahi = at("ahi", [P, NF, T], F32R, R0 + 32 * K)
        alo = at("alo", [P, NF, T], F32R, R0 + 76 * K)
        silu_g = at("silu_g", [P, T], F32, R0 + 120 * K)
        prod = at("prod", [P, T], F32, R0 + 122 * K)
        sq = at("sq", [P, KD, T], F32, R0)
        hn = at("hn", [P, KD, T], F32, R0 + 16 * K)
        ssums = [at(f"ssum{n}", [P, T], F32, R0 + k * K) for n, k in enumerate((124, 124, 102, 124))]
        squares = [at(f"squares{n}", [P, T], F32, R0 + k * K) for n, k in enumerate((126, 126, 104, 126))]
        iq = at("iq", [P, 4, T], F32, R0 + 32 * K)
        ik = at("ik", [P, T], F32, R0 + 40 * K)
        iwt = at("iwt", [P, T], F32, R0 + 42 * K)
        iw = at("iw", [P, NQ, P], F32, R0 + 44 * K)
        relu = at("relu", [P, 2, T], F32, R0 + 46 * K)
        score = at("score", [P, 3, T], F32, R0 + 56 * K)
        work = at("work", [P, 3, T], F32, R0 + 62 * K)
        bias = at("bias", [P, NQ, T], F32, R0 + 48 * K)
        shl = at("shl", [P, 2, T + 8], F32, R0 + 76 * K)
        shd = at("shd", [P, 2, T], F32, R0 + 81 * K)
        lora = at("lora", [P, 2, D], F32, R0 + 68 * K)
        zs = at("zs", [P, PAIRS, T], F32, R0 + 76 * K)
        az = at("az", [P, PAIRS, T], F32, R0 + 92 * K)
        kr = at("kr", [P, 2, T], F32, R0 + 32 * K)
        t_v = at("t_v", [P, T], F32, R0 + 36 * K)
        t_r = at("t_r", [P, T], F32, R0 + 38 * K)
        t_k = at("t_k", [P, T], F32, R0 + 40 * K)
        t_kk = at("t_kk", [P, T], F32, R0 + 42 * K)
        t_sq = at("t_sq", [P, T], F32, R0 + 44 * K)
        t_s = at("t_s", [P, T], F32, R0 + 46 * K)
        t_sm = at("t_sm", [P, T], F32, R0 + 48 * K)
        t_d = at("t_d", [P, T], F32, R0 + 50 * K)
        t_e = at("t_e", [P, T], F32, R0 + 52 * K)
        a_l = at("a_l", [P, NCH, P], F32, R0 + 68 * K)
        b_l = at("b_l", [P, NCH, P], F32, R0 + 72 * K)
        sh = at("sh", [P, 3, T + 8], F32, R0 + 108 * K)
        gt = at("gt", [P, T], F32, R0 + 114 * K + 128)
        lst = at("lst", [P, NCH, P], F32, R0 + 146 * K)
        top8 = at("top8", [P, 8], F32, R0 + 117 * K)
        qa = at("qa", [P, PAIRS, T], F32, R0 + 118 * K)
        ka = at("ka", [P, PAIRS, T], F32, R0 + 134 * K)
        va = at("va", [P, PAIRS, T], F32, R0 + 32 * K)
        vf = at("vf", [P, T], F32, R0 + 112 * K)
        ls = at("ls", [P, CH, CH], F32, R0 + 76 * K)
        tt = at("tt", [P, CH, CH], F32, R0 + 92 * K)
        tprod = at("tprod", [P, 2, HALF, HALF], F32, R0 + 68 * K)
        t11 = at("t11", [P, HALF, HALF], F32, R0 + 108 * K)
        qs = at("qs", [P, T], F32, R0 + 80 * K)
        ks = at("ks", [P, T], F32, R0 + 82 * K)
        vs = at("vs", [P, T], F32, R0 + 84 * K)
        prob = at("prob", [P, NQ, T], F32, R0 + 86 * K)
        probt = at("probt", [P, NQ, T], F32, R0 + 94 * K)
        abkrv = [at(f"abkrv{g}", [P, 4, 5, P], F32, R0 + (56, 0)[g] * K) for g in (0, 1)]
        a_bd, b_bd, k_bd, r_bd, v_bd = [[m[:, :, j, :] for m in abkrv] for j in range(5)]
        slots = iter([R0 + 2 * K * n for n in (33, 5, 34, 6, 35, 7, 36, 37, 38, 39, 8, 9, 10, 11, 12, 13, 14, 15)])

        def bd(name):
            return at(name, [P, 4, P], F32, next(slots))

        pd, t11b, l21 = [[bd(f"{n}_{g}") for g in (0, 1)] for n in ("pd", "t11b", "l21")]
        state = [bd("state0"), bd("state1")]
        m_x, m_u, m_g, m_p, vt, bt, kt = [bd(n) for n in ("m_x", "m_u", "m_g", "m_p", "vt", "bt", "kt")]
        m_ak, m_rb, m_rk = bd("m_ak"), bd("m_rb"), bd("m_rk")
        yo = at("yo", [P, PAIRS, T], F32, R0 + 102 * K)
        sgb = at("sgb", [P, KD, T], F32, R0 + 32 * K)
        rkw = at("rkw", [P, PAIRS, P], F32, R0 + 48 * K)
        glora = at("glora", [P, D], F32, R0 + 52 * K)
        krv = at("krv", [P, 2, 3, T], F32, R0 + 56 * K)
        g_d = at("g_d", [P, 2, T], F32, R0 + 68 * K)
        g_q = at("g_q", [P, T], F32, R0 + 72 * K)
        g_t = at("g_t", [P, 2 * NQ, HD], F32, R0 + 74 * K)
        g_s = rmax[:, 0:2 * NQ]
        g_b = at("g_b", [P, T], F32, R0 + 76 * K)
        g_c = at("g_c", [P, T], F32, R0 + 78 * K)
        g_v = at("g_v", [P, T], F32, R0 + 84 * K)
        sga = at("sga", [P, KD, T], F32, R0 + 86 * K)
        mtmp = at("mtmp", [P, 2, T], F32, R0 + 80 * K)
        outt = at("outt", [P, KD, T], F32, R0)

        bank = [ctx.enter_context(nc.psum_tensor(f"bank{n}", [P, T], F32)) for n in range(8)]

        def sem(name):
            return ctx.enter_context(nc.semaphore(name))

        loaded = [sem(f"loaded{n}") for n in range(4)]
        hi_ready, lo_ready, block_done = sem("hi_ready"), sem("lo_ready"), sem("block_done")
        taken = [sem(f"taken{n}") for n in range(4)]
        params = sem("params")
        x_loaded = [sem(f"x_loaded{k}") for k in range(KD)]
        x_done = sem("x_done")
        n_sq, n_sum, n_mean, n_sd, n_diag, n_spread = (sem("n_sq"), sem("n_sum"), sem("n_mean"), sem("n_sd"),
                                                       sem("n_diag"), sem("n_spread"))
        n_even, n_odd = sem("n_even"), sem("n_odd")
        n_hn, h_hi, h_lo = sem("n_hn"), sem("h_hi"), sem("h_lo")
        silu_ready, prod_ready, act_hi, act_lo = sem("silu_ready"), sem("prod_ready"), sem("act_hi"), sem("act_lo")
        dve_step = sem("dve_step")
        iwt_done, iw_ready, sc_done, relu_ready, sc_used = (sem("iwt_done"), sem("iw_ready"), sem("sc_done"),
                                                           sem("relu_ready"), sem("sc_used"))
        lx_ready, lx_raw = sem("lx_ready"), sem("lx_raw")
        lora_loaded, lora_mm, lora_ready = sem("lora_loaded"), sem("lora_mm"), sem("lora_ready")
        zeroed = sem("zeroed")
        shifted, kq_ready, kq_sq, kk_ss, kk_norm = (sem("shifted"), sem("kq_ready"), sem("kq_sq"), sem("kk_ss"),
                                                    sem("kk_norm"))
        scanned, decays, ab_ready, prepped = sem("scanned"), sem("decays"), sem("ab_ready"), sem("prepped")
        v_kept, kr_kept, ab_kept = sem("v_kept"), sem("kr_kept"), sem("ab_kept")
        sa_kept, sb_kept, l_kept, p_kept = sem("sa_kept"), sem("sb_kept"), sem("l_kept"), sem("p_kept")
        l_mm, l_out, ls_loaded, solved = sem("l_mm"), sem("l_out"), sem("ls_loaded"), sem("solved")
        vt_done, va_ready = sem("vt_done"), sem("va_ready")
        qk_copied, v_copied = sem("qk_copied"), sem("v_copied")
        logit, negmax, exped, prob_ready = sem("logit"), sem("negmax"), sem("exped"), sem("prob_ready")
        ptr, pt_taken, pv_done, y_hi, y_lo = sem("ptr"), sem("pt_taken"), sem("pv_done"), sem("y_hi"), sem("y_lo")
        c_cleared, c_loaded = [sem("c_clear0"), sem("c_clear1")], [sem("c_loaded0"), sem("c_loaded1")]
        c_tr, c_gram, c_g, c_gs, c_ag = sem("c_tr"), sem("c_gram"), sem("c_g"), sem("c_gs"), sem("c_ag")
        c_av, c_us, c_mat, c_x, c_xs, c_u = (sem("c_av"), sem("c_us"), sem("c_mat"), sem("c_x"), sem("c_xs"),
                                             sem("c_u"))
        c_y, c_ys, c_s, c_sr, c_ss = sem("c_y"), sem("c_ys"), sem("c_s"), sem("c_sr"), sem("c_ss")
        rkw_ready, krv_loaded, p_mean, p_sq, p_sd, p_ss = (sem("rkw_ready"), [sem("krv_a"), sem("krv_b")],
                                                           sem("p_mean"), sem("p_sq"), sem("p_sd"), sem("p_ss"))
        p_bonus, p_gate, p_y, p_rk, p_diff = sem("p_bonus"), sem("p_gate"), sem("p_y"), sem("p_rk"), sem("p_diff")
        p_turn, p_spread = sem("p_turn"), sem("p_spread")
        sga_loaded, sgb_loaded, merged, g_loaded = sem("sga_loaded"), sem("sgb_loaded"), sem("merged"), sem("g_loaded")
        settled = sem("settled")
        out_ready, out_kept = sem("out_ready"), sem("out_kept")

        block = ctx.enter_context(nc.Block())

        def settle(engine):
            engine.sem_inc(settled, 1)

        def begin_at_one(engine, *sems):
            for s in sems:
                engine.sem_inc(s, 1)

        def halves(buf):
            return [buf[HD * h:HD * h + HD, :, HD * h:HD * h + HD] for h in (0, 1)]

        @block.sync
        def _(sp):
            for k in range(KD):
                sp.dma_start(x[:, k, :], x_in[k, :, :]).then_inc(x_loaded[k], 16)
                if k == KD // 2:
                    sp.dma_start(cst[:, 0:NCST], cst_in).then_inc(params, 16)
                    sp.dma_start(par[:, :], par_in).then_inc(params, 16)
            for u in range(4):
                sp.dma_start(raw[:, u, :, :], ws[u, :, :, :]).then_inc(loaded[u], 16)

            def stream(turns):
                with sp.Fori(*turns) as i:
                    for u in range(4):
                        sp.wait_ge(lo_ready, 4 * i + u - 3)
                        sp.dma_start(raw[:, u, :, :], ws[4 * i + u, :, :, :]).then_inc(loaded[u], 16)

            def stage(g, c):
                g4 = 4 * g
                for h in range(2):
                    o = HD * h
                    sp.dma_start(abkrv[g][o:o + HD, :, :, o:o + HD].rearrange("p n j t -> p (n j) t"),
                                 rw_dram[g4:g4 + 4, :, o:o + HD, bass.ds(CH * c, CH)]
                                 .rearrange("n j p t -> p (n j) t")).then_inc(c_loaded[g], 16)
                for h in range(2):
                    o = HD * h
                    sp.dma_start(l21[g][o + HALF:o + CH, :, o:o + HALF],
                                 l_dram[g4:g4 + 4, h, c, HALF:CH, 0:HALF].rearrange("n t s -> t n s"))\
                        .then_inc(c_loaded[g], 16)
                    sp.dma_start(pd[g][o:o + HD, :, o:o + HD],
                                 pd_dram[g4:g4 + 4, h, c, :, :].rearrange("n s t -> s n t"))\
                        .then_inc(c_loaded[g], 16)
                    sp.dma_start(t11b[g][o:o + HALF, :, o:o + HALF],
                                 t11_dram[g4:g4 + 4, h, c, :, :].rearrange("n a b -> a n b"))\
                        .then_inc(c_loaded[g], 16)

            stream((1, FIRST["ob"] // 4))
            sp.wait_ge(ab_kept, 1 + 64 * PAIRS)
            sp.wait_ge(kr_kept, 1 + 16 * PAIRS)
            sp.wait_ge(v_kept, 1 + 16 * PAIRS)
            sp.wait_ge(p_kept, 32)
            sp.wait_ge(c_cleared[0], 1)
            stage(0, 0)
            stream((FIRST["ob"] // 4, FIRST["ob"] // 4 + 1))
            sp.wait_ge(c_cleared[1], 1)
            stage(1, 0)
            with sp.Fori(1, NCH) as c:
                for g in range(2):
                    sp.wait_ge(c_s, 2 * c + g)
                    stage(g, c)
            stream((FIRST["ob"] // 4 + 1, NBLK // 4))
            for k in range(KD):
                sp.wait_ge(out_ready, k + 1)
                sp.dma_start(out[k, :, :], outt[:, k, :]).then_inc(out_kept, 16)
            sp.wait_ge(out_kept, 16 * KD)

        @block.gpsimd
        def _(pool):
            def low_part(i, u):
                pool.wait_ge(hi_ready, 4 * i + u + 1)
                nc.gpsimd.tensor_tensor(wlo[:, u % 2, :, :], raw[:, u, :, :], whi[:, u % 2, :, :].bitcast(F32),
                                        ALU.subtract).then_inc(lo_ready, 1)

            def low_parts(turns):
                with pool.Fori(*turns) as i:
                    for u in range(4):
                        low_part(i, u)

            def normed_phase(turn, h0):
                low_part(turn, 0)
                low_part(turn, 1)
                for k in range(1, KD, 2):
                    pool.wait_ge(h_hi, h0 + k + 1)
                    nc.gpsimd.tensor_tensor(hlo[:, k, :], hn[:, k, :], hhi[:, k, :].bitcast(F32), ALU.subtract)\
                        .then_inc(n_odd, 1)
                low_part(turn, 2)
                low_part(turn, 3)

            def stage(p):
                nc.gpsimd.tensor_copy(qs[:, :], qa[:, p, :]).then_inc(qk_copied, 1)
                nc.gpsimd.tensor_copy(ks[:, :], ka[:, p, :]).then_inc(qk_copied, 1)

            normed_phase(0, 0)
            low_parts((1, FIRST["idx"] // 4))
            normed_phase(FIRST["idx"] // 4, KD)
            low_parts((FIRST["idx"] // 4 + 1, FIRST["ob"] // 4))
            pool.wait_ge(solved, 2)
            pool.wait_ge(va_ready, 1)
            stage(0)
            nc.gpsimd.tensor_copy(vs[:, :], va[:, 0, :]).then_inc(v_copied, 1)
            pool.wait_ge(block_done, 1 + FIRST["ob"])
            for buf in (abkrv[1][:, :, :, :], pd[1][:, :, :], l21[1][:, :, :]):
                nc.gpsimd.memset(buf, 0.0)
            nc.gpsimd.memset(t11b[1][:, :, :], 0.0).then_inc(c_cleared[1], 1)
            with pool.Fori(1, NCH) as c:
                pool.wait_ge(logit, 6 * c)
                settle(pool)
                stage(c)
                pool.wait_ge(pv_done, 1 + 2 * c)
                settle(pool)
                nc.gpsimd.tensor_copy(vs[:, :], va[:, c, :]).then_inc(v_copied, 1)
            low_parts((FIRST["ob"] // 4, FIRST["f2"] // 4))
            normed_phase(FIRST["f2"] // 4, 3 * KD)
            low_parts((FIRST["f2"] // 4 + 1, NBLK // 4))

        @block.scalar
        def _(act):

            def split(first, per, i, u):
                b = first + u
                act.wait_ge(loaded[b % 4], 16 * (b // 4 + 1) + 4 * per * i)
                if b >= 2 or per:
                    act.wait_ge(block_done, b + per * i)
                nc.scalar.copy(whi[:, b % 2, :, :], raw[:, b % 4, :, :]).then_inc(hi_ready, 1)

            def fetch_table(function, source=ones[:, 0:1]):
                nc.scalar.activation(warm, source, function, scale=0.0)

            def square_chunks(src_ready, chunks):
                for k in chunks:
                    if src_ready is None:
                        act.wait_ge(x_loaded[k], 16)
                    else:
                        act.wait_ge(x_done, src_ready + k + 1)
                    if k == 0:
                        fetch_table(ACT.Sqrt, x[:, 0, 0:1])
                    nc.scalar.activation(sq[:, k, :], x[:, k, :], ACT.Square).then_inc(n_sq, 1)

            def norm(which, src_ready):
                square_chunks(src_ready, range(KD) if src_ready is None else (KD - 1,))
                if src_ready is None:
                    act.wait_ge(params, 32)
                    split(0, 0, 0, 0)
                act.wait_ge(n_mean, which + 1)
                nc.scalar.activation(rms[:, :], bank[4][:, 0:NQ], ACT.Sqrt, scale=1.0 / D,
                                     bias=cst[:, C_EPS:C_EPS + 1]).then_inc(n_sd, 1)
                if which == 3:
                    return
                split(FIRST[("f1", "idx", "f2")[which]], 0, 0, 1)
                for k in range(KD):
                    act.wait_ge(n_hn, which * KD + k + 1)
                    nc.scalar.copy(hhi[:, k, :], hn[:, k, :]).then_inc(h_hi, 1)

            def feed(name, j0):
                b0 = FIRST[name]

                def quad(i, last):
                    for jj in range(2):
                        u = 2 * jj
                        act.wait_ge(block_done, 1 + b0 + u + 1 + 4 * i)
                        nc.scalar.activation(silu_g[:, :], bank[u][:, :], ACT.Silu).then_inc(silu_ready, 1)
                        split(b0, 4, i, u + 2)
                        if not (last and jj):
                            split(b0, 4, i, u + 3)
                        act.wait_ge(prod_ready, 2 + j0 + jj + 1 + 2 * i)
                        settle(act)
                        nc.scalar.copy(ahi[:, 2 * i + jj, :], prod[:, :]).then_inc(act_hi, 1)

                with act.Fori(0, NF // 2 - 1) as i:
                    quad(i, False)
                quad(NF // 2 - 1, True)

            def down(name, src_ready, last):
                b0 = FIRST[name]
                for u in range(DBLK - 1):
                    split(b0, 0, 0, u + 1)
                square_chunks(src_ready, range(KD - 1))
                if not last:
                    split(b0, 0, 0, DBLK)

            begin_at_one(act, pt_taken, sa_kept, sb_kept, v_kept, kr_kept, ab_kept, l_kept, l_out, c_ys, c_av)
            norm(0, None)
            feed("f1", 0)
            down("d1", 0, False)
            norm(1, 0)

            act.dma_start(lora[:, :, :], lora_in).then_inc(lora_loaded, 16)
            b0 = FIRST["idx"]
            for u in range(8):
                if u >= 1:
                    split(b0, 0, 0, u + 1)
                act.wait_ge(block_done, 1 + b0 + u + 1)
                if u < 4:
                    nc.scalar.copy(iq[:, u, :], bank[u][:, :]).then_inc(taken[u], 1)
                elif u == 4:
                    nc.scalar.copy(ik[:, :], bank[0][:, :]).then_inc(taken[0], 1)
                elif u == 5:
                    nc.scalar.mul(iwt[:, :], bank[1][:, :], IW_SCALE).then_inc(taken[1], 1)
                else:
                    nc.scalar.copy(shl[:, u - 6, 1:T + 1], bank[u - 4][:, :]).then_inc(taken[u - 4], 1)
            for n in range(3 * IDX_HEADS):
                w = P * (n // IDX_HEADS + 2)
                if n == 2 * IDX_HEADS + 1:
                    act.wait_ge(lx_raw, 2)
                    nc.scalar.activation(lx[0:64, :], shd[0:64, 0, :], ACT.Tanh).then_inc(lx_ready, 1)
                    nc.scalar.copy(lx[64:128, :], shd[64:128, 0, :]).then_inc(lx_ready, 1)
                act.wait_ge(sc_done, n + 1)
                if n >= 2:
                    act.wait_ge(sc_used, n - 1)
                nc.scalar.activation(relu[:, n % 2, 0:w], bank[4 + n % 4][:, 0:w], ACT.Relu)\
                    .then_inc(relu_ready, 1)

            nc.scalar.activation(xg[:, :], shd[:, 1, :], ACT.Sigmoid).then_inc(lx_ready, 1)
            act.wait_ge(lx_ready, 3)
            for n in range(2 * KD):
                m, which = n // 2, n % 2
                act.wait_ge(lora_mm, n + 1)
                nc.scalar.activation((zs, az)[which][:, m, :], bank[4 + n % 4][:, :], ACT.Sigmoid,
                                     bias=gain(("decay_base", "aaa_base")[which], m)).then_inc(lora_ready, 1)

            def norm_keys(p):
                act.wait_ge(kk_ss, p + 1)
                nc.scalar.activation(t_sq[:, :], bank[4][:, :], ACT.Sqrt).then_inc(kk_norm, 1)

            def finish_decays(p):
                act.wait_ge(scanned, p + 1)
                nc.scalar.activation(t_e[:, :], t_s[:, :], ACT.Exp, scale=DECAY_C).then_inc(decays, 1)
                nc.scalar.activation(t_sm[:, :], t_sm[:, :], ACT.Exp, scale=-DECAY_C).then_inc(decays, 1)
                nc.scalar.activation(t_s[:, :], t_s[:, :], ACT.Exp, scale=-DECAY_C).then_inc(decays, 1)
                act.dma_start(rw_dram[p, 4, :, :], t_v[:, :]).then_inc(v_kept, 16)

            def keep_pair(p):
                act.wait_ge(prepped, p + 1)
                act.dma_start(rw_dram[p, 2:4, :, :].rearrange("j p t -> p j t"), kr[:, :, :]).then_inc(kr_kept, 16)
                for j, buf in enumerate((a_l, b_l)):
                    for h in range(2):
                        o = HD * h
                        act.dma_start(rw_dram[p, j, o:o + HD, :].rearrange("p (c t) -> p c t", c=NCH),
                                      buf[o:o + HD, :, o:o + HD]).then_inc(ab_kept, 16)
                act.wait_ge(l_kept, 1 + 32 * p)
                for n in range(2):
                    act.wait_ge(l_mm, 2 * p + n + 1)
                    nc.scalar.copy(lst[:, 4 * n:4 * n + 4, :], bank[5 + n][:, :].rearrange("p (n s) -> p n s", n=4))\
                        .then_inc(l_out, 1)
                act.wait_ge(l_out, 1 + 2 * p + 2)
                for h in range(2):
                    o = HD * h
                    act.dma_start(l_dram[p, h].rearrange("c t s -> t c s"), lst[o:o + HD, :, o:o + HD])\
                        .then_inc(l_kept, 16)

            def rwkv_pair(p, p_before):
                b0, t0 = FIRST["rw"], USES["rw"]
                for s in range(4):
                    if s == 0 and p_before is not None:
                        norm_keys(p_before)
                    if s >= 1:
                        split(b0, 4, p, s + 1)
                    if s == 1 and p_before is not None:
                        finish_decays(p_before)
                    if s == 3:
                        act.wait_ge(kq_ready, p + 1)
                        nc.scalar.activation(t_sq[:, :], t_kk[:, :], ACT.Square).then_inc(kq_sq, 1)
                    if s == 3 and p_before is not None:
                        keep_pair(p_before)
                    act.wait_ge(block_done, 1 + b0 + s + 1 + 4 * p)
                    if s < 3:
                        if s == 0:
                            act.wait_ge(zeroed, 1)
                        if p_before is not None:
                            act.wait_ge(shifted, 1 + 3 * p_before + (2, 1, 3)[s])
                        nc.scalar.copy(sh[:, s, 1:T + 1], bank[s][:, :]).then_inc(taken[s], 1)
                    if s == 3:
                        split(b0, 4, p, 5)
                        act.wait_ge(sa_kept, 1 + 16 * p)
                        nc.scalar.activation(gt[:, :], bank[3][:, :], ACT.Sigmoid).then_inc(taken[3], 1)
                        act.wait_ge(taken[3], 1 + t0 + 1 + p)
                        act.dma_start(sa_dram[p, :, :], gt[:, :]).then_inc(sa_kept, 16)

            def attention_pair(p, first):
                b0, t0 = FIRST["att"], USES["att"]
                for s in range(4):
                    if s == 0 and first:
                        norm_keys(PAIRS - 1)
                    if s >= 1:
                        split(b0, 4, p, s + 1)
                    if s == 1 and first:
                        finish_decays(PAIRS - 1)
                    if s == 3 and first:
                        keep_pair(PAIRS - 1)
                    act.wait_ge(block_done, 1 + b0 + s + 1 + 4 * p)
                    settle(act)
                    if s == 0:
                        nc.scalar.activation(qa[:, p, :], bank[0][:, :], ACT.Copy, scale=HD ** -0.5).then_inc(taken[0], 1)
                    elif s == 1:
                        nc.scalar.copy(ka[:, p, :], bank[1][:, :]).then_inc(taken[1], 1)
                    elif s == 2:
                        if first:
                            act.wait_ge(shifted, 1 + 3 * PAIRS)
                        nc.scalar.copy(vf[:, :], bank[2][:, :]).then_inc(taken[2], 1)
                    else:
                        split(b0, 4, p, 5)
                        if first:
                            act.wait_ge(sa_kept, 1 + 16 * PAIRS)
                        act.wait_ge(sb_kept, 1 + 16 * p)
                        nc.scalar.activation(gt[:, :], bank[3][:, :], ACT.Sigmoid).then_inc(taken[3], 1)
                        act.wait_ge(taken[3], 1 + t0 + 1 + p)
                        act.dma_start(sb_dram[p, :, :], gt[:, :]).then_inc(sb_kept, 16)
                        if first:
                            act.wait_ge(kr_kept, 1 + 16 * PAIRS)
                            act.wait_ge(v_kept, 1 + 16 * PAIRS)
                        act.wait_ge(vt_done, p + 1)
                        settle(act)
                        nc.scalar.copy(va[:, p, :], bank[7][:, :]).then_inc(va_ready, 1)

            split(FIRST["rw"], 0, 0, 1)
            rwkv_pair(0, None)
            with act.Fori(0, PAIRS // 2 - 1) as i:
                rwkv_pair(2 * i + 1, 2 * i)
                rwkv_pair(2 * i + 2, 2 * i + 1)
            rwkv_pair(PAIRS - 1, PAIRS - 2)
            attention_pair(0, True)
            attention_pair(1, False)
            act.wait_ge(l_kept, 1 + 32 * PAIRS)
            act.dma_start(ls[:, :, :], l_dram.rearrange("n h c t s -> (n h c) t s")).then_inc(ls_loaded, 16)
            with act.Fori(2, PAIRS - 1) as i:
                fetch_table(ACT.Sigmoid)
                attention_pair(i, False)
            act.wait_ge(solved, 2)
            act.dma_start(pd_dram.rearrange("n h c s t -> (n h c) s t"), tt[:, :, :]).then_inc(p_kept, 16)
            act.dma_start(t11_dram.rearrange("n h c a b -> (n h c) a b"), t11[:, :, :]).then_inc(p_kept, 16)
            attention_pair(PAIRS - 1, False)
            act.wait_ge(p_kept, 32)
            act.wait_ge(sb_kept, 1 + 16 * PAIRS)

            with act.Fori(0, NCH) as c:
                fetch_table(ACT.Exp)
                for g in range(2):
                    it = 2 * c + g
                    o = HD * g
                    act.wait_ge(negmax, it + 1)
                    for q in range(NQ):
                        w = P * (q + 1)
                        nc.scalar.activation(prob[:, q, 0:w], prob[:, q, 0:w], ACT.Exp, bias=rmax[:, 4 + q:5 + q],
                                             accum_out=rmax[:, 8 + q:9 + q]).then_inc(exped, 1)
                    act.wait_ge(c_g, it + 1)
                    nc.scalar.copy(m_g[:, :, :], bank[3][:, :].rearrange("p (n s) -> p n s", n=4)).then_inc(c_gs, 1)
                    act.wait_ge(c_tr, 3 * it + 1)
                    nc.scalar.copy(vt[:, :, :], bank[0][:, :].rearrange("p (n s) -> p n s", n=4)).then_inc(c_av, 1)
                    act.wait_ge(c_tr, 3 * it + 3)
                    nc.scalar.copy(kt[:, :, :], bank[2][:, :].rearrange("p (n s) -> p n s", n=4)).then_inc(c_av, 1)
                    act.wait_ge(pv_done, 1 + it)
                    for n in range(3):
                        act.wait_ge(ptr, 1 + 3 * it + n + 1)
                        if n < 2:
                            nc.scalar.copy(probt[:, n, P * n:T], bank[4 + n][:, 0:P * (4 - n)]).then_inc(pt_taken, 1)
                        else:
                            nc.scalar.copy(probt[:, 2, 2 * P:T], bank[6][:, 0:2 * P]).then_inc(pt_taken, 1)
                            nc.scalar.copy(probt[:, 3, 3 * P:T], bank[6][:, 2 * P:3 * P]).then_inc(pt_taken, 1)
                    act.wait_ge(c_x, it + 1)
                    nc.scalar.copy(m_x[:, :, :], bank[2][:, :].rearrange("p (n s) -> p n s", n=4)).then_inc(c_xs, 1)
                    act.wait_ge(pv_done, 1 + it + 1)
                    settle(act)
                    nc.scalar.copy(yhi[o:o + HD, c, :], bank[7][o:o + HD, :]).then_inc(y_hi, 1)
                    act.wait_ge(c_y, it + 1)
                    settle(act)
                    for h in range(2):
                        nc.scalar.copy(yo[HD * h:HD * h + HD, 4 * g:4 * g + 4, bass.ds(CH * c, CH)],
                                       bank[0][HD * h:HD * h + HD, :].rearrange("p (n s) -> p n s", n=4)
                                       [:, :, HD * h:HD * h + HD]).then_inc(c_ys, 1)

            act.wait_ge(v_copied, PAIRS)
            act.wait_ge(y_lo, 1 + HEADS)
            act.wait_ge(sb_kept, 1 + 16 * PAIRS)
            act.dma_start(sgb[:, :, :], sb_dram.rearrange("k p t -> p k t")).then_inc(sgb_loaded, 16)
            act.dma_start(glora[:, :], glora_in).then_inc(g_loaded, 16)
            act.wait_ge(c_ss, 2 * NCH)
            for p in range(2):
                act.dma_start(krv[:, p, :, :], rw_dram[p, 2:5, :, :].rearrange("j p t -> p j t"))\
                    .then_inc(krv_loaded[p], 16)
            act.dma_start(sga[:, :, :], sa_dram.rearrange("k p t -> p k t")).then_inc(sga_loaded, 16)
            b0 = FIRST["ob"]

            def square(p):
                act.wait_ge(p_diff, p + 1)
                nc.scalar.activation(g_q[:, :], g_d[:, p % 2, :], ACT.Square).then_inc(p_sq, 1)

            for p in range(PAIRS):
                if p == 0:
                    square(0)
                split(b0, 0, 0, p + 2)
                act.wait_ge(p_ss, p + 1)
                nc.scalar.activation(g_s[:, :], bank[5][:, 0:2 * NQ], ACT.Sqrt, scale=1.0 / HD,
                                     bias=cst[:, C_EPS + 1:C_EPS + 2]).then_inc(p_sd, 1)
                if p + 1 < PAIRS:
                    square(p + 1)
                act.wait_ge(p_y, p + 1)
                nc.scalar.copy(hhi[:, p, :], g_c[:, :]).then_inc(h_hi, 1)
                if p + 2 < PAIRS:
                    act.dma_start(krv[:, p % 2, :, :], rw_dram[p + 2, 2:5, :, :].rearrange("j p t -> p j t"))\
                        .then_inc(krv_loaded[p % 2], 16)

            b0 = FIRST["oa"]
            for u in range(KD):
                if u >= 1:
                    split(b0, 0, 0, u + 1)
                if u == KD - 1:
                    split(b0, 0, 0, u + 2)
                act.wait_ge(merged, u + 1)
                nc.scalar.copy(yhi[:, u, :], mtmp[:, u % 2, :]).then_inc(y_hi, 1)
            b0 = FIRST["out"]
            for u in range(1, KD - 1):
                split(b0, 0, 0, u + 1)
            square_chunks(KD, range(KD - 1))
            split(b0, 0, 0, KD)
            norm(2, KD)
            feed("f2", NF)
            down("d2", 2 * KD, True)
            norm(3, 2 * KD)

        @block.vector
        def _(dve):
            step = Tally(dve_step)

            def chain(ins):
                dve.wait_ge(dve_step, step.mark(ins))

            def add_squares(which, chunks):
                ssum, total = ssums[which], squares[which]
                for k in chunks:
                    dve.wait_ge(n_sq, which * KD + k + 1)
                    src = sq[:, 0, :] if k == 1 else ssum[:, :]
                    if k < KD - 1:
                        chain(nc.vector.tensor_tensor(ssum[:, :], src, sq[:, k, :], ALU.add))
                    else:
                        nc.vector.tensor_tensor(total[:, :], src, sq[:, k, :], ALU.add).then_inc(n_sum, 1)

            def norm(which, name, h0):
                ssum = ssums[which]
                dve.wait_ge(n_sd, which + 1)
                chain(nc.vector.reciprocal(rms[:, :], rms[:, :]))
                nc.vector.tensor_tensor(ssum[:, :].rearrange("p (q t) -> p q t", q=NQ),
                                        ident.unsqueeze(1).to_broadcast([P, NQ, P]),
                                        rms[:, :].unsqueeze(2).to_broadcast([P, NQ, P]), ALU.mult).then_inc(n_diag, 1)
                dve.wait_ge(n_spread, which + 1)
                for k in range(KD):
                    dst = outt[:, k, :] if which == 3 else hn[:, k, :]
                    nc.vector.scalar_tensor_tensor(out=dst, in0=x[:, k, :], scalar=gain(name, k), in1=bank[5][:, :],
                                                   op0=ALU.mult, op1=ALU.mult)\
                        .then_inc(out_ready if which == 3 else n_hn, 1)
                for k in range(0, KD if which < 3 else 0, 2):
                    dve.wait_ge(h_hi, h0 + k + 1)
                    nc.vector.tensor_tensor(hlo[:, k, :], hn[:, k, :], hhi[:, k, :].bitcast(F32), ALU.subtract)\
                        .then_inc(n_even, 1)

            def feed(name, j0):
                b0 = FIRST[name]
                with dve.Fori(0, NF // 2) as i:
                    for jj in range(2):
                        dve.wait_ge(silu_ready, j0 + jj + 1 + 2 * i)
                        dve.wait_ge(block_done, 1 + b0 + 2 * jj + 2 + 4 * i)
                        dve.wait_ge(act_lo, 1 + j0 + jj + 2 * i)
                        nc.vector.tensor_tensor(prod[:, :], silu_g[:, :], bank[2 * jj + 1][:, :], ALU.mult)\
                            .then_inc(prod_ready, 1)
                        dve.wait_ge(act_hi, j0 + jj + 1 + 2 * i)
                        nc.vector.tensor_tensor(alo[:, 2 * i + jj, :], prod[:, :],
                                                ahi[:, 2 * i + jj, :].bitcast(F32), ALU.subtract).then_inc(act_lo, 1)

            def down(name, which):
                b0 = FIRST[name]
                for m in range(KD):
                    if m == KD - 1:
                        add_squares(which, range(1, KD - 1))
                    dve.wait_ge(block_done, 1 + b0 + 3 * m + 3)
                    nc.vector.scalar_tensor_tensor(out=x[:, m, :], in0=bank[m % 4][:, :], scalar=0.5, in1=x[:, m, :],
                                                   op0=ALU.mult, op1=ALU.add).then_inc(x_done, 1)
                    dve.wait_ge(x_done, X0[name] + m + 1)
                    dve.sem_inc(taken[m % 4], 1)
                add_squares(which, (KD - 1,))

            X0 = {"d1": 0, "d2": 2 * KD}
            begin_at_one(dve, *taken, act_lo, y_lo, shifted, c_us, c_mat, c_sr)
            dve.sem_inc(prod_ready, 2)
            add_squares(0, range(1, KD))
            dve.wait_ge(params, 32)
            norm(0, "ffn1_norm", 0)
            feed("f1", 0)
            down("d1", 1)
            norm(1, "mix_norm", KD)

            dve.wait_ge(iwt_done, 1)
            nc.vector.tensor_copy(iw[:, :, :], bank[4][:, :].rearrange("p (n s) -> p n s", n=4)).then_inc(iw_ready, 1)
            nc.vector.memset(sh[:, :, 0:1], 0.0).then_inc(zeroed, 1)
            chain(nc.vector.memset(shl[:, :, 0:1], 0.0))
            for s in range(2):
                dve.wait_ge(taken[2 + s], 1 + USES["idx"] + 2)
                chain(nc.vector.tensor_tensor(shd[:, s, :], shl[:, s, 0:T], shl[:, s, 1:T + 1], ALU.subtract))
                nc.vector.scalar_tensor_tensor(out=shd[:, s, :], in0=shd[:, s, :], scalar=gain("time_mix", 24 + s),
                                               in1=shl[:, s, 1:T + 1], op0=ALU.mult, op1=ALU.add).then_inc(lx_raw, 1)
            dve.wait_ge(iw_ready, 1)
            for n in range(3 * IDX_HEADS):
                q, hd = n // IDX_HEADS + 1, n % IDX_HEADS
                w = P * (q + 1)
                sc = score[:, q - 1, 0:w]
                dve.wait_ge(relu_ready, n + 1)
                if hd == 0:
                    ins = nc.vector.tensor_scalar(sc, relu[:, n % 2, 0:w], iw[:, q, hd:hd + 1], None, ALU.mult)
                else:
                    dve.wait_ge(sc_used, n)
                    ins = nc.vector.scalar_tensor_tensor(out=sc, in0=relu[:, n % 2, 0:w], scalar=iw[:, q, hd:hd + 1],
                                                         in1=sc, op0=ALU.mult, op1=ALU.add)
                ins.then_inc(sc_used, 1)
            dve.wait_ge(sc_used, 3 * IDX_HEADS)
            dve.wait_ge(lora_mm, 2 * KD)
            chain(nc.vector.memset(a_l[:, :, :], 0.0))
            chain(nc.vector.memset(b_l[:, :, :], 0.0))
            dve.wait_ge(lora_ready, 2 * KD)

            def chunks(buf):
                return [buf[HD * h:HD * h + HD, :].rearrange("p (c t) -> p c t", c=NCH) for h in (0, 1)]

            def shift_pair(p):
                t0 = USES["rw"]
                for n, (s, dst) in enumerate(((1, t_k), (0, t_r), (2, t_v))):
                    dve.wait_ge(taken[s], 1 + t0 + 1 + p)
                    if s == 2:
                        dve.wait_ge(v_kept, 1 + 16 * p)
                    chain(nc.vector.tensor_tensor(t_d[:, :], sh[:, s, 0:T], sh[:, s, 1:T + 1], ALU.subtract))
                    mix = PAR["time_mix"] + 8 * s
                    nc.vector.scalar_tensor_tensor(out=dst[:, :], in0=t_d[:, :], scalar=par[:, bass.ds(mix + p, 1)],
                                                   in1=sh[:, s, 1:T + 1], op0=ALU.mult, op1=ALU.add)\
                        .then_inc(shifted, 1)
                    dve.wait_ge(shifted, 1 + 3 * p + n + 1)
                    if s == 1:
                        nc.vector.tensor_scalar(t_kk[:, :], t_k[:, :], par[:, bass.ds(PAR["k_k"] + p, 1)], None,
                                                ALU.mult).then_inc(kq_ready, 1)
                chain(nc.vector.tensor_tensor_scan(t_s[:, :], resets, zs[:, p, :], 0.0, ALU.mult, ALU.add))
                nc.vector.tensor_tensor(t_sm[:, :], t_s[:, :], zs[:, p, :], ALU.subtract).then_inc(scanned, 1)

            def prepare_pair(p):
                chain(nc.vector.tensor_scalar(t_d[:, :], az[:, p, :], -1.0, par[:, bass.ds(PAR["k_a"] + p, 1)],
                                              ALU.add, ALU.mult))
                chain(nc.vector.scalar_tensor_tensor(out=t_d[:, :], in0=t_d[:, :], scalar=1.0, in1=t_k[:, :],
                                                     op0=ALU.add, op1=ALU.mult))
                dve.wait_ge(kk_norm, p + 1)
                chain(nc.vector.tensor_scalar(t_sq[:, :], t_sq[:, :], 1e-12, None, ALU.max))
                chain(nc.vector.reciprocal(t_sq[:, :], t_sq[:, :]))
                chain(nc.vector.tensor_tensor(t_kk[:, :], t_kk[:, :], t_sq[:, :], ALU.mult))
                chain(nc.vector.tensor_tensor(t_sq[:, :], t_kk[:, :], az[:, p, :], ALU.mult))
                dve.wait_ge(decays, 3 * p + 3)
                dve.wait_ge(ab_kept, 1 + 64 * p)
                dve.wait_ge(kr_kept, 1 + 16 * p)
                for d, k_, s_ in zip(halves(a_l), chunks(t_kk), chunks(t_sm)):
                    nc.vector.scalar_tensor_tensor(out=d, in0=k_, scalar=-1.0, in1=s_, op0=ALU.mult, op1=ALU.mult)
                for d, b_, e_ in zip(halves(b_l), chunks(t_sq), chunks(t_e)):
                    nc.vector.tensor_tensor(d, b_, e_, ALU.mult).then_inc(ab_ready, 1)
                nc.vector.tensor_tensor(kr[:, 0, :], t_d[:, :], t_e[:, :], ALU.mult)
                chain(nc.vector.tensor_copy(wend[:, p, :], t_s[:, CH - 1:T:CH]))
                chain(nc.vector.tensor_tensor(kr[:, 1, :], t_r[:, :], t_s[:, :], ALU.mult))
                dve.sem_inc(prepped, 1)

            shift_pair(0)
            with dve.Fori(0, PAIRS - 1) as i:
                step.enter(i, 8 + 4)
                prepare_pair(i)
                shift_pair(i + 1)
            step.leave(PAIRS - 1)
            prepare_pair(PAIRS - 1)

            for q in range(1, NQ):
                w = P * (q + 1)
                chain(nc.vector.memset(score[0:CH, q - 1, w - CH:w], NEG))
                chain(nc.vector.tensor_copy(work[:, q - 1, 0:w], score[:, q - 1, 0:w]))
                for _ in range(TOPK // 8):
                    chain(nc.vector.max(top8[:, :], work[:, q - 1, 0:w]))
                    chain(nc.vector.match_replace(work[:, q - 1, 0:w], top8[:, :], work[:, q - 1, 0:w], NEG))
                chain(nc.vector.tensor_tensor(bias[:, q, 0:w], score[:, q - 1, 0:w], work[:, q - 1, 0:w],
                                              ALU.not_equal))
                chain(nc.vector.tensor_scalar(bias[:, q, 0:w], bias[:, q, 0:w], -1.0, MASKED, ALU.add, ALU.mult))
            chain(nc.vector.tensor_scalar(bias[:, 0, 0:P], visible, -1.0, MASKED, ALU.add, ALU.mult))

            def blocks(buf, a, b, step_a, step_b, n_a, n_b):
                return bass.AP(buf, buf[:, a, b:b + 1].offset,
                               [list(buf[:, 0, 0:1].ap[0]), [HALF * CH + HALF, 2], [step_a, n_a], [step_b, n_b]])

            dve.wait_ge(l_mm, 2 * PAIRS)
            dve.wait_ge(ab_kept, 1 + 64 * PAIRS)
            dve.wait_ge(ls_loaded, 16)
            chain(nc.vector.memset(tt[:, :, :], 0.0))
            chain(nc.vector.memset(tt[:, :, :].rearrange("p a b -> p (a b)")[:, 0::CH + 1], 1.0))
            for t in range(1, HALF):
                chain(nc.vector.tensor_tensor(tprod[:, :, 0:t, 0:t], blocks(ls, t, 0, 0, 1, t, t),
                                              blocks(tt, 0, 0, CH, 1, t, t), ALU.mult))
                chain(nc.vector.tensor_reduce(blocks(tt, 0, t, CH, 1, t, 1), tprod[:, :, 0:t, 0:t], AX.X, ALU.add))
            nc.vector.tensor_copy(t11[:, :, :], tt[:, 0:HALF, 0:HALF].rearrange("p a b -> p b a")).then_inc(solved, 2)

            dve.wait_ge(solved, 2)
            nc.vector.memset(state[0][:, :, :], 0.0)
            chain(nc.vector.memset(state[1][:, :, :], 0.0))
            for buf in (abkrv[0][:, :, :, :], pd[0][:, :, :], l21[0][:, :, :]):
                nc.vector.memset(buf, 0.0)
            chain(nc.vector.memset(t11b[0][:, :, :], 0.0))
            dve.sem_inc(c_cleared[0], 1)
            dve.wait_ge(p_kept, 32)
            dve.wait_ge(block_done, 1 + FIRST["ob"])

            def four(b):
                return bank[b][:, :].rearrange("p (n s) -> p n s", n=4)

            def masked(dst, b, mask):
                nc.vector.tensor_tensor(dst[:, :, :], four(b), mask.unsqueeze(1).to_broadcast([P, 4, P]),
                                        ALU.mult).then_inc(c_us, 1)

            def biased_logits(it):
                dve.wait_ge(ptr, 1 + 3 * it)
                for q in range(NQ):
                    w = P * (q + 1)
                    if q != 1:
                        dve.wait_ge(logit, 3 * it + max(q, 1))
                    c0 = P if q == 1 else 0
                    settle(dve)
                    chain(nc.vector.tensor_tensor_reduce(
                        out=prob[:, q, 0:w], in0=bank[(4, 4, 5, 6)[q]][:, c0:c0 + w], in1=bias[:, q, 0:w],
                        scale=1.0, scalar=NEG, op0=ALU.add, op1=ALU.max, accum_out=rmax[:, q:q + 1]))
                nc.vector.tensor_scalar(rmax[:, 4:8], rmax[:, 0:4], -1.0, None, ALU.mult).then_inc(negmax, 1)

            def chunk(c, last):
                for g in range(2):
                    it = 2 * c + g
                    g4 = 4 * g
                    o = HD * g
                    dve.wait_ge(exped, 4 * it + 4)
                    chain(nc.vector.reciprocal(rmax[:, 12:16], rmax[:, 8:12]))
                    for q in range(NQ):
                        w = P * (q + 1)
                        nc.vector.tensor_scalar(prob[:, q, 0:w], prob[:, q, 0:w], rmax[:, 12 + q:13 + q], None,
                                                ALU.mult).then_inc(prob_ready, 1)
                    dve.wait_ge(c_tr, 3 * it + 2)
                    nc.vector.tensor_copy(bt[:, :, :], four(1)).then_inc(c_us, 1)
                    dve.wait_ge(c_gram, 3 * it + 1)
                    masked(m_rb, 7, incl)
                    dve.wait_ge(c_gram, 3 * it + 2)
                    masked(m_ak, 0, strict)
                    dve.wait_ge(c_ag, it + 1)
                    nc.vector.tensor_tensor(m_p[:, :, :], pd[g][:, :, :], four(3), ALU.add).then_inc(c_mat, 1)
                    dve.wait_ge(c_gram, 3 * it + 3)
                    masked(m_rk, 1, incl)
                    dve.wait_ge(c_u, it + 1)
                    nc.vector.tensor_copy(m_u[:, :, :], four(3)).then_inc(c_us, 1)
                    dve.wait_ge(y_hi, it + 1)
                    nc.vector.tensor_tensor(ylo[o:o + HD, c, :], bank[7][o:o + HD, :],
                                            yhi[o:o + HD, c, :].bitcast(F32), ALU.subtract).then_inc(y_lo, 1)
                    if not (last and g):
                        biased_logits(it + 1)
                    dve.wait_ge(c_s, 1 + it + 1)
                    nc.vector.tensor_tensor(state[g][:, :, :], state[g][:, :, :], four(1), ALU.add).then_inc(c_sr, 1)
                    dve.wait_ge(c_sr, 1 + it + 1)
                    nc.vector.tensor_tensor(state[g][:, :, :], state[g][:, :, :],
                                            wend[:, g4:g4 + 4, bass.ds(c, 1)].to_broadcast([P, 4, P]), ALU.mult)\
                        .then_inc(c_ss, 1)

            biased_logits(0)
            with dve.Fori(0, NCH - 1) as c:
                step.enter(c, 2 * 5)
                chunk(c, False)
            step.leave(NCH - 1)
            chunk(NCH - 1, True)

            for p in range(PAIRS):
                nc.vector.tensor_scalar(rkw[:, p, :], headsum, gain("r_k", p), None, ALU.mult).then_inc(rkw_ready, 1)
            b0 = FIRST["ob"]
            dve.wait_ge(c_ys, 1 + 4 * NCH)

            def difference(p):
                dve.wait_ge(p_mean, p + 1)
                nc.vector.scalar_tensor_tensor(out=g_d[:, p % 2, :], in0=bank[4][:, :], scalar=-1.0 / HD,
                                               in1=yo[:, p, :], op0=ALU.mult, op1=ALU.add).then_inc(p_diff, 1)

            def keys_queries(p):
                dve.wait_ge(krv_loaded[p % 2], 16 * (p // 2 + 1))
                nc.vector.tensor_tensor(g_b[:, :], krv[:, p % 2, 1, :], krv[:, p % 2, 0, :], ALU.mult).then_inc(p_rk, 1)

            def gated(m):
                dve.wait_ge(block_done, 1 + b0 + m + 1)
                dve.wait_ge(sgb_loaded, 16)
                nc.vector.tensor_tensor(sgb[:, m, :], sgb[:, m, :], bank[m % 4][:, :], ALU.mult)\
                    .then_inc(taken[m % 4], 1)

            for p in range(PAIRS):
                if p == 0:
                    difference(0)
                    keys_queries(0)
                dve.wait_ge(p_sd, p + 1)
                chain(nc.vector.reciprocal(g_s[:, :], g_s[:, :]))
                nc.vector.tensor_copy(g_t[:, :, :], g_s[:, :].unsqueeze(2).to_broadcast([P, 2 * NQ, HD]))\
                    .then_inc(p_turn, 1)
                if p + 1 < PAIRS:
                    difference(p + 1)
                dve.wait_ge(p_bonus, p + 1)
                chain(nc.vector.tensor_tensor(g_v[:, :], krv[:, p % 2, 2, :], bank[6][:, :], ALU.mult))
                if p + 1 < PAIRS:
                    keys_queries(p + 1)
                dve.wait_ge(p_spread, p + 1)
                chain(nc.vector.scalar_tensor_tensor(out=g_c[:, :], in0=g_d[:, p % 2, :], scalar=gain("gn_weight", p),
                                                     in1=bank[5][:, :], op0=ALU.mult, op1=ALU.mult))
                chain(nc.vector.scalar_tensor_tensor(out=g_c[:, :], in0=g_c[:, :], scalar=gain("gn_bias", p),
                                                     in1=g_v[:, :], op0=ALU.add, op1=ALU.add))
                dve.wait_ge(p_gate, p + 1)
                nc.vector.tensor_tensor(g_c[:, :], g_c[:, :], bank[7][:, :], ALU.mult).then_inc(p_y, 1)
                dve.wait_ge(h_hi, 2 * KD + p + 1)
                nc.vector.tensor_tensor(hlo[:, p, :], g_c[:, :], hhi[:, p, :].bitcast(F32), ALU.subtract)\
                    .then_inc(h_lo, 1)
                gated(p)

            b0 = FIRST["oa"]
            dve.wait_ge(sga_loaded, 16)
            for m in range(KD):
                dve.wait_ge(block_done, 1 + b0 + m + 1)
                if m >= 2:
                    dve.wait_ge(y_lo, 1 + HEADS + m - 1)
                nc.vector.tensor_tensor(mtmp[:, m % 2, :], sga[:, m, :], bank[m % 4][:, :], ALU.mult)\
                    .then_inc(taken[m % 4], 1)
                dve.wait_ge(taken[m % 4], 1 + USES["oa"] + 1 + m // 4)
                nc.vector.tensor_tensor(mtmp[:, m % 2, :], mtmp[:, m % 2, :], sgb[:, m, :], ALU.add)\
                    .then_inc(merged, 1)
                dve.wait_ge(y_hi, HEADS + m + 1)
                nc.vector.tensor_tensor(ylo[:, m, :], mtmp[:, m % 2, :], yhi[:, m, :].bitcast(F32), ALU.subtract)\
                    .then_inc(y_lo, 1)
            b0 = FIRST["out"]
            for m in range(KD):
                if m == KD - 1:
                    add_squares(2, range(1, KD - 1))
                dve.wait_ge(block_done, 1 + b0 + m + 1)
                nc.vector.tensor_tensor(x[:, m, :], x[:, m, :], bank[m % 4][:, :], ALU.add).then_inc(x_done, 1)
                dve.wait_ge(x_done, KD + m + 1)
                dve.sem_inc(taken[m % 4], 1)
            add_squares(2, (KD - 1,))
            norm(2, "ffn2_norm", 3 * KD)
            feed("f2", NF)
            down("d2", 3)
            norm(3, "final_norm", 0)

        @block.tensor
        def _(pe):
            def products(u, acc, hi, lo, tiles, first, last):
                n = len(tiles)
                for t, k in enumerate(tiles):
                    a, b = whi[:, u % 2, t, :], wlo[:, u % 2, t, :]
                    nc.tensor.matmul(acc, a, hi[:, k, :], start=first and t == 0, stop=False)
                    nc.tensor.matmul(acc, a, lo[:, k, :], start=False, stop=False)
                    ins = nc.tensor.matmul(acc, b, hi[:, k, :], start=False, stop=last and t == n - 1)
                ins.then_inc(block_done, 1)

            def project(first, per, i, u, hi, lo):
                pe.wait_ge(lo_ready, first + u + 1 + per * i)
                products(u, bank[u % 4][:, :], hi, lo, range(8), True, True)

            def products_of_normed(first, which, h0):
                pe.wait_ge(lo_ready, first + 1)
                for k in range(KD):
                    pe.wait_ge(h_hi, h0 + k + 1)
                    nc.tensor.matmul(bank[0][:, :], whi[:, 0, k, :], hhi[:, k, :], start=k == 0, stop=False)
                    nc.tensor.matmul(bank[0][:, :], wlo[:, 0, k, :], hhi[:, k, :], start=False, stop=False)
                for n, k in enumerate((1, 3, 5, 0, 2, 7, 4, 6)):
                    pe.wait_ge((n_even, n_odd)[k % 2], KD // 2 * which + k // 2 + 1)
                    ins = nc.tensor.matmul(bank[0][:, :], whi[:, 0, k, :], hlo[:, k, :], start=False, stop=n == KD - 1)
                ins.then_inc(block_done, 1)

            def project_late(first, hi, lo, ready, h0):
                pe.wait_ge(lo_ready, first + 1)
                for k in range(KD):
                    pe.wait_ge(ready, h0 + k + 1)
                    nc.tensor.matmul(bank[0][:, :], whi[:, 0, k, :], hi[:, k, :], start=k == 0, stop=False)
                    nc.tensor.matmul(bank[0][:, :], whi[:, 0, k, :], lo[:, k, :], start=False, stop=False)
                    ins = nc.tensor.matmul(bank[0][:, :], wlo[:, 0, k, :], hi[:, k, :], start=False, stop=k == KD - 1)
                ins.then_inc(block_done, 1)

            def norm(which):
                pe.wait_ge(n_sum, which + 1)
                for q in range(NQ):
                    ins = nc.tensor.matmul(bank[4][:, q:q + 1], squares[which][:, P * q:P * q + P], ones[:, 0:1],
                                           start=True, stop=True)
                ins.then_inc(n_mean, 1)
                pe.wait_ge(n_diag, which + 1)
                nc.tensor.matmul(bank[5][:, :], ones, ssums[which][:, :], start=True, stop=True).then_inc(n_spread, 1)

            def feed(name, j0, h0):
                def quad(i, units=range(4)):
                    for u in units:
                        if u % 2 == 0:
                            pe.wait_ge(prod_ready, 2 + j0 + u // 2 - 1 + 2 * i)
                        project(FIRST[name], 4, i, u, hhi, hlo)

                pe.wait_ge(prod_ready, 2 + j0 - 1)
                products_of_normed(FIRST[name], (0, 2)[j0 > 0], h0)
                quad(0, (1, 2, 3))
                with pe.Fori(1, NF // 2) as i:
                    quad(i)

            def down(name, a0):
                b0, t0 = FIRST[name], USES[name]
                pe.wait_ge(act_lo, 1 + a0 - NF + 2 * KD)
                with pe.Fori(0, 2) as i:
                    for m in range(4):
                        pe.wait_ge(taken[m], 1 + t0 + i)
                        for k in range(3):
                            u = 3 * m + k
                            if u == 2:
                                pe.wait_ge(act_lo, 1 + a0)
                            pe.wait_ge(lo_ready, b0 + u + 1 + 12 * i)
                            products(u, bank[m][:, :], ahi, alo, range(8 * k, min(8 * k + 8, NF)), k == 0, k == 2)

            begin_at_one(pe, block_done, ptr, pv_done, c_s)
            pe.wait_ge(params, 32)
            norm(0)
            feed("f1", 0, 0)
            down("d1", NF)
            norm(1)

            b0, t0 = FIRST["idx"], USES["idx"]
            pe.wait_ge(taken[0], 1 + t0)
            products_of_normed(b0, 1, KD)
            for u in range(1, 8):
                pe.wait_ge(taken[u % 4], 1 + t0 + u // 4)
                project(b0, 0, 0, u, hhi, hlo)
                if u == 6:
                    pe.wait_ge(taken[1], 1 + t0 + 2)
                    for q in range(NQ):
                        ins = nc.tensor.transpose(bank[4][:, P * q:P * q + P], iwt[:, P * q:P * q + P], ident)
                    ins.then_inc(iwt_done, 1)
            pe.wait_ge(taken[0], 1 + t0 + 2)
            pe.wait_ge(taken[3], 1 + t0 + 1)
            for n in range(3 * IDX_HEADS):
                q, hd = n // IDX_HEADS + 1, n % IDX_HEADS
                o = HD * (hd % 2)
                if n == 0:
                    pe.wait_ge(iw_ready, 1)
                if n >= 4:
                    pe.wait_ge(relu_ready, n - 3)
                nc.tensor.matmul(bank[4 + n % 4][:, 0:P * (q + 1)], iq[o:o + HD, hd // 2, P * q:P * q + P],
                                 ik[o:o + HD, 0:P * (q + 1)], start=True, stop=True).then_inc(sc_done, 1)

            pe.wait_ge(lx_ready, 2)
            pe.wait_ge(lora_loaded, 16)
            for n in range(2 * KD):
                if n >= 4:
                    pe.wait_ge(lora_ready, n - 3)
                else:
                    pe.wait_ge(relu_ready, 3 * IDX_HEADS - 3 + n)
                m = n // 2
                nc.tensor.matmul(bank[4 + n % 4][:, :], lora[:, n % 2, P * m:P * m + P], lx[:, :],
                                 start=True, stop=True).then_inc(lora_mm, 1)
            pe.wait_ge(lora_ready, 2 * KD)

            def chunk_products(p):
                pe.wait_ge(ab_ready, 2 * p + 2)
                pe.wait_ge(l_out, 1 + 2 * p)
                for n in range(2):
                    for j in range(4):
                        ins = nc.tensor.matmul(bank[5 + n][:, P * j:P * j + P], a_l[:, 4 * n + j, :],
                                               b_l[:, 4 * n + j, :], start=True, stop=True)
                    ins.then_inc(l_mm, 1)

            def quad(name, p, p_before):
                b0, t0 = FIRST[name], USES[name]
                for u in range(4):
                    pe.wait_ge(taken[u], 1 + t0 + p)
                    project(b0, 4, p, u, hhi, hlo)
                    if u == 2 and p_before is not None:
                        chunk_products(p_before)

            def rwkv_pair(p, p_before):
                quad("rw", p, p_before)
                pe.wait_ge(kq_sq, p + 1)
                nc.tensor.matmul(bank[4][:, :], headsum, t_sq[:, :], start=True, stop=True).then_inc(kk_ss, 1)

            def attention_pair(p, p_before):
                quad("att", p, p_before)
                pe.wait_ge(taken[2], 1 + USES["att"] + 1 + p)
                if p_before is None:
                    pe.wait_ge(va_ready, p)
                for q in range(NQ):
                    ins = nc.tensor.transpose(bank[7][:, P * q:P * q + P], vf[:, P * q:P * q + P], ident)
                ins.then_inc(vt_done, 1)

            rwkv_pair(0, None)
            with pe.Fori(0, PAIRS - 1) as i:
                rwkv_pair(i + 1, i)
            attention_pair(0, PAIRS - 1)
            with pe.Fori(1, PAIRS) as i:
                attention_pair(i, None)

            def group(b, *terms):
                for n in range(4):
                    for k, (lhs, rhs) in enumerate(terms):
                        ins = nc.tensor.matmul(bank[b][:, P * n:P * n + P], lhs[:, n, :], rhs[:, n, :],
                                               start=k == 0, stop=k == len(terms) - 1)
                return ins

            def turned(b, src):
                for n in range(4):
                    ins = nc.tensor.transpose(bank[b][:, P * n:P * n + P], src[:, n, :], ident)
                return ins

            def logits(c, g):
                it = 2 * c + g
                o = HD * g
                pe.wait_ge(qk_copied, 2 * c + 2)
                pe.wait_ge(pt_taken, 1 + 4 * it)
                for q in range(NQ):
                    w = P * (q + 1)
                    c0 = P if q == 1 else 0
                    ins = nc.tensor.matmul(bank[(4, 4, 5, 6)[q]][:, c0:c0 + w], qs[o:o + HD, P * q:P * q + P],
                                           ks[o:o + HD, 0:w], start=True, stop=True)
                    if q != 0:
                        ins.then_inc(logit, 1)

            def chunk(c, last):
                for g in range(2):
                    it = 2 * c + g
                    o = HD * g
                    pe.wait_ge(c_loaded[g], 128 * c + 128)
                    pe.wait_ge(c_us, 1 + 5 * it)
                    group(3, (l21[g], pd[g])).then_inc(c_g, 1)
                    pe.wait_ge(c_ys, 1 + 2 * it)
                    turned(0, v_bd[g]).then_inc(c_tr, 1)
                    pe.wait_ge(c_sr, 1 + it)
                    turned(1, b_bd[g]).then_inc(c_tr, 1)
                    turned(2, k_bd[g]).then_inc(c_tr, 1)
                    pe.wait_ge(y_lo, 1 + it)
                    group(7, (b_bd[g], r_bd[g])).then_inc(c_gram, 1)
                    pe.wait_ge(c_gs, it + 1)
                    group(3, (t11b[g], m_g)).then_inc(c_ag, 1)
                    pe.wait_ge(c_av, 1 + 2 * it + 1)
                    group(0, (k_bd[g], a_bd[g])).then_inc(c_gram, 1)
                    pe.wait_ge(prob_ready, 4 * it + 4)
                    for kt_, (lo_q, bk, c0) in enumerate([(0, 4, 0), (1, 5, 0), (2, 6, 0), (3, 6, 2 * P)]):
                        for q in range(lo_q, NQ):
                            ins = nc.tensor.transpose(bank[bk][:, c0 + P * (q - lo_q):c0 + P * (q - lo_q) + P],
                                                      prob[:, q, P * kt_:P * kt_ + P], ident)
                        if kt_ != 2:
                            ins.then_inc(ptr, 1)
                    pe.wait_ge(c_av, 1 + 2 * it + 2)
                    pe.wait_ge(c_us, 1 + 5 * it + 3)
                    group(2, (a_bd[g], state[g]), (m_ak, vt)).then_inc(c_x, 1)
                    group(1, (k_bd[g], r_bd[g])).then_inc(c_gram, 1)
                    pe.wait_ge(c_mat, 1 + it + 1)
                    pe.wait_ge(c_xs, it + 1)
                    group(3, (m_p, m_x)).then_inc(c_u, 1)
                    pe.wait_ge(v_copied, c + 1)
                    pe.wait_ge(pt_taken, 1 + 4 * it + 4)
                    for kt_ in range(NQ):
                        ins = nc.tensor.matmul(bank[7][o:o + HD, P * kt_:T], vs[:, P * kt_ + o:P * kt_ + o + HD],
                                               probt[:, kt_, P * kt_:T], start=(kt_ == 0), stop=(kt_ == NQ - 1))
                    ins.then_inc(pv_done, 1)
                    if not (last and g):
                        logits(c + g, 1 - g)
                    pe.wait_ge(c_us, 1 + 5 * it + 5)
                    group(0, (state[g], r_bd[g]), (m_u, m_rb), (vt, m_rk)).then_inc(c_y, 1)
                    group(1, (bt, m_u), (kt, vt)).then_inc(c_s, 1)

            pe.wait_ge(l_out, 1 + 2 * PAIRS)
            pe.wait_ge(kk_norm, PAIRS)
            logits(0, 0)
            for m in range(4):
                pe.wait_ge(taken[m], 1 + USES["ob"])
            pe.wait_ge(va_ready, PAIRS)
            with pe.Fori(0, NCH - 1) as c:
                chunk(c, False)
            chunk(NCH - 1, True)

            b0, t0 = FIRST["ob"], USES["ob"]
            pe.wait_ge(c_ys, 1 + 4 * NCH)
            pe.wait_ge(c_sr, 1 + 2 * NCH)
            pe.wait_ge(y_lo, 1 + HEADS)

            def mean(p):
                nc.tensor.matmul(bank[4][:, :], headsum, yo[:, p, :], start=True, stop=True).then_inc(p_mean, 1)

            for p in range(PAIRS):
                if p == 0:
                    mean(0)
                pe.wait_ge(taken[p % 4], 1 + t0 + p // 4)
                project(b0, 0, 0, p, yhi, ylo)
                if p == 0:
                    pe.wait_ge(rkw_ready, PAIRS)
                    pe.wait_ge(g_loaded, 16)
                    pe.wait_ge(lx_ready, 3)
                pe.wait_ge(p_sq, p + 1)
                if p >= 1:
                    pe.wait_ge(p_y, p)
                for q in range(NQ):
                    ins = nc.tensor.matmul(bank[5][:, 2 * q:2 * q + 2], g_q[:, P * q:P * q + P], headsum[:, 0:P:HD],
                                           start=True, stop=True)
                ins.then_inc(p_ss, 1)
                if p + 1 < PAIRS:
                    mean(p + 1)
                pe.wait_ge(p_rk, p + 1)
                nc.tensor.matmul(bank[6][:, :], rkw[:, p, :], g_b[:, :], start=True, stop=True).then_inc(p_bonus, 1)
                nc.tensor.matmul(bank[7][:, :], glora[:, P * p:P * p + P], xg[:, :], start=True, stop=True)\
                    .then_inc(p_gate, 1)
                pe.wait_ge(p_turn, p + 1)
                for q in range(NQ):
                    ins = nc.tensor.transpose(bank[5][:, P * q:P * q + P],
                                              g_t[:, 2 * q:2 * q + 2, :].rearrange("p a b -> p (a b)"), ident)
                ins.then_inc(p_spread, 1)

            b0, t0 = FIRST["oa"], USES["oa"]
            pe.wait_ge(taken[0], 1 + t0)
            project_late(b0, hhi, hlo, h_lo, 0)
            for u in range(1, KD):
                pe.wait_ge(taken[u % 4], 1 + t0 + u // 4)
                project(b0, 0, 0, u, hhi, hlo)
            b0, t0 = FIRST["out"], USES["out"]
            pe.wait_ge(taken[0], 1 + t0)
            project_late(b0, yhi, ylo, y_lo, 1 + HEADS)
            for u in range(1, KD):
                pe.wait_ge(taken[u % 4], 1 + t0 + u // 4)
                project(b0, 0, 0, u, yhi, ylo)
            norm(2)
            feed("f2", NF, 3 * KD)
            down("d2", 2 * NF)
            norm(3)


def _tiles(w):
    k, n = w.shape
    return w.reshape(k // P, P, n // P, P).transpose(2, 1, 0, 3)


def _down(w):
    t = _tiles(w)
    pad = np.zeros((t.shape[0], P, 24 - NF, P), w.dtype)
    return np.concatenate([t, pad], 2).reshape(KD, P, 3, 8, P).transpose(0, 2, 1, 3, 4).reshape(DBLK, P, 8, P)


def _stream(inp):
    w_in = inp["w_in"][0]
    c = np.cumsum([0, D, D, D, 128, 128, D, D, D, 512, 64, 8, D, D])
    r, k, v, xwa, xg, q, ka, va, iq, ik, iw, ga, gb = [w_in[:, a:b] for a, b in zip(c[:-1], c[1:])]
    pad = np.zeros((D, P - IDX_HEADS), w_in.dtype)

    def woven(*parts):
        t = np.stack([_tiles(p) for p in parts], 1)
        return t.reshape(-1, *t.shape[2:])

    return np.concatenate([
        woven(inp["ffn1_w_gate"][0], inp["ffn1_w_up"][0]), _down(inp["ffn1_w_down"][0]),
        _tiles(np.concatenate([iq, ik, ik, iw, pad, xwa, xg], 1)),
        woven(r, k, v, ga), woven(q, ka, va, gb),
        _tiles(inp["w_out_attn"][0]), _tiles(inp["w_out_rwkv"][0]), _tiles(inp["w_out"][0]),
        woven(inp["ffn2_w_gate"][0], inp["ffn2_w_up"][0]), _down(inp["ffn2_w_down"][0])])


def _params(inp):
    cols = [np.ravel(inp[n]).reshape(-1, P).T for n in PAR]
    return np.ascontiguousarray(np.concatenate(cols, 1))


def _constants():
    c = np.zeros((P, NCST), np.float32)
    i = np.arange(P)
    same = i[:, None] // HD == i[None, :] // HD
    c[:, C_ID:C_ID + P] = np.eye(P)
    c[:, C_ONE:C_ONE + P] = 1
    c[:, C_HEAD:C_HEAD + P] = same
    c[:, C_STRICT:C_STRICT + P] = same & (i[:, None] < i[None, :])
    c[:, C_INCL:C_INCL + P] = same & (i[:, None] <= i[None, :])
    c[:, C_SCAN:C_SCAN + T] = np.arange(T) % CH != 0
    c[:, C_VIS:C_VIS + P] = i[None, :] // CH <= i[:, None] // CH
    c[:, C_EPS], c[:, C_EPS + 1] = NORM_EPS, GN_EPS
    return c


def _layout(inputs):
    inp = {k: np.asarray(v) for k, v in inputs.items()}
    lora = np.zeros((P, 2, D), np.float32)
    lora[0:64, 0] = inp["decay_lora"][0]
    lora[64:128, 1] = inp["aaa_lora"][0]
    return {
        "x_in": np.ascontiguousarray(inp["x"][0].T.reshape(KD, P, T)),
        "ws": np.ascontiguousarray(_stream(inp)),
        "par_in": _params(inp),
        "cst_in": _constants(),
        "lora_in": lora,
        "glora_in": np.ascontiguousarray(inp["gate_lora"][0]),
    }


SHAPES = {"x_in": (KD, P, T), "ws": (NBLK, P, 8, P), "par_in": (P, NPAR), "cst_in": (P, NCST),
          "lora_in": (P, 2, D), "glora_in": (P, D)}
SCRATCH = {"sa_dram": (KD, P, T), "sb_dram": (KD, P, T), "rw_dram": (PAIRS, 5, P, T),
           "l_dram": (PAIRS, 2, NCH, CH, CH), "pd_dram": (PAIRS, 2, NCH, CH, CH),
           "t11_dram": (PAIRS, 2, NCH, HALF, HALF)}


def program(nc):
    ins = [nc.dram_tensor(n, s, F32, kind="ExternalInput").ap() for n, s in SHAPES.items()]
    out = nc.dram_tensor("out", (KD, P, T), F32, kind="ExternalOutput").ap()
    scratch = [nc.dram_tensor(n, s, F32, kind="Internal").ap() for n, s in SCRATCH.items()]
    build(nc, *ins, out, *scratch)


def kernel(**inputs):
    import concourse.bacc as _bacc
    from concourse.bass_utils import run_bass_kernel_spmd as _run

    nc = _bacc.Bacc("TRN2", target_bir_lowering=False, num_devices=1)
    program(nc)
    r = _run(nc, [_layout(inputs)], core_ids=[0])
    return r.results[0]["out"].reshape(1, D, T).transpose(0, 2, 1)
```
